# Optimizing a Trainium2 kernel written in Bass

```python
import jax, jax.numpy as jnp
from jax import lax
import numpy as np

D_MODEL = 1024
BATCH = 1
SEQ = 512
DEPTH = 2

N_A_LAYERS = DEPTH // 2
N_B_LAYERS = DEPTH - N_A_LAYERS

GLA_HEADS = 4
GLA_DK = D_MODEL // 2 // GLA_HEADS
GLA_DV = D_MODEL // GLA_HEADS
GLA_GATE_RANK = 16
GLA_GATE_NORM = 16.0
GLA_CHUNK = 64

FOX_HEADS = 16
FOX_DH = D_MODEL // FOX_HEADS
FOX_BLOCK = 128

N_EXPERTS = 16
N_GROUPS = 4
EXPERTS_PER_GROUP = N_EXPERTS // N_GROUPS
TOP_K = 2
D_EXPERT = D_MODEL // 2

ALPHA = float((2 * DEPTH) ** 0.25)
BETA = float((8 * DEPTH) ** -0.25)
LN_EPS = 1e-5
RMS_EPS = 1e-6

kernel_name = "yoco_gla_fox_grouped_moe_deepnorm"

def layer_norm(x, g, b):
    xf = x.astype(jnp.float32)
    mu = jnp.mean(xf, axis=-1, keepdims=True)
    var = jnp.mean(jnp.square(xf - mu), axis=-1, keepdims=True)
    return ((xf - mu) * lax.rsqrt(var + LN_EPS) * g.astype(jnp.float32) + b.astype(jnp.float32)).astype(x.dtype)

def gla_mixer(x, w_in, w_gk, b_gk, norm_g, w_out):
    B, S, _ = x.shape
    HK = GLA_HEADS * GLA_DK
    HV = GLA_HEADS * GLA_DV
    C = GLA_CHUNK
    N = S // C
    proj = x @ w_in
    q, k, v, g, gr = jnp.split(proj, [HK, 2 * HK, 2 * HK + HV, 2 * HK + 2 * HV], axis=-1)
    gk = jax.nn.log_sigmoid((gr @ w_gk + b_gk).astype(jnp.float32)) / GLA_GATE_NORM

    def to_chunks(t, d):
        return t.reshape(B, N, C, GLA_HEADS, d).transpose(0, 1, 3, 2, 4)

    qc = to_chunks(q.astype(jnp.float32), GLA_DK) * (GLA_DK ** -0.5)
    kc = to_chunks(k.astype(jnp.float32), GLA_DK)
    vc = to_chunks(v.astype(jnp.float32), GLA_DV)
    bc = jnp.cumsum(to_chunks(gk, GLA_DK), axis=3)
    b_last = bc[:, :, :, -1:, :]
    q_dec = qc * jnp.exp(bc)
    k_inv = kc * jnp.exp(-bc)
    k_end = kc * jnp.exp(b_last - bc)

    causal = jnp.tril(jnp.ones((C, C), dtype=bool))
    attn = jnp.where(causal, jnp.einsum('bnhcd,bnhsd->bnhcs', q_dec, k_inv), 0.0)
    o_intra = jnp.einsum('bnhcs,bnhsv->bnhcv', attn, vc)

    kv_chunk = jnp.einsum('bnhcd,bnhcv->nbhdv', k_end, vc)
    chunk_decay = jnp.exp(b_last[:, :, :, 0, :]).transpose(1, 0, 2, 3)

    def step(state, inp):
        kv_n, dec_n = inp
        return state * dec_n[..., None] + kv_n, state

    init = jnp.zeros((B, GLA_HEADS, GLA_DK, GLA_DV), jnp.float32)
    _, states = lax.scan(step, init, (kv_chunk, chunk_decay))
    o_inter = jnp.einsum('bnhcd,nbhdv->bnhcv', q_dec, states)

    o = (o_intra + o_inter).transpose(0, 1, 3, 2, 4).reshape(B, S, GLA_HEADS, GLA_DV)
    o = o * lax.rsqrt(jnp.mean(jnp.square(o), axis=-1, keepdims=True) + RMS_EPS) * norm_g.astype(jnp.float32)
    o = o * jax.nn.silu(g.astype(jnp.float32).reshape(B, S, GLA_HEADS, GLA_DV))
    return (o.reshape(B, S, HV).astype(x.dtype) @ w_out).astype(x.dtype)

def fox_shared_kv(h, kv_w, forget_bias):
    B, S, _ = h.shape
    FD = FOX_HEADS * FOX_DH
    proj = h @ kv_w
    k, v, fl = jnp.split(proj, [FD, 2 * FD], axis=-1)
    k = k.reshape(B, S, FOX_HEADS, FOX_DH).astype(jnp.float32)
    v = v.reshape(B, S, FOX_HEADS, FOX_DH).astype(jnp.float32)
    log_f = jax.nn.log_sigmoid(fl.astype(jnp.float32) + forget_bias.astype(jnp.float32))
    cum = jnp.cumsum(log_f, axis=1)
    return k, v, cum

def fox_mixer(x, k, v, cum, w_qg, w_out):
    B, S, _ = x.shape
    FD = FOX_HEADS * FOX_DH
    nb = S // FOX_BLOCK
    proj = x @ w_qg
    q, g = jnp.split(proj, [FD], axis=-1)
    q = q.reshape(B, S, FOX_HEADS, FOX_DH).astype(jnp.float32) * (FOX_DH ** -0.5)
    qb = q.reshape(B, nb, FOX_BLOCK, FOX_HEADS, FOX_DH).transpose(1, 0, 2, 3, 4)
    cum_bhs = cum.transpose(0, 2, 1)
    cqb = cum_bhs.reshape(B, FOX_HEADS, nb, FOX_BLOCK).transpose(2, 0, 1, 3)
    key_pos = jnp.arange(S)

    def block(args):
        q_blk, c_blk, i = args
        s = jnp.einsum('bqhd,bkhd->bhqk', q_blk, k)
        decay = c_blk[..., :, None] - cum_bhs[..., None, :]
        q_pos = i * FOX_BLOCK + jnp.arange(FOX_BLOCK)
        mask = key_pos[None, :] <= q_pos[:, None]
        p = jax.nn.softmax(jnp.where(mask, s + decay, -jnp.inf), axis=-1)
        return jnp.einsum('bhqk,bkhd->bqhd', p, v)

    o = lax.map(block, (qb, cqb, jnp.arange(nb)))
    o = o.transpose(1, 0, 2, 3, 4).reshape(B, S, FD)
    o = o * jax.nn.sigmoid(g.astype(jnp.float32))
    return (o.astype(x.dtype) @ w_out).astype(x.dtype)

def grouped_moe(x, router_w, router_bias, w_gate, w_up, w_down):
    B, S, D = x.shape
    xt = x.reshape(-1, D)
    T = xt.shape[0]
    scores = jax.nn.softmax((xt @ router_w).astype(jnp.float32), axis=-1)
    sel = scores + router_bias.astype(jnp.float32)
    grouped = sel.reshape(T, N_GROUPS, EXPERTS_PER_GROUP)
    group_score = jnp.sum(lax.top_k(grouped, TOP_K)[0], axis=-1)
    best_group = jnp.argmax(group_score, axis=-1)
    in_group = jnp.take_along_axis(grouped, best_group[:, None, None], axis=1)[:, 0]
    _, local_idx = lax.top_k(in_group, TOP_K)
    expert_idx = best_group[:, None] * EXPERTS_PER_GROUP + local_idx
    w = jnp.take_along_axis(scores, expert_idx, axis=-1)
    w = w / jnp.sum(w, axis=-1, keepdims=True)
    gates = jnp.sum(jax.nn.one_hot(expert_idx, N_EXPERTS, dtype=jnp.float32) * w[..., None], axis=1)
    h = jax.nn.silu(jnp.einsum('td,edf->tef', xt, w_gate)) * jnp.einsum('td,edf->tef', xt, w_up)
    h = h * gates[..., None].astype(h.dtype)
    y = jnp.einsum('tef,efd->td', h, w_down)
    return y.reshape(B, S, D).astype(x.dtype)

def setup_inputs(seed: int = 0) -> dict:
    key = jax.random.key(seed)
    ks = jax.random.split(key, 24)

    def nrm(k, shape, scale):
        return jax.random.normal(k, shape, jnp.float32) * scale

    HK = GLA_HEADS * GLA_DK
    HV = GLA_HEADS * GLA_DV
    FD = FOX_HEADS * FOX_DH
    s_in = D_MODEL ** -0.5
    x = nrm(ks[0], (BATCH, SEQ, D_MODEL), 1.0)
    gla_w_in = jnp.concatenate([
        nrm(ks[1], (N_A_LAYERS, D_MODEL, 2 * HK), s_in),
        nrm(ks[2], (N_A_LAYERS, D_MODEL, HV), s_in * BETA),
        nrm(ks[3], (N_A_LAYERS, D_MODEL, HV + GLA_GATE_RANK), s_in),
    ], axis=-1)
    gla_w_gk = nrm(ks[4], (N_A_LAYERS, GLA_GATE_RANK, HK), GLA_GATE_RANK ** -0.5)
    gla_b_gk = nrm(ks[5], (N_A_LAYERS, HK), 0.1)
    gla_norm_g = 1.0 + nrm(ks[6], (N_A_LAYERS, GLA_DV), 0.02)
    gla_w_out = nrm(ks[7], (N_A_LAYERS, HV, D_MODEL), (HV ** -0.5) * BETA)
    kv_w = jnp.concatenate([
        nrm(ks[8], (D_MODEL, FD), s_in),
        nrm(ks[9], (D_MODEL, FD), s_in * BETA),
        nrm(ks[10], (D_MODEL, FOX_HEADS), s_in),
    ], axis=-1)
    forget_bias = jax.random.uniform(ks[11], (FOX_HEADS,), jnp.float32, minval=1.0, maxval=4.0)
    fox_w_qg = nrm(ks[12], (N_B_LAYERS, D_MODEL, 2 * FD), s_in)
    fox_w_out = nrm(ks[13], (N_B_LAYERS, FD, D_MODEL), (FD ** -0.5) * BETA)
    router_w = nrm(ks[14], (D_MODEL, N_EXPERTS), s_in)
    router_bias = nrm(ks[15], (N_EXPERTS,), 0.01)
    moe_w_gate = nrm(ks[16], (DEPTH, N_EXPERTS, D_MODEL, D_EXPERT), s_in)
    moe_w_up = nrm(ks[17], (DEPTH, N_EXPERTS, D_MODEL, D_EXPERT), s_in)
    moe_w_down = nrm(ks[18], (DEPTH, N_EXPERTS, D_EXPERT, D_MODEL), (D_EXPERT ** -0.5) * BETA)
    ln_g = 1.0 + nrm(ks[19], (DEPTH, 2, D_MODEL), 0.02)
    ln_b = nrm(ks[20], (DEPTH, 2, D_MODEL), 0.02)
    return {"x": x, "gla_w_in": gla_w_in, "gla_w_gk": gla_w_gk, "gla_b_gk": gla_b_gk,
            "gla_norm_g": gla_norm_g, "gla_w_out": gla_w_out, "kv_w": kv_w,
            "forget_bias": forget_bias, "fox_w_qg": fox_w_qg, "fox_w_out": fox_w_out,
            "router_w": router_w, "router_bias": router_bias, "moe_w_gate": moe_w_gate,
            "moe_w_up": moe_w_up, "moe_w_down": moe_w_down, "ln_g": ln_g, "ln_b": ln_b}

def reference(x, gla_w_in, gla_w_gk, gla_b_gk, gla_norm_g, gla_w_out, kv_w, forget_bias,
              fox_w_qg, fox_w_out, router_w, router_bias, moe_w_gate, moe_w_up, moe_w_down,
              ln_g, ln_b):
    h = x
    k_sh = v_sh = cum_sh = None
    for layer in range(DEPTH):
        if layer < N_A_LAYERS:
            mix = gla_mixer(h, gla_w_in[layer], gla_w_gk[layer], gla_b_gk[layer],
                            gla_norm_g[layer], gla_w_out[layer])
        else:
            j = layer - N_A_LAYERS
            mix = fox_mixer(h, k_sh, v_sh, cum_sh, fox_w_qg[j], fox_w_out[j])
        h = layer_norm(ALPHA * h + mix, ln_g[layer, 0], ln_b[layer, 0])
        ffn = grouped_moe(h, router_w, router_bias, moe_w_gate[layer], moe_w_up[layer], moe_w_down[layer])
        h = layer_norm(ALPHA * h + ffn, ln_g[layer, 1], ln_b[layer, 1])
        if layer == N_A_LAYERS - 1:
            k_sh, v_sh, cum_sh = fox_shared_kv(h, kv_w, forget_bias)
    return h


_drawn_inputs = setup_inputs


def setup_inputs(seed=0):
    import zlib

    import numpy as np

    out = dict(_drawn_inputs(seed))
    spreads = {}
    factors = {'gla_norm_g': 2.938}
    for name, (base, spread) in spreads.items():
        noise = np.random.default_rng([zlib.crc32(name.encode()), seed]).standard_normal(out[name].shape)
        drawn = base * np.exp(spread * noise) if base else spread * noise
        out[name] = __import__('jax').numpy.asarray(drawn.astype(out[name].dtype))
    for name, factor in factors.items():
        out[name] = (out[name] * factor).astype(out[name].dtype)
    return out
```

```python
from contextlib import ExitStack

import concourse.bass as bass
from concourse import mybir

F32 = mybir.dt.float32
I32 = mybir.dt.int32
U32 = mybir.dt.uint32
ALU = mybir.AluOpType
ACT = mybir.ActivationFunctionType
AX = mybir.AxisListType

P = 128
BANK = 512


class Steps:

    def __init__(self, sem):
        self.sem, self.n = sem, 0

    def mark(self, ins):
        self.n += 1
        ins.then_inc(self.sem, 1)

    def settle(self, eng):
        eng.wait_ge(self.sem, self.n)


def yoco_trunk(nc, x, gla_w_in, gla_w_gk, gla_b_gk, gla_norm_g, gla_w_out, kv_w, forget_bias, fox_w_qg,
               fox_w_out, router_w, router_bias, moe_w_gate, moe_w_up, moe_w_down, ln_g, ln_b, out):
    _, S, D = x.shape
    DEPTH, E, _, DE = moe_w_gate.shape
    RANK, HK = gla_w_gk.shape[1:]
    DV = gla_norm_g.shape[1]
    HV = gla_w_out.shape[1]
    H_A = HV // DV
    DK = HK // H_A
    H_B = forget_bias.shape[0]
    DH = fox_w_out.shape[1] // H_B
    CH = 64
    GROUPS = 4
    EPG = E // GROUPS
    T = S // P
    K = D // P
    KE = DE // P
    CPT = P // CH
    ALPHA = float((2 * DEPTH) ** 0.25)
    LN_EPS, RMS_EPS, GATE_NORM = 1e-5, 1e-6, 16.0
    BIG = float(1 << 20)
    NEG = -1e37
    LOW = -3e38
    assert DEPTH == 2 and T == 4 and K == 8 and DK == P and S == BANK and DE == BANK and DH == 64

    h_rows = nc.dram_tensor("h_rows", [S, D], F32).ap()
    cum_rows = nc.dram_tensor("cum_rows", [2, 16, S], F32).ap()
    y_rows = nc.dram_tensor("y_rows", [2 * S, D], F32).ap()

    RING = 6
    GLA_PIECES = 8
    FOX_PIECES = 10
    MOE_PIECES = 3 * E
    gla0 = 0
    moe0 = [GLA_PIECES, GLA_PIECES + MOE_PIECES + FOX_PIECES]
    fox0 = GLA_PIECES + MOE_PIECES
    BODY = 4

    ctx = ExitStack()
    with ctx:
        def sb(name, shape, dt=F32):
            return ctx.enter_context(nc.sbuf_tensor(name, shape, dt))

        def sem(name):
            return ctx.enter_context(nc.semaphore(name))

        ring = sb("ring", [P, RING, K * BANK])
        H = sb("resid", [P, T, D])
        hT = sb("featT", [P, K, S])
        arena = sb("arena", [P, 18752])
        ident = sb("ident", [P, P])
        chunk_sums = sb("chunk_sums", [P, 2 * P])
        upto = sb("upto", [P, P])
        ones = sb("ones", [P, P])
        causal = sb("causal", [P, P])
        slot1 = sb("slot1", [P, P])
        rw = sb("rw", [P, K, E])
        rbias = sb("rbias", [P, E])
        fbias = sb("fbias", [P, H_B])
        kvf = sb("kvf", [P, K, H_B])
        iota_e = sb("iota_e", [P, E])
        iota_g = sb("iota_g", [P, GROUPS])
        row_id = sb("row_id", [P, T])
        counts = sb("counts", [1, E], I32)
        parts = sb("parts", [1, E], I32)
        scan = sb("scan", [1, 2, 8 + E])
        part3 = sb("part3", [1, E])
        carry = sb("carry", [1, 1])
        ln_mv = sb("ln_mv", [P, T, 2])
        ln_bn = sb("ln_bn", [P, T, 2, 6])
        ln_r = sb("ln_r", [P, T, 3])
        half = sb("half", [P, 16])
        tokv = sb("tokv", [P, 4, 2], U32)
        tokg = sb("tokg", [P, 4])
        cold_rows = sb("cold_rows", [P, 2], U32)
        cold_gate = sb("cold_gate", [P, 1])
        cold_rank = sb("cold_rank", [P, T])
        ranks = sb("ranks", [P, T, E + 3])
        ps = ctx.enter_context(nc.psum_tensor("ps", [P, 8, BANK], F32))

        def at(off, *dims):
            n = 1
            for d in dims:
                n *= d
            v = arena[:, off:off + n]
            if len(dims) == 2:
                v = v.rearrange("p (a b) -> p a b", a=dims[0])
            if len(dims) == 3:
                v = v.rearrange("p (a b c) -> p a b c", a=dims[0], b=dims[1])
            return v

        ln_p = at(0, 2, D)
        q_a, k_a, gk = at(0, H_A, S), at(2048, H_A, S), at(4096, T, HK)
        mix = at(6144, T, HV)
        e_bc, k_inv, k_end = at(10240, 2, S), at(11264, 2, S), at(12288, 2, S)
        k_tok, att, states = at(13312, T, P), at(13824, T, P), at(14336, 2 * T, DV)
        gr_in, wgk = at(16384, S)[0:RANK + 1, :], at(16896, HK)[0:RANK + 1, :]
        grw, normg = at(17408, K, RANK), at(17536, DV)
        ssq = at(17792, T * H_A)
        rms = at(17808, T * H_A)
        squares = at(17824, DV)
        gate_a = at(10240, 2, BANK)
        qa, ka = at(0, 2, 4, S), at(4096, 2, 4, S)
        v_b = at(8192, T, D)
        o_b = at(12288, T, D)
        prob, prob_t = at(16384, 2, S), at(17408, 2, S)
        nmax = at(18432, 64)
        rsum = at(18496, 64)
        rinv = at(18560, 64)
        f_log = at(18624, T * H_B)
        f_tmp = at(18688, T * H_B)
        cumT = at(16384, 2, S)
        gate_b = at(16384, 2, BANK)
        xg, xgT = at(2048, 2, D), at(4096, 2, D)
        hid, hidT, silu = at(6144, BANK), at(6656, BANK), at(7168, BANK)
        yb = at(7680, 2, D)
        onehot = at(9728, 2, BANK)
        cxg, cxgT, cyb, coneh = at(10752, D), at(11776, D), at(12800, D), at(13824, BANK)
        info = at(14336, T, E + 2, 3)
        ysum = at(14592, 2, 2 * D)
        rt = [at(14592 + 64 * n, T, E) for n in range(12)]
        rs = [at(14592 + 64 * 12 + 16 * n, T, GROUPS) for n in range(8)]
        rv = [at(14592 + 64 * 14 + 4 * n, T) for n in range(8)]

        w_loaded = [sem(f"w_loaded{n}") for n in range(RING)]
        w_free = sem("w_free")
        x_loaded = [sem(f"x_loaded{n}") for n in range(T)]
        par_loaded = sem("par_loaded")
        consts = sem("consts")
        one_rows = sem("one_rows")
        tp_done, tp_act, tp_dve = sem("tp_done"), sem("tp_act"), sem("tp_dve")
        proj_done = sem("proj_done")
        ev_act, ev_dve = sem("ev_act"), sem("ev_dve")
        dve_step, act_step, pool_step = sem("dve_step"), sem("act_step"), sem("pool_step")
        gr_done, gr_ev, z_done, z_min, z_abs, z_ln, gk_ready = (
            sem(n) for n in ("gr_done", "gr_ev", "z_done", "z_min", "z_abs", "z_ln", "gk_ready"))
        bc_done, bc_exp, decayed = sem("bc_done"), sem("bc_exp"), sem("decayed")
        kt_done, kt_ev, att_done, att_ev = sem("kt_done"), sem("kt_ev"), sem("att_done"), sem("att_ev")
        kv_done, st_done, o_done, o_ev, sq_done = (
            sem(n) for n in ("kv_done", "st_done", "o_done", "o_ev", "sq_done"))
        rms_in, rms_out, normed = sem("rms_in"), sem("rms_out"), sem("normed")
        gate_done, gated = sem("gate_done"), sem("gated")
        lnp_loaded = sem("lnp_loaded")
        ln_stats, ln_rstd, ln_bias, ln_norm, ln_scaled, ln_ready = (
            sem(n) for n in ("ln_stats", "ln_rstd", "ln_bias", "ln_norm", "ln_scaled", "ln_ready"))
        h_stored = sem("h_stored")
        rt_logits, rt_in, rt_exp, rt_picked, rt_ranks, rt_ready = (
            sem(n) for n in ("rt_logits", "rt_in", "rt_exp", "rt_picked", "rt_ranks", "rt_ready"))
        pads_clear = sem("pads_clear")
        moves = sem("moves")
        hot, tbl_done, tbl_ev = sem("hot"), sem("tbl_done"), sem("tbl_ev")
        gathered = [sem("gathered0"), sem("gathered1")]
        scattered = [sem("scattered0"), sem("scattered1")]
        xt_done, xt_ev = sem("xt_done"), sem("xt_ev")
        gate_mm, up_mm, silu_done, hid_done = sem("gate_mm"), sem("up_mm"), sem("silu_done"), sem("hid_done")
        ht_done, ht_ev, y_mm, y_act, y_dve = (sem(n) for n in ("ht_done", "ht_ev", "y_mm", "y_act", "y_dve"))
        c_copy, c_rank, c_hot, c_tbl, c_idx, c_gat, c_xt, c_xe, c_gu, c_silu, c_hid, c_ht, c_he, c_y, c_ya, c_yd, c_sca = (
            sem("cold_" + n) for n in ("copy", "rank", "hot", "tbl", "idx", "gathered", "xt", "xt_ev", "gate_up", "silu",
                                       "hid", "ht", "ht_ev", "y", "y_act", "y_dve", "scattered"))
        y_loaded = [sem("y_loaded0"), sem("y_loaded1")]
        fl_done, fl_z, fl_abs, fl_ln, f_ready, cum_done, cum_ev, cum_stored = (
            sem(n) for n in ("fl_done", "fl_z", "fl_abs", "fl_ln", "f_ready", "cum_done", "cum_ev", "cum_stored"))
        cum_put = [sem("cum_put0"), sem("cum_put1")]
        sc_done, sc_masked, sc_max, p_done, pt_done, pt_ev, pv_done, pv_ev = (
            sem(n) for n in ("sc_done", "sc_masked", "sc_max", "p_done", "pt_done", "pt_ev", "pv_done", "pv_ev"))
        stored = sem("stored")

        KV_BANKS = (4, 2)

        units = []

        def plan(kind, piece, block, engine):
            units.append((kind, piece, block, engine))

        for f in range(H_A):
            plan("qa", gla0, f, "act")
        for f in range(H_A):
            plan("ka", gla0 + 1, f, "dve")
        for p in range(2):
            for t in range(T):
                plan("va", gla0 + 2 + p, (p, t), "act" if t % 2 else "dve")
        U_GLA_TAIL = len(units)
        for t in range(T):
            for p in range(2):
                plan("ga", gla0 + 4 + p, (p, t), "act")
        for t in range(T):
            for p in range(2):
                plan("oa", gla0 + 6 + p, (p, t), "dve")
        U_FOX = len(units)
        for p in range(2):
            for t in range(T):
                plan("vb", fox0 + p, (p, t), "act" if t % 2 else "dve")
        U_QUARTERS = len(units)
        for c in range(4):
            for f in range(2):
                plan("kb", fox0 + 2 + 2 * (c // 2), (c, f), "dve")
            for f in range(2):
                plan("qb", fox0 + 3 + 2 * (c // 2), (c, f), "act")
        U_FOX_TAIL = len(units)
        for t in range(T):
            for p in range(2):
                plan("gb", fox0 + 6 + p, (p, t), "act")
        for t in range(T):
            for p in range(2):
                plan("ob", fox0 + 8 + p, (p, t), "dve")
        U_END = len(units)

        def taken(u):
            e = units[u][3]
            return (ev_act if e == "act" else ev_dve), sum(1 for x_ in units[:u + 1] if x_[3] == e)

        tails = [(U_GLA_TAIL, mix, gate_a, ACT.Silu), (U_FOX_TAIL, o_b, gate_b, ACT.Sigmoid)]
        TP_X, TP_MIX, TP_RT, TP_L0 = 0, [1, 4], [2, 5], 3

        def wait_piece(eng, n):
            eng.wait_ge(w_loaded[n % RING], 16 * (n // RING + 1))

        def moe_turn(L, i, j):
            return i * BODY + j

        block = ctx.enter_context(nc.Block())

        @block.sync
        def _(sp):
            for t in range(T):
                sp.dma_start(H[:, t, :], x[0, t * P:(t + 1) * P, :]).then_inc(x_loaded[t], 16)

            def load(n, src, free):
                if free is not None:
                    sp.wait_ge(w_free, free)
                dst = ring[:, n % RING, :].rearrange("p (k n) -> p k n", k=src.shape[1])
                sp.dma_start(dst, src).then_inc(w_loaded[n % RING], 16)

            def cols(w, c):
                return w[:, c * BANK:(c + 1) * BANK].rearrange("(k p) n -> p k n", p=P)

            def straight(n0, srcs):
                for m, src in enumerate(srcs):
                    n = n0 + m
                    load(n, src, n - RING + 1 if n >= RING else None)

            def experts(L):
                with sp.Fori(0, E // BODY) as i:
                    for j in range(BODY):
                        e = i * BODY + j
                        for m, w in enumerate((moe_w_gate, moe_w_up, moe_w_down)):
                            n = moe0[L] + 3 * j + m
                            src = w[L][bass.ds(e, 1), :, :].rearrange("e (k p) f -> p (e k) f", p=P)
                            load(n, src, i * (3 * BODY) + n - RING + 1)

            w_in, w_out, w_qg, w_o2 = gla_w_in[0], gla_w_out[0], fox_w_qg[0], fox_w_out[0]
            straight(gla0, [cols(w_in, c) for c in range(6)] + [cols(w_out, c) for c in range(2)])
            experts(0)
            straight(fox0, [cols(kv_w, 2), cols(kv_w, 3), cols(kv_w, 0), cols(w_qg, 0), cols(kv_w, 1),
                            cols(w_qg, 1), cols(w_qg, 2), cols(w_qg, 3), cols(w_o2, 0), cols(w_o2, 1)])
            experts(1)

        @block.gpsimd
        def _(pool):
            own = Steps(pool_step)
            last_row = [pool.to_reg(S - 1), pool.to_reg(2 * S - 1)]
            n_const = [0]

            def const(ins):
                n_const[0] += 1
                ins.then_inc(consts, 1)

            def settle():
                pool.wait_ge(consts, n_const[0])

            const(pool.memset(ident[:, :], 0.0))
            const(pool.memset(chunk_sums[:, :], 1.0 / GATE_NORM))
            const(pool.memset(upto[:, :], 1.0))
            const(pool.memset(ones[:, :], 1.0))
            const(pool.memset(causal[:, :], 0.0))
            const(pool.memset(half[:, :], -0.5))
            const(pool.memset(att[:, :, :], 0.0))
            const(pool.iota(slot1[:, :], pattern=[[1, P]], base=1, channel_multiplier=0,
                            allow_small_or_imprecise_dtypes=True))
            const(pool.iota(iota_e[:, :], pattern=[[1, E]], base=0, channel_multiplier=0,
                            allow_small_or_imprecise_dtypes=True))
            const(pool.iota(iota_g[:, :], pattern=[[1, GROUPS]], base=0, channel_multiplier=0,
                            allow_small_or_imprecise_dtypes=True))
            const(pool.iota(row_id[:, :], pattern=[[P, T]], base=-int(BIG), channel_multiplier=1,
                            allow_small_or_imprecise_dtypes=True))
            settle()
            const(pool.affine_select(out=ident[:, :], in_=ident[:, :], compare_op=ALU.not_equal, fill=1.0,
                                     base=0, pattern=[[-1, P]], channel_multiplier=1))
            const(pool.affine_select(out=upto[:, :], in_=upto[:, :], compare_op=ALU.is_ge, fill=0.0,
                                     base=0, pattern=[[1, P]], channel_multiplier=-1))
            const(pool.affine_select(out=causal[:, :], in_=causal[:, :], compare_op=ALU.is_ge, fill=NEG,
                                     base=0, pattern=[[-1, P]], channel_multiplier=1))
            const(pool.affine_select(out=chunk_sums[:, 0:P], in_=chunk_sums[:, 0:P], compare_op=ALU.is_ge,
                                     fill=0.0, base=0, pattern=[[1, P]], channel_multiplier=-1))
            const(pool.affine_select(out=chunk_sums[:, P:2 * P], in_=chunk_sums[:, P:2 * P],
                                     compare_op=ALU.is_gt, fill=0.0, base=0, pattern=[[-1, P]],
                                     channel_multiplier=1))
            settle()
            const(pool.affine_select(out=chunk_sums[:, CH:P], in_=chunk_sums[:, CH:P], compare_op=ALU.is_ge,
                                     fill=0.0, base=-CH, pattern=[[0, P - CH]], channel_multiplier=1))
            const(pool.affine_select(out=chunk_sums[:, P:P + CH], in_=chunk_sums[:, P:P + CH],
                                     compare_op=ALU.is_gt, fill=0.0, base=CH, pattern=[[0, CH]],
                                     channel_multiplier=-1))

            def layer_norm(N):
                for s in range(T + 2):
                    if s < T:
                        pool.wait_ge(ln_stats, N * T + s + 1)
                        pool.tensor_tensor(ln_r[:, s, 1:2], ln_r[:, s, 0:1], half[:, 0:1],
                                           ALU.pow).then_inc(ln_rstd, 1)
                    if s >= 2:
                        t = s - 2
                        pool.wait_ge(ln_scaled, N * T + t + 1)
                        pool.wait_ge(lnp_loaded, 32 * (N + 1))
                        pool.tensor_tensor(H[:, t, :], H[:, t, :], ln_p[:, 1, :], ALU.add).then_inc(ln_ready, 1)

            def load_ln(N):
                L, which = divmod(N, 2)
                for m, w in enumerate((ln_g, ln_b)):
                    pool.dma_start(ln_p[:, m, :], w[L, which:which + 1, :].to_broadcast([P, D])
                                   ).then_inc(lnp_loaded, 16)

            def store_rows(N, dst):
                for t in range(T):
                    pool.wait_ge(ln_ready, N * T + t + 1)
                    pool.dma_start(dst[t * P:(t + 1) * P, :], H[:, t, :]).then_inc(
                        h_stored if dst is h_rows else stored, 16)

            def gather(dst, rows, done):
                pool.sem_inc(moves, 1)
                pool.indirect_dma_start(out=dst, out_offset=None, in_=h_rows,
                                        in_offset=bass.IndirectOffsetOnAxis(ap=rows, axis=0),
                                        bounds_check=last_row[0], oob_is_err=False).then_inc(done, 16)

            def scatter(src, rows, done):
                pool.sem_inc(moves, 1)
                pool.indirect_dma_start(out=y_rows, out_offset=bass.IndirectOffsetOnAxis(ap=rows, axis=0),
                                        in_=src, in_offset=None,
                                        bounds_check=last_row[1], oob_is_err=False).then_inc(done, 16)

            def experts(L):
                TB, XT, EX, SC = 18 * L, 17 * L + 1, 16 * L + 1, 8 * L + 1
                if L == 0:
                    for dst, done in ((yb[0:1, 0, 0:P], scattered[0]), (yb[0:1, 1, 0:P], scattered[1]),
                                      (cyb[0:1, 0:P], c_sca)):
                        pool.dma_start(dst, x[0, 0:1, 0:P]).then_inc(done, 16)
                for n in range(2):
                    pool.memset(xg[:, n, :], 0.0).then_inc(pads_clear, 1)
                pool.memset(cxg, 0.0).then_inc(pads_clear, 1)
                pool.wait_ge(pads_clear, 3 * (L + 1))
                pool.wait_ge(h_stored, 64 * (L + 1))
                for e in range(2):
                    pool.wait_ge(tbl_ev, 2 * (TB + e + 1))
                    gather(xg[:, e, :], tokv[:, e, 0:1], gathered[e])
                with pool.Fori(0, E // BODY) as i:
                    for j in range(BODY):
                        e = i * BODY + j
                        n = pool.value_load(counts[0:1, bass.ds(e, 1)], min_val=0, max_val=S)
                        pool.wait_ge(tbl_ev, (e + TB + 3) * 2)
                        pool.wait_ge(xt_done, (e + XT + 1) * 2)
                        gather(xg[:, j % 2, :], tokv[:, (j + 2) % 4, 0:1], gathered[j % 2])
                        pool.wait_ge(y_act, e + EX + 1)
                        pool.wait_ge(y_dve, e + EX + 1)
                        scatter(yb[:, j % 2, :], tokv[:, j % 4, 1:2], scattered[j % 2])
                        with pool.If(n > P):
                            before = pool.value_load(parts[0:1, bass.ds(e, 1)], min_val=0, max_val=6 * E + 1)
                            with pool.Fori(0, 3) as m:
                                c = before + m
                                pool.wait_ge(c_sca, c * 16)
                                pool.wait_ge(c_idx, (c + 1) * 2)
                                gather(cxg, cold_rows[:, 0:1], c_gat)
                                pool.wait_ge(c_ya, c + 1)
                                pool.wait_ge(c_yd, c + 1)
                                scatter(cyb, cold_rows[:, 1:2], c_sca)
                            pool.wait_ge(c_sca, (before + 3) * 16)
                            pool.nop()
                        with pool.Else():
                            pool.nop()
                        pool.nop()
                for n in range(2):
                    pool.wait_ge(gathered[n], 16 * 9 * (L + 1))
                    pool.wait_ge(scattered[n], 16 * (SC + 8))
                y_by_choice = y_rows.rearrange("(c t p) d -> t p c d", c=2, p=P)
                for t in range(T):
                    if t >= 2:
                        pool.wait_ge(ln_stats, (2 * L + 1) * T + t - 1)
                    pool.dma_start(ysum[:, t % 2, :].rearrange("p (c d) -> p c d", c=2),
                                   y_by_choice[t]).then_inc(y_loaded[t % 2], 16)

            pool.wait_ge(sq_done, T * H_A)
            pool.wait_ge(rms_in, 1)
            pool.tensor_tensor(rms, ssq, half[:, 0:T * H_A], ALU.pow).then_inc(rms_out, 1)
            pool.wait_ge(normed, 1)
            load_ln(0)
            layer_norm(0)
            store_rows(0, h_rows)
            load_ln(1)
            experts(0)
            layer_norm(1)
            pool.wait_ge(ln_ready, 2 * T)
            for buf in (qa, ka):
                pool.memset(buf[DH:DH + 2, :, :, :], 1.0).then_inc(one_rows, 1)
            pool.wait_ge(one_rows, 2)
            pool.wait_ge(cum_ev, 2)
            pool.dma_start(cum_rows.rearrange("a h s -> h a s"), cumT[0:H_B, :, :]).then_inc(cum_stored, 16)
            pool.wait_ge(cum_stored, 16)
            for c in range(4):
                if c >= 2:
                    pool.wait_ge(pv_done, 16 * (c - 1))
                for buf, row, src in ((qa, DH + 1, 0), (ka, DH, 1)):
                    pool.dma_start(buf[row:row + 1, c % 2, :, :], cum_rows[src:src + 1, 4 * c:4 * c + 4, :]
                                   ).then_inc(cum_put[c % 2], 16)
            pool.wait_ge(pv_ev, 64)
            load_ln(2)
            layer_norm(2)
            store_rows(2, h_rows)
            load_ln(3)
            experts(1)
            layer_norm(3)
            store_rows(3, out[0])
            pool.wait_ge(stored, 16 * T)

        @block.tensor
        def _(pe):
            def transpose_tile(turn, t, src):
                for kk, gone in enumerate((tp_act, tp_dve)):
                    if 4 * turn + t:
                        pe.wait_ge(gone, 4 * turn + t)
                    for j in range(4):
                        mm = pe.transpose(ps[:, kk, j * P:(j + 1) * P],
                                          src[:, t, (4 * kk + j) * P:(4 * kk + j + 1) * P], ident[:, :])
                    mm.then_inc(tp_done, 1)

            def unit(u, frees=0):
                kind, piece, blk, _ = units[u]
                wait_piece(pe, piece)
                if u >= 4:
                    pe.wait_ge(*taken(u - 4))
                o = ps[:, 2 + u % 4, :]
                w = ring[:, piece % RING, :].rearrange("p (k n) -> p k n", k=K)
                for k in range(K):
                    if kind in ("qa", "ka"):
                        mm = pe.matmul(o, w[:, k, blk * P:(blk + 1) * P], hT[:, k, :], start=k == 0, stop=k == K - 1)
                    elif kind in ("qb", "kb"):
                        f = 2 * (blk[0] % 2) + blk[1]
                        mm = pe.matmul(o, w[:, k, f * P:(f + 1) * P], hT[:, k, :], start=k == 0, stop=k == K - 1)
                    else:
                        t = blk[1]
                        mm = pe.matmul(o, hT[:, k, t * P:(t + 1) * P], w[:, k, :], start=k == 0, stop=k == K - 1)
                mm.then_inc(proj_done, 1)
                if frees:
                    marker(frees)

            def marker(frees):
                pe.matmul(ps[:, 7, BANK - 2:BANK], ident[:, :], ident[:, 0:2], start=True, stop=True
                          ).then_inc(w_free, frees)

            def tail(L):
                u0, src, _, _ = tails[L]
                for s in range(T + 1):
                    if s < T:
                        unit(u0 + 2 * s)
                        unit(u0 + 2 * s + 1, frees=2 if s == T - 1 else 0)
                    if s >= 1:
                        pe.wait_ge(gated, 8 * L + 2 * s)
                        transpose_tile(TP_MIX[L], s - 1, src)
                for t in range(T):
                    pe.wait_ge(tp_act, 4 * TP_MIX[L] + t + 1)
                    pe.wait_ge(tp_dve, 4 * TP_MIX[L] + t + 1)
                    unit(u0 + 8 + 2 * t)
                    unit(u0 + 9 + 2 * t, frees=2 if t == T - 1 else 0)
                for t in range(T):
                    pe.wait_ge(ln_ready, 2 * L * T + t + 1)
                    transpose_tile(TP_RT[L], t, H)

            def router(L):
                pe.wait_ge(tp_act, 4 * (TP_RT[L] + 1))
                pe.wait_ge(tp_dve, 4 * (TP_RT[L] + 1))
                for t in range(T):
                    for k in range(K):
                        mm = pe.matmul(ps[:, 6, t * E:(t + 1) * E], hT[:, k, t * P:(t + 1) * P], rw[:, k, :],
                                       start=k == 0, stop=k == K - 1)
                mm.then_inc(rt_logits, 1)
                pe.wait_ge(rt_picked, L + 1)
                picked = rt[8]
                for t in range(T):
                    for s in range(t + 1):
                        pe.matmul(ps[:, 6, t * E:(t + 1) * E], (upto if s == t else ones)[:, :], picked[:, s, :],
                                  start=s == 0, stop=s == t)
                for s in range(T):
                    mm = pe.matmul(ps[:, 6, T * E:(T + 1) * E], ones[:, :], picked[:, s, :],
                                   start=s == 0, stop=s == T - 1)
                mm.then_inc(rt_ranks, 1)

            def experts(L):
                TB, HB, XT, EX = 18 * L, 19 * L, 17 * L + 1, 16 * L + 1
                if L == 0:
                    for s, n in ((xt_done, 2), (gate_mm, 1), (up_mm, 1), (ht_done, 1), (y_mm, 1), (c_tbl, 1),
                                 (c_xt, 2), (c_gu, 1), (c_ht, 1), (c_y, 1)):
                        pe.sem_inc(s, n)

                def table(e, hots):
                    for s in range(T):
                        mm = pe.matmul(ps[:, 7, 0:3], hots[:, s * P:(s + 1) * P],
                                       info[:, s, bass.ds(e, 1), :].rearrange("p e c -> p (e c)")
                                       if not isinstance(e, int) else info[:, s, e, :],
                                       start=s == 0, stop=s == T - 1)
                    return mm

                def turn_rows(src, done, halves=range(2)):
                    for kk in halves:
                        for j in range(4):
                            mm = pe.transpose(ps[:, kk, j * P:(j + 1) * P],
                                              src[:, (4 * kk + j) * P:(4 * kk + j + 1) * P], ident[:, :])
                        mm.then_inc(done, 1)

                def w_of(n, k):
                    return ring[:, n % RING, :].rearrange("p (k n) -> p k n", k=k)

                def gate_up(xT, n, bank):
                    for k in range(K):
                        mm = pe.matmul(ps[:, bank, :], xT[:, k * P:(k + 1) * P], w_of(n, K)[:, k, :],
                                       start=k == 0, stop=k == K - 1)
                    return mm

                def down(n):
                    w = w_of(n, KE)
                    for b in range(2):
                        for k in range(KE):
                            mm = pe.matmul(ps[:, 4 + b, :], hidT[:, k * P:(k + 1) * P],
                                           w[:, k, b * BANK:(b + 1) * BANK], start=k == 0, stop=k == KE - 1)
                    return mm

                def turn_hidden():
                    for k in range(KE):
                        mm = pe.transpose(ps[:, 6, k * P:(k + 1) * P], hid[:, k * P:(k + 1) * P], ident[:, :])
                    return mm

                pe.wait_ge(rt_ready, L + 1)
                for e in range(2):
                    pe.wait_ge(hot, HB + e + 1)
                    if e:
                        pe.wait_ge(tbl_ev, 2 * (TB + e))
                    table(e, onehot[:, e, :]).then_inc(tbl_done, 1)
                pe.wait_ge(gathered[0], 16 * (9 * L + 1))
                turn_rows(xg[:, 0, :], xt_done)
                pe.wait_ge(tbl_ev, 2 * (TB + 2))
                with pe.Fori(0, E // BODY) as i:
                    for j in range(BODY):
                        e = i * BODY + j
                        n0 = moe0[L] + 3 * j

                        def piece(n):
                            pe.wait_ge(w_loaded[n % RING], i * (16 * 3 * BODY // RING) + 16 * (n // RING + 1))

                        xT = xgT[:, j % 2, :]
                        pe.wait_ge(hot, e + HB + 3)
                        table(e + 2, onehot[:, j % 2, :]).then_inc(tbl_done, 1)
                        piece(n0)
                        pe.wait_ge(xt_ev, (e + XT + 1) * 2)
                        gate_up(xT, n0, 2).then_inc(gate_mm, 1)
                        piece(n0 + 1)
                        gate_up(xT, n0 + 1, 3).then_inc(up_mm, 1)
                        n_rows = pe.value_load(counts[0:1, bass.ds(e, 1)], min_val=0, max_val=S)
                        b = (j + 1) % 2
                        pe.wait_ge(gathered[b], (i * 2 + 9 * L + (j + 1) // 2 + 1) * 16)
                        turn_rows(xg[:, b, :], xt_done, range(1))
                        pe.wait_ge(hid_done, e + EX + 1)
                        turn_hidden().then_inc(ht_done, 1)
                        turn_rows(xg[:, b, :], xt_done, range(1, 2))
                        piece(n0 + 2)
                        pe.wait_ge(ht_ev, e + EX + 1)
                        pe.wait_ge(y_act, e + EX)
                        pe.wait_ge(y_dve, e + EX)
                        down(n0 + 2).then_inc(y_mm, 1)
                        with pe.If(n_rows > P):
                            before = pe.value_load(parts[0:1, bass.ds(e, 1)], min_val=0, max_val=6 * E + 1)
                            with pe.Fori(0, 3) as m:
                                c = before + m
                                pe.wait_ge(tbl_ev, (e + TB + 3) * 2)
                                pe.wait_ge(xt_ev, (e + XT + 2) * 2)
                                pe.wait_ge(y_act, e + EX + 1)
                                pe.wait_ge(y_dve, e + EX + 1)
                                pe.wait_ge(c_ya, c)
                                pe.wait_ge(c_yd, c)
                                pe.wait_ge(c_hot, c + 1)
                                table(e, coneh).then_inc(c_tbl, 1)
                                pe.wait_ge(c_gat, c * 16)
                                turn_rows(cxg, c_xt)
                                pe.wait_ge(c_xe, (c + 1) * 2)
                                gate_up(cxgT, n0, 2)
                                gate_up(cxgT, n0 + 1, 3).then_inc(c_gu, 1)
                                pe.wait_ge(c_hid, c + 1)
                                turn_hidden().then_inc(c_ht, 1)
                                pe.wait_ge(c_he, c + 1)
                                down(n0 + 2).then_inc(c_y, 1)
                            pe.wait_ge(c_ya, before + 3)
                            pe.wait_ge(c_yd, before + 3)
                            pe.matmul(ps[:, 7, 0:2], ident[:, :], ident[:, 0:2], start=True, stop=True)
                        with pe.Else():
                            pe.nop()
                        pe.wait_ge(tbl_ev, (e + TB + 3) * 2)
                        marker(3)

            pe.wait_ge(consts, 18)
            for t in range(T):
                pe.wait_ge(x_loaded[t], 16)
                transpose_tile(TP_X, t, H)
            pe.wait_ge(par_loaded, 16 * 8)
            pe.wait_ge(tp_act, T)
            pe.wait_ge(tp_dve, T)
            for k in range(K):
                mm = pe.matmul(ps[0:RANK, 6, :], grw[:, k, :], hT[:, k, :], start=k == 0, stop=k == K - 1)
            mm.then_inc(gr_done, 1)
            for f in range(H_A):
                unit(f)
            pe.wait_ge(gr_ev, 2)
            for t in range(T):
                if t >= 1:
                    pe.wait_ge(z_abs, t)
                pe.matmul(ps[:, 6, :], gr_in[:, t * P:(t + 1) * P], wgk, start=True, stop=True).then_inc(z_done, 1)
            marker(1)
            for u in range(H_A, 2 * H_A):
                unit(u, frees=1 if u == 2 * H_A - 1 else 0)
            for u in range(2 * H_A, U_GLA_TAIL):
                unit(u, frees=1 if u % T == T - 1 else 0)

            def decay_sums(h):
                pe.wait_ge(gk_ready, T) if h == 0 else pe.wait_ge(bc_exp, 6 * h)
                for t in range(T):
                    mm = pe.matmul(ps[:, t // 2, (t % 2) * 2 * P:(t % 2 + 1) * 2 * P],
                                   gk[:, t, h * DK:(h + 1) * DK], chunk_sums[:, :], start=True, stop=True)
                    if t % 2:
                        mm.then_inc(bc_done, 1)

            for s in (ev_act, ev_dve):
                pe.wait_ge(s, sum(1 for x_ in units[:U_GLA_TAIL] if x_[3] == ("act" if s is ev_act else "dve")))
            decay_sums(0)
            for h in range(H_A):
                b = h % 2
                pe.wait_ge(decayed, 3 * (h + 1))
                if h:
                    pe.wait_ge(kt_ev, h)
                for t in range(T):
                    mm = pe.transpose(ps[:, 2, t * P:(t + 1) * P], k_end[:, b, t * P:(t + 1) * P], ident[:, :])
                mm.then_inc(kt_done, 1)
                if h:
                    pe.wait_ge(att_ev, h)
                for t in range(T):
                    mm = pe.matmul(ps[:, 3, t * P:(t + 1) * P], k_inv[:, b, t * P:(t + 1) * P],
                                   q_a[:, h, t * P:(t + 1) * P], start=True, stop=True)
                mm.then_inc(att_done, 1)
                if h + 1 < H_A:
                    decay_sums(h + 1)
                pe.wait_ge(kt_ev, h + 1)
                for t in range(T):
                    if t == 1:
                        pe.wait_ge(att_ev, h + 1)
                    elif 2 * h + t >= 2:
                        pe.wait_ge(st_done, 7 * h + 2 * t - 2 if t else 7 * h - 1)
                    for c in range(CPT if t < T - 1 else 1):
                        mm = pe.matmul(ps[:, KV_BANKS[t % 2] + c, 0:DV],
                                       k_tok[c * CH:(c + 1) * CH, t, :],
                                       mix[c * CH:(c + 1) * CH, t, h * DV:(h + 1) * DV], start=True, stop=True)
                    mm.then_inc(kv_done, 1)
                pe.wait_ge(att_ev, h + 1)
                for t in range(T):
                    if 4 * h + t >= 2:
                        pe.wait_ge(o_ev, 4 * h + t - 1)
                    pe.wait_ge(st_done, 7 * h + 2 * t + 1)
                    bank = ps[:, 6 + t % 2, 0:DV]
                    mm = pe.matmul(bank, att[:, t, :], mix[:, t, h * DV:(h + 1) * DV], start=True, stop=False,
                                   skip_group_check=True)
                    for c in range(CPT):
                        n = CPT * t + c
                        if n:
                            mm = pe.matmul(ps[c * CH:(c + 1) * CH, 6 + t % 2, 0:DV],
                                           q_a[:, h, n * CH:(n + 1) * CH], states[:, n, :],
                                           start=False, stop=True, skip_group_check=True)
                    mm.then_inc(o_done, 1)
            pe.wait_ge(o_ev, 4 * H_A)
            tail(0)
            router(0)
            experts(0)
            for t in range(T):
                pe.wait_ge(ln_ready, T + t + 1)
                transpose_tile(TP_L0, t, H)
            pe.wait_ge(tp_act, 4 * (TP_L0 + 1))
            pe.wait_ge(tp_dve, 4 * (TP_L0 + 1))
            for t in range(T):
                for k in range(K):
                    mm = pe.matmul(ps[:, 6, t * H_B:(t + 1) * H_B], hT[:, k, t * P:(t + 1) * P], kvf[:, k, :],
                                   start=k == 0, stop=k == K - 1)
            mm.then_inc(fl_done, 1)
            for u in range(U_FOX, U_QUARTERS):
                unit(u, frees=1 if (u - U_FOX) % T == T - 1 else 0)
            pe.wait_ge(f_ready, 1)
            for t in range(T):
                for s in range(t + 1):
                    mm = pe.matmul(ps[0:H_B, 7, t * P:(t + 1) * P], f_log[:, s * H_B:(s + 1) * H_B],
                                   (upto if s == t else ones)[:, :], start=s == 0, stop=s == t)
            mm.then_inc(cum_done, 1)
            pe.wait_ge(cum_ev, 2)
            for c in range(4):
                for m in range(4):
                    last = c % 2 == 1 and m in (1, 3)
                    unit(U_QUARTERS + 4 * c + m, frees=1 if last else 0)
                b = c % 2
                pe.wait_ge(cum_put[c % 2], 32 * (c // 2 + 1))
                pe.wait_ge(*taken(U_QUARTERS + 4 * c + 1))
                pe.wait_ge(*taken(U_QUARTERS + 4 * c + 3))

                def scores(r):
                    g, (s, i) = 16 * c + r, divmod(r, T)
                    if g >= 2:
                        pe.wait_ge(p_done, g - 1)
                    pe.matmul(ps[:, g % 2, 0:(i + 1) * P], qa[0:DH + 2, b, s, i * P:(i + 1) * P],
                              ka[0:DH + 2, b, s, 0:(i + 1) * P], start=True, stop=True).then_inc(sc_done, 1)

                def turn(r):
                    g, i = 16 * c + r, r % T
                    pe.wait_ge(p_done, g + 1)
                    if g >= 2:
                        pe.wait_ge(pt_ev, g - 1)
                    for n in range(i + 1):
                        mm = pe.transpose(ps[:, 2 + g % 2, n * P:(n + 1) * P], prob[:, g % 2, n * P:(n + 1) * P],
                                          ident[:, :])
                    mm.then_inc(pt_done, 1)

                def values(r):
                    g, (s, i) = 16 * c + r, divmod(r, T)
                    hd = 4 * c + s
                    pe.wait_ge(pt_ev, g + 1)
                    if g >= 2:
                        pe.wait_ge(pv_ev, g - 1)
                    for n in range(i + 1):
                        mm = pe.matmul(ps[:, 4 + g % 2, 0:DH], prob_t[:, g % 2, n * P:(n + 1) * P],
                                       v_b[:, n, hd * DH:(hd + 1) * DH], start=n == 0, stop=n == i)
                    mm.then_inc(pv_done, 1)

                for r in range(16 + 2):
                    if r < 16:
                        scores(r)
                    if 1 <= r <= 16:
                        turn(r - 1)
                    if r >= 2:
                        values(r - 2)
                pe.wait_ge(pv_ev, 16 * (c + 1))
            tail(1)
            router(1)
            experts(1)

        @block.scalar
        def _(act):
            own = Steps(act_step)
            w_in = gla_w_in[0]
            act.dma_start(grw, w_in[:, 2 * HK + 2 * HV:].rearrange("(k p) n -> p k n", p=P)).then_inc(par_loaded, 16)
            act.dma_start(wgk[0:RANK, :], gla_w_gk[0]).then_inc(par_loaded, 16)
            act.dma_start(wgk[RANK:RANK + 1, :], gla_b_gk).then_inc(par_loaded, 16)
            act.dma_start(normg, gla_norm_g.to_broadcast([P, DV])).then_inc(par_loaded, 16)
            act.dma_start(rw[:, :, :], router_w.rearrange("(k p) n -> p k n", p=P)).then_inc(par_loaded, 16)
            act.dma_start(rbias[:, :], router_bias.rearrange("(a e) -> a e", a=1).to_broadcast([P, E])
                          ).then_inc(par_loaded, 16)
            act.dma_start(fbias[:, :], forget_bias.rearrange("(a e) -> a e", a=1).to_broadcast([P, H_B])
                          ).then_inc(par_loaded, 16)
            act.dma_start(kvf[:, :, :], kv_w[:, 2 * D:].rearrange("(k p) n -> p k n", p=P)).then_inc(par_loaded, 16)

            def take_tile(turn, t):
                act.wait_ge(tp_done, 8 * turn + 2 * t + 1)
                act.copy(hT[:, 0:4, t * P:(t + 1) * P],
                         ps[:, 0, :].rearrange("p (k n) -> p k n", k=4)).then_inc(tp_act, 1)

            def take(u):
                kind, _, blk, engine = units[u]
                if engine != "act":
                    return
                act.wait_ge(proj_done, u + 1)
                src = ps[:, 2 + u % 4, :]
                if kind == "qa":
                    ins = act.copy(q_a[:, blk, :], src)
                elif kind == "va":
                    ins = act.copy(mix[:, blk[1], blk[0] * BANK:(blk[0] + 1) * BANK], src)
                elif kind == "vb":
                    ins = act.copy(v_b[:, blk[1], blk[0] * BANK:(blk[0] + 1) * BANK], src)
                elif kind == "qb":
                    c, f = blk
                    if f == 0 and c >= 2:
                        act.wait_ge(pv_done, 16 * (c - 1))
                    own.mark(act.mul(qa[0:DH, c % 2, 2 * f, :], ps[0:DH, 2 + u % 4, :], float(DH) ** -0.5))
                    ins = act.mul(qa[0:DH, c % 2, 2 * f + 1, :], ps[DH:P, 2 + u % 4, :], float(DH) ** -0.5)
                ins.then_inc(ev_act, 1)

            def tail(L):
                u0, _, gate, func = tails[L]
                for s in range(T + 1):
                    if s < T:
                        for p in range(2):
                            u = u0 + 2 * s + p
                            act.wait_ge(proj_done, u + 1)
                            if 2 * s + p >= 2:
                                act.wait_ge(gated, 8 * L + 2 * s + p - 1)
                            act.activation(gate[:, p, :], ps[:, 2 + u % 4, :], func).then_inc(ev_act, 1)
                    if s >= 1:
                        take_tile(TP_MIX[L], s - 1)
                layer_norm(2 * L)
                for t in range(T):
                    take_tile(TP_RT[L], t)

            def layer_norm(N):
                for t in range(T):
                    act.wait_ge(ln_bias, N * T + t + 1)
                    act.activation(H[:, t, :], H[:, t, :], ACT.Identity, bias=ln_r[:, t, 2:3],
                                   scale=ln_r[:, t, 1:2]).then_inc(ln_norm, 1)

            def router(L):
                act.wait_ge(rt_in, L + 1)
                act.activation(rt[1], rt[0], ACT.Exp).then_inc(rt_exp, 1)

            def experts(L):
                XT, EX = 17 * L + 1, 16 * L + 1
                if L == 0:
                    for s, n in ((xt_ev, 2), (silu_done, 1), (y_act, 1), (c_xe, 2), (c_silu, 1), (c_ya, 1)):
                        act.sem_inc(s, n)

                def take_rows(dst, at_done, base):
                    for kk in range(2):
                        act.wait_ge(at_done, base + kk + 1)
                        yield act.copy(dst[:, kk * BANK:(kk + 1) * BANK], ps[:, kk, :])

                for ins in take_rows(xgT[:, 0, :], xt_done, 2 * XT):
                    ins.then_inc(xt_ev, 1)
                with act.Fori(0, E // BODY) as i:
                    for j in range(BODY):
                        e = i * BODY + j
                        n_rows = act.value_load(counts[0:1, bass.ds(e, 1)], min_val=0, max_val=S)
                        act.wait_ge(gate_mm, e + EX + 1)
                        act.wait_ge(hid_done, e + EX)
                        act.activation(silu, ps[:, 2, :], ACT.Silu).then_inc(silu_done, 1)
                        for ins in take_rows(xgT[:, (j + 1) % 2, :], xt_done, (e + XT + 1) * 2):
                            ins.then_inc(xt_ev, 1)
                        act.wait_ge(y_mm, e + EX + 1)
                        act.wait_ge(scattered[j % 2], (i * 2 + 8 * L + 1 + j // 2) * 16)
                        act.copy(yb[:, j % 2, 0:BANK], ps[:, 4, :]).then_inc(y_act, 1)
                        with act.If(n_rows > P):
                            before = act.value_load(parts[0:1, bass.ds(e, 1)], min_val=0, max_val=6 * E + 1)
                            with act.Fori(0, 3) as m:
                                c = before + m
                                for ins in take_rows(cxgT, c_xt, c * 2):
                                    ins.then_inc(c_xe, 1)
                                act.wait_ge(c_gu, c + 1)
                                act.wait_ge(hid_done, e + EX + 1)
                                act.wait_ge(c_hid, c)
                                act.activation(silu, ps[:, 2, :], ACT.Silu).then_inc(c_silu, 1)
                                act.wait_ge(c_y, c + 1)
                                act.wait_ge(c_sca, c * 16)
                                act.copy(cyb[:, 0:BANK], ps[:, 4, :]).then_inc(c_ya, 1)
                        with act.Else():
                            act.nop()
                        act.nop()

            for t in range(T):
                take_tile(TP_X, t)
            for u in range(H_A):
                take(u)
            z_t = states.rearrange("p a b -> p (a b)").rearrange("p (t n) -> p t n", t=T)
            for t in range(T):
                act.wait_ge(z_min, t + 1)
                act.activation(z_t[:, t, :], ps[:, 6, :], ACT.Abs).then_inc(z_abs, 1)
            for t in range(T):
                act.wait_ge(z_abs, t + 1)
                own.mark(act.activation(z_t[:, t, :], z_t[:, t, :], ACT.Exp, scale=-1.0))
            for t in range(T):
                own.settle(act)
                act.activation(z_t[:, t, :], z_t[:, t, :], ACT.Ln, bias=1.0).then_inc(z_ln, 1)
            for u in range(H_A, U_GLA_TAIL):
                take(u)

            def exps(h):
                b = h % 2
                for m in range(2):
                    act.wait_ge(bc_done, 2 * h + m + 1)
                    if h >= 2 and m == 0:
                        act.wait_ge(o_ev, 4 * (h - 1))
                    src = ps[:, m, :].rearrange("p (t c n) -> p t c n", t=2, c=2)
                    cols = slice(m * 2 * P, (m + 1) * 2 * P)
                    for dst, part, sign in ((e_bc, 0, 1.0), (k_inv, 0, -1.0), (k_end, 1, 1.0)):
                        act.activation(dst[:, b, cols].rearrange("p (t n) -> p t n", t=2), src[:, :, part, :],
                                       ACT.Exp, scale=sign).then_inc(bc_exp, 1)

            exps(0)
            for h in range(H_A):
                if h + 1 < H_A:
                    exps(h + 1)
                for t in range(T):
                    act.wait_ge(o_ev, 4 * h + t + 1)
                    if 4 * h + t:
                        act.wait_ge(sq_done, 4 * h + t)
                    act.activation(squares, mix[:, t, h * DV:(h + 1) * DV], ACT.Square,
                                   accum_out=ssq[:, t * H_A + h:t * H_A + h + 1]).then_inc(sq_done, 1)
            tail(0)
            router(0)
            experts(0)
            layer_norm(1)
            for t in range(T):
                take_tile(TP_L0, t)
            act.wait_ge(fl_z, 1)
            own.mark(act.activation(f_tmp, f_tmp, ACT.Abs))
            own.settle(act)
            own.mark(act.activation(f_tmp, f_tmp, ACT.Exp, scale=-1.0))
            own.settle(act)
            act.activation(f_tmp, f_tmp, ACT.Ln, bias=1.0).then_inc(fl_ln, 1)
            for u in range(U_FOX, U_QUARTERS):
                take(u)
            for c in range(4):
                for m in range(4):
                    take(U_QUARTERS + 4 * c + m)
                for r in range(16):
                    g, i = 16 * c + r, r % T
                    act.wait_ge(sc_max, g + 1)
                    if g >= 2:
                        act.wait_ge(pt_done, g - 1)
                    if g == 0:
                        act.wait_ge(cum_stored, 16)
                    act.activation(prob[:, g % 2, 0:(i + 1) * P], ps[:, g % 2, 0:(i + 1) * P], ACT.Exp,
                                   bias=nmax[:, g:g + 1], accum_out=rsum[:, g:g + 1]).then_inc(p_done, 1)
            tail(1)
            router(1)
            experts(1)
            layer_norm(3)

        @block.vector
        def _(dve):
            own = Steps(dve_step)

            def do(ins):
                own.mark(ins)
                own.settle(dve)

            def take_tile(turn, t):
                dve.wait_ge(tp_done, 8 * turn + 2 * t + 2)
                dve.tensor_copy(hT[:, 4:8, t * P:(t + 1) * P],
                                ps[:, 1, :].rearrange("p (k n) -> p k n", k=4)).then_inc(tp_dve, 1)

            def take(u):
                kind, _, blk, engine = units[u]
                if engine != "dve":
                    return
                dve.wait_ge(proj_done, u + 1)
                src = ps[:, 2 + u % 4, :]
                if kind == "ka":
                    ins = dve.tensor_copy(k_a[:, blk, :], src)
                elif kind == "va":
                    ins = dve.tensor_copy(mix[:, blk[1], blk[0] * BANK:(blk[0] + 1) * BANK], src)
                elif kind == "vb":
                    ins = dve.tensor_copy(v_b[:, blk[1], blk[0] * BANK:(blk[0] + 1) * BANK], src)
                elif kind == "kb":
                    c, f = blk
                    if f == 0 and c >= 2:
                        dve.wait_ge(pv_done, 16 * (c - 1))
                    own.mark(dve.tensor_copy(ka[0:DH, c % 2, 2 * f, :], ps[0:DH, 2 + u % 4, :]))
                    ins = dve.tensor_copy(ka[0:DH, c % 2, 2 * f + 1, :], ps[DH:P, 2 + u % 4, :])
                ins.then_inc(ev_dve, 1)

            def layer_norm(N, add):
                for s in range(T + 2):
                    if s < T:
                        add(s)
                        for p in range(2):
                            own.mark(dve.bn_stats(ln_bn[:, s, p, :], H[:, s, p * BANK:(p + 1) * BANK]))
                        own.settle(dve)
                        do(dve.bn_aggr(ln_mv[:, s, :], ln_bn[:, s, :, :].rearrange("p a b -> p (a b)")))
                        dve.tensor_scalar(ln_r[:, s, 0:1], ln_mv[:, s, 1:2], LN_EPS, None,
                                          ALU.add).then_inc(ln_stats, 1)
                    if 1 <= s <= T:
                        t = s - 1
                        dve.wait_ge(ln_rstd, N * T + t + 1)
                        dve.scalar_tensor_tensor(out=ln_r[:, t, 2:3], in0=ln_mv[:, t, 0:1], scalar=-1.0,
                                                 in1=ln_r[:, t, 1:2], op0=ALU.mult,
                                                 op1=ALU.mult).then_inc(ln_bias, 1)
                    if s >= 2:
                        t = s - 2
                        dve.wait_ge(ln_norm, N * T + t + 1)
                        dve.wait_ge(lnp_loaded, 32 * (N + 1))
                        dve.tensor_tensor(H[:, t, :], H[:, t, :], ln_p[:, 0, :], ALU.mult).then_inc(ln_scaled, 1)

            def tail(L):
                u0, src, gate, _ = tails[L]
                for s in range(T + 1):
                    if s < T:
                        for p in range(2):
                            dve.wait_ge(*taken(u0 + 2 * s + p))
                            v = src[:, s, p * BANK:(p + 1) * BANK]
                            dve.tensor_tensor(v, v, gate[:, p, :], ALU.mult).then_inc(gated, 1)
                    if s >= 1:
                        take_tile(TP_MIX[L], s - 1)

                def add(t):
                    for p in range(2):
                        u = u0 + 8 + 2 * t + p
                        dve.wait_ge(proj_done, u + 1)
                        hp = H[:, t, p * BANK:(p + 1) * BANK]
                        dve.scalar_tensor_tensor(out=hp, in0=hp, scalar=ALPHA, in1=ps[:, 2 + u % 4, :],
                                                 op0=ALU.mult, op1=ALU.add).then_inc(ev_dve, 1)
                    dve.wait_ge(*taken(u0 + 8 + 2 * t + 1))

                layer_norm(2 * L, add)
                for t in range(T):
                    take_tile(TP_RT[L], t)

            def router(L):
                def over_e(v):
                    return v.unsqueeze(2).to_broadcast([P, T, E])

                def each_t(v, n):
                    return v.unsqueeze(1).to_broadcast([P, T, n])

                logits = ps[:, 6, 0:T * E].rearrange("p (t e) -> p t e", t=T)
                dve.wait_ge(rt_logits, L + 1)
                do(dve.tensor_reduce(rv[0], logits, AX.X, ALU.max))
                dve.tensor_tensor(rt[0], logits, over_e(rv[0]), ALU.subtract).then_inc(rt_in, 1)
                dve.wait_ge(rt_exp, L + 1)
                do(dve.tensor_reduce(rv[1], rt[1], AX.X, ALU.add))
                do(dve.reciprocal(rv[2], rv[1]))
                scores, sel = rt[2], rt[3]
                do(dve.tensor_tensor(scores, rt[1], over_e(rv[2]), ALU.mult))
                do(dve.tensor_tensor(sel, scores, each_t(rbias[:, :], E), ALU.add))
                pair = sel.rearrange("p t (g a b) -> p (t g) a b", g=GROUPS, a=2)
                big = rt[4].rearrange("p t e -> p (t e)")[:, 0:2 * T * GROUPS].rearrange("p (n a) -> p n a", a=2)
                small = rt[5].rearrange("p t e -> p (t e)")[:, 0:2 * T * GROUPS].rearrange("p (n a) -> p n a", a=2)
                own.mark(dve.tensor_tensor(big, pair[:, :, :, 0], pair[:, :, :, 1], ALU.max))
                do(dve.tensor_tensor(small, pair[:, :, :, 0], pair[:, :, :, 1], ALU.min))
                flat = [v.rearrange("p t g -> p (t g)") for v in rs]
                own.mark(dve.tensor_tensor(flat[0], big[:, :, 0], big[:, :, 1], ALU.max))
                own.mark(dve.tensor_tensor(flat[1], big[:, :, 0], big[:, :, 1], ALU.min))
                do(dve.tensor_tensor(flat[2], small[:, :, 0], small[:, :, 1], ALU.max))
                do(dve.tensor_tensor(flat[1], flat[1], flat[2], ALU.max))
                do(dve.tensor_tensor(rs[3], rs[0], rs[1], ALU.add))

                def first_largest(v, iota, n, hit, key, most, low):
                    def wide(a):
                        return a.unsqueeze(2).to_broadcast([P, T, n])
                    do(dve.tensor_reduce(most, v, AX.X, ALU.max))
                    do(dve.tensor_tensor(hit, v, wide(most), ALU.is_equal))
                    do(dve.tensor_scalar(hit, hit, -float(n), None, ALU.mult))
                    do(dve.tensor_tensor(key, hit, each_t(iota, n), ALU.add))
                    do(dve.tensor_reduce(low, key, AX.X, ALU.min))
                    do(dve.tensor_tensor(hit, key, wide(low), ALU.is_equal))

                first_largest(rs[3], iota_g[:, :], GROUPS, rs[4], rs[5], rv[3], rv[4])
                in_group = rs[4].unsqueeze(3).to_broadcast([P, T, GROUPS, EPG])
                four = [v.rearrange("p t (g e) -> p t g e", g=GROUPS) for v in rt]
                do(dve.tensor_scalar(rs[5], rs[4], -LOW, LOW, ALU.mult, ALU.add))
                outside = rs[5].unsqueeze(3).to_broadcast([P, T, GROUPS, EPG])
                do(dve.tensor_tensor(four[4], four[3], in_group, ALU.mult))
                do(dve.tensor_tensor(four[4], four[4], outside, ALU.add))
                first_largest(rt[4], iota_e[:, :], E, rt[5], rt[6], rv[3], rv[4])
                do(dve.scalar_tensor_tensor(out=rt[4], in0=rt[5], scalar=LOW, in1=rt[4], op0=ALU.mult, op1=ALU.add))
                first_largest(rt[4], iota_e[:, :], E, rt[7], rt[6], rv[3], rv[4])
                dve.tensor_tensor(rt[8], rt[5], rt[7], ALU.add).then_inc(rt_picked, 1)
                dve.wait_ge(rt_picked, L + 1)
                do(dve.tensor_tensor(rt[9], scores, rt[8], ALU.mult))
                do(dve.tensor_reduce(rv[5], rt[9], AX.X, ALU.add))
                do(dve.reciprocal(rv[6], rv[5]))
                own.mark(dve.memset(info[:, :, E:E + 2, :], 0.0))
                own.mark(dve.memset(ranks[:, :, E:E + 3], 0.0))
                own.mark(dve.tensor_copy(info[:, :, 0:E, 0], over_e(row_id[:, :])))
                own.mark(dve.scalar_tensor_tensor(out=info[:, :, 0:E, 1], in0=rt[7], scalar=float(S),
                                                  in1=over_e(row_id[:, :]), op0=ALU.mult, op1=ALU.add))
                do(dve.tensor_tensor(info[:, :, 0:E, 2], rt[9], over_e(rv[6]), ALU.mult))
                dve.wait_ge(rt_ranks, L + 1)
                do(dve.tensor_tensor(ranks[:, :, 0:E], ps[:, 6, 0:T * E].rearrange("p (t e) -> p t e", t=T),
                                     rt[8], ALU.mult))
                total = ps[0:1, 6, T * E:(T + 1) * E]
                own.mark(dve.tensor_copy(counts[:, :], total))
                if L == 0:
                    do(dve.memset(scan[:, :, :], 0.0))
                    do(dve.memset(scan[:, 1, 0:1], 1.0))
                else:
                    do(dve.tensor_copy(scan[:, 1, 0:1], scan[:, 0, E + 7:E + 8]))
                    do(dve.memset(scan[:, :, 1:8], 0.0))
                    do(dve.memset(scan[:, 0, 0:1], 0.0))
                do(dve.tensor_scalar(scan[:, 0, 8:], total, float(P), 3.0, ALU.is_gt, ALU.mult))
                do(dve.tensor_copy(part3[:, :], scan[:, 0, 8:]))
                for m, d in enumerate((1, 2, 4, 8)):
                    a, b = scan[:, m % 2, :], scan[:, 1 - m % 2, :]
                    if m == 0:
                        do(dve.tensor_copy(carry[:, :], scan[:, 1, 0:1]))
                        do(dve.memset(scan[:, 1, 0:1], 0.0))
                    do(dve.tensor_tensor(b[:, 8:], a[:, 8:], a[:, 8 - d:8 - d + E], ALU.add))
                do(dve.tensor_scalar(scan[:, 0, 8:], scan[:, 0, 8:], carry[:, 0:1], None, ALU.add))
                dve.tensor_tensor(parts[:, :], scan[:, 0, 8:], part3[:, :], ALU.subtract).then_inc(rt_ready, 1)
                dve.wait_ge(rt_ready, L + 1)

            def experts(L):
                TB, EX, SC = 18 * L, 16 * L + 1, 8 * L + 1
                if L == 0:
                    for s, n in ((hid_done, 1), (ht_ev, 1), (y_dve, 1), (c_copy, 1), (c_rank, 1), (c_hot, 1), (c_idx, 2),
                                 (c_hid, 1), (c_he, 1), (c_yd, 1)):
                        dve.sem_inc(s, n)

                def take_table(rows, gate, done):
                    dve.tensor_scalar(rows, ps[:, 7, 0:2], BIG, None, ALU.add).then_inc(done, 1)
                    dve.tensor_copy(gate, ps[:, 7, 2:3]).then_inc(done, 1)

                def hidden(gate):
                    return dve.scalar_tensor_tensor(out=hid, in0=silu, scalar=gate, in1=ps[:, 3, :],
                                                    op0=ALU.mult, op1=ALU.mult)

                for e in range(2):
                    one_hots4(dve, e, onehot[:, e, :], hot, ranks, slot1)
                for e in range(2):
                    dve.wait_ge(tbl_done, TB + e + 1)
                    take_table(tokv[:, e, :], tokg[:, e:e + 1], tbl_ev)
                    if e == 0:
                        one_hots4(dve, 2, onehot[:, 0, :], hot, ranks, slot1)
                with dve.Fori(0, E // BODY) as i:
                    for j in range(BODY):
                        e = i * BODY + j
                        dve.wait_ge(tbl_done, e + TB + 3)
                        dve.wait_ge(scattered[j % 2], (i * 2 + SC + j // 2) * 16)
                        take_table(tokv[:, (j + 2) % 4, :], tokg[:, (j + 2) % 4:(j + 2) % 4 + 1], tbl_ev)
                        one_hots4(dve, e + 3, onehot[:, (j + 1) % 2, :], hot, ranks, slot1)
                        n_rows = dve.value_load(counts[0:1, bass.ds(e, 1)], min_val=0, max_val=S)
                        dve.wait_ge(tbl_ev, (e + TB + 1) * 2)
                        dve.wait_ge(silu_done, e + EX + 1)
                        dve.wait_ge(up_mm, e + EX + 1)
                        dve.wait_ge(ht_done, e + EX)
                        hidden(tokg[:, j:j + 1]).then_inc(hid_done, 1)
                        dve.wait_ge(ht_done, e + EX + 1)
                        dve.wait_ge(y_mm, e + EX)
                        dve.tensor_copy(hidT, ps[:, 6, :]).then_inc(ht_ev, 1)
                        dve.wait_ge(y_mm, e + EX + 1)
                        dve.tensor_copy(yb[:, j % 2, BANK:2 * BANK], ps[:, 5, :]).then_inc(y_dve, 1)
                        with dve.If(n_rows > P):
                            before = dve.value_load(parts[0:1, bass.ds(e, 1)], min_val=0, max_val=6 * E + 1)
                            dve.tensor_copy(cold_rank[:, :].unsqueeze(2), ranks[:, :, bass.ds(e, 1)]
                                            ).then_inc(c_copy, 3)
                            with dve.Fori(0, 3) as m:
                                c = before + m
                                dve.wait_ge(c_copy, before + 3)
                                dve.wait_ge(c_hot, c)
                                dve.tensor_scalar(cold_rank[:, :], cold_rank[:, :], -float(P), None,
                                                  ALU.add).then_inc(c_rank, 1)
                                dve.wait_ge(c_rank, c + 1)
                                for s in range(T - 1):
                                    dve.tensor_scalar(coneh[:, s * P:(s + 1) * P], slot1[:, :],
                                                      cold_rank[:, s:s + 1], None, ALU.is_equal)
                                s = T - 1
                                dve.tensor_scalar(coneh[:, s * P:(s + 1) * P], slot1[:, :],
                                                  cold_rank[:, s:s + 1], None, ALU.is_equal).then_inc(c_hot, 1)
                                dve.wait_ge(c_tbl, c + 1)
                                dve.wait_ge(c_sca, c * 16)
                                take_table(cold_rows[:, :], cold_gate[:, :], c_idx)
                                dve.wait_ge(c_silu, c + 1)
                                dve.wait_ge(c_idx, (c + 1) * 2)
                                hidden(cold_gate[:, 0:1]).then_inc(c_hid, 1)
                                dve.wait_ge(c_ht, c + 1)
                                dve.tensor_copy(hidT, ps[:, 6, :]).then_inc(c_he, 1)
                                dve.wait_ge(c_y, c + 1)
                                dve.tensor_copy(cyb[:, BANK:2 * BANK], ps[:, 5, :]).then_inc(c_yd, 1)
                        with dve.Else():
                            dve.nop()
                        dve.nop()

                def add(t):
                    dve.wait_ge(y_loaded[t % 2], 16 * (2 * L + t // 2 + 1))
                    do(dve.scalar_tensor_tensor(out=H[:, t, :], in0=H[:, t, :], scalar=ALPHA,
                                                in1=ysum[:, t % 2, 0:D], op0=ALU.mult, op1=ALU.add))
                    do(dve.tensor_tensor(H[:, t, :], H[:, t, :], ysum[:, t % 2, D:2 * D], ALU.add))

                layer_norm(2 * L + 1, add)

            dve.memset(gr_in, 1.0).then_inc(gr_ev, 1)
            for t in range(T):
                take_tile(TP_X, t)
            dve.wait_ge(gr_done, 1)
            dve.wait_ge(gr_ev, 1)
            dve.tensor_copy(gr_in[0:RANK, :], ps[0:RANK, 6, :]).then_inc(gr_ev, 1)
            for t in range(T):
                dve.wait_ge(z_done, t + 1)
                dve.tensor_scalar(gk[:, t, :], ps[:, 6, :], 0.0, None, ALU.min).then_inc(z_min, 1)
            z_t = states.rearrange("p a b -> p (a b)").rearrange("p (t n) -> p t n", t=T)
            for u in range(H_A, 2 * H_A):
                take(u)
            for t in range(T):
                dve.wait_ge(z_ln, t + 1)
                dve.tensor_tensor(gk[:, t, :], gk[:, t, :], z_t[:, t, :], ALU.subtract).then_inc(gk_ready, 1)
            for u in range(2 * H_A, U_GLA_TAIL):
                take(u)

            def decay(h):
                b = h % 2
                dve.wait_ge(bc_exp, 6 * (h + 1))
                dve.scalar_tensor_tensor(out=q_a[:, h, :], in0=q_a[:, h, :], scalar=float(DK) ** -0.5,
                                         in1=e_bc[:, b, :], op0=ALU.mult, op1=ALU.mult).then_inc(decayed, 1)
                for v in (k_inv, k_end):
                    dve.tensor_tensor(v[:, b, :], v[:, b, :], k_a[:, h, :], ALU.mult).then_inc(decayed, 1)

            dve.wait_ge(*taken(H_A - 1))
            dve.wait_ge(*taken(2 * H_A - 1))
            dve.wait_ge(consts, 18)
            dve.wait_ge(par_loaded, 16 * 8)
            decay(0)
            for h in range(H_A):
                b = h % 2
                dve.wait_ge(kt_done, h + 1)
                dve.tensor_copy(k_tok.rearrange("p t n -> p (t n)"), ps[:, 2, :]).then_inc(kt_ev, 1)
                dve.wait_ge(att_done, h + 1)
                mask = chunk_sums[:, 0:P].bitcast(U32).unsqueeze(1).to_broadcast([P, T, P])
                dve.copy_predicated(att, mask, ps[:, 3, :].rearrange("p (t n) -> p t n", t=T)).then_inc(att_ev, 1)
                for n in range(2 * T - 1):
                    t, c = divmod(n, CPT)
                    if c == 0:
                        dve.wait_ge(kv_done, 4 * h + t + 1)
                    kv = ps[:, KV_BANKS[t % 2] + c, 0:DV]
                    if n == 0:
                        dve.tensor_copy(states[:, 1, :], kv).then_inc(st_done, 1)
                    else:
                        dve.wait_ge(st_done, 7 * h + n)
                        last = n * CH + CH - 1
                        dve.scalar_tensor_tensor(out=states[:, n + 1, :], in0=states[:, n, :],
                                                 scalar=e_bc[:, b, last:last + 1], in1=kv,
                                                 op0=ALU.mult, op1=ALU.add).then_inc(st_done, 1)
                if h + 1 < H_A:
                    decay(h + 1)
                for t in range(T):
                    dve.wait_ge(o_done, 4 * h + t + 1)
                    dve.tensor_copy(mix[:, t, h * DV:(h + 1) * DV], ps[:, 6 + t % 2, 0:DV]).then_inc(o_ev, 1)
            dve.wait_ge(sq_done, T * H_A)
            dve.tensor_scalar(ssq, ssq, 1.0 / DV, RMS_EPS, ALU.mult, ALU.add).then_inc(rms_in, 1)
            dve.wait_ge(rms_out, 1)
            for t in range(T):
                for h in range(H_A):
                    v = mix[:, t, h * DV:(h + 1) * DV]
                    own.mark(dve.scalar_tensor_tensor(out=v, in0=v, scalar=rms[:, t * H_A + h:t * H_A + h + 1],
                                                      in1=normg, op0=ALU.mult, op1=ALU.mult))
            own.settle(dve)
            dve.tensor_copy(ssq, rms).then_inc(normed, 1)
            dve.wait_ge(normed, 1)
            tail(0)
            router(0)
            experts(0)
            for t in range(T):
                take_tile(TP_L0, t)
            dve.wait_ge(fl_done, 1)
            f3 = f_tmp.rearrange("p (t h) -> p t h", t=T)
            do(dve.tensor_tensor(f3, ps[:, 6, 0:T * H_B].rearrange("p (t h) -> p t h", t=T),
                                 fbias[:, :].unsqueeze(1).to_broadcast([P, T, H_B]), ALU.add))
            dve.tensor_scalar(f_log, f_tmp, 0.0, None, ALU.min).then_inc(fl_z, 1)
            dve.wait_ge(fl_ln, 1)
            dve.tensor_tensor(f_log, f_log, f_tmp, ALU.subtract).then_inc(f_ready, 1)
            for u in range(U_FOX, U_QUARTERS):
                take(u)
            dve.wait_ge(cum_done, 1)
            dve.tensor_copy(cumT[0:H_B, 0, :], ps[0:H_B, 7, :]).then_inc(cum_ev, 1)
            dve.tensor_scalar(cumT[0:H_B, 1, :], ps[0:H_B, 7, :], -1.0, None, ALU.mult).then_inc(cum_ev, 1)

            def values_out(g):
                hd, i = divmod(g, T)
                dve.wait_ge(pv_done, g + 1)
                dve.tensor_scalar(o_b[:, i, hd * DH:(hd + 1) * DH], ps[:, 4 + g % 2, 0:DH], rinv[:, g:g + 1],
                                  None, ALU.mult).then_inc(pv_ev, 1)

            for c in range(4):
                for m in range(4):
                    take(U_QUARTERS + 4 * c + m)
                for r in range(16 + 2):
                    if r < 16:
                        g, i = 16 * c + r, r % T
                        dve.wait_ge(sc_done, g + 1)
                        diag = ps[:, g % 2, i * P:(i + 1) * P]
                        dve.tensor_tensor(diag, diag, causal[:, :], ALU.add).then_inc(sc_masked, 1)
                        dve.wait_ge(sc_masked, g + 1)
                        dve.tensor_reduce(nmax[:, g:g + 1], ps[:, g % 2, 0:(i + 1) * P], AX.X, ALU.max,
                                          negate=True).then_inc(sc_max, 1)
                    if 1 <= r <= 16:
                        g, i = 16 * c + r - 1, (r - 1) % T
                        dve.wait_ge(pt_done, g + 1)
                        own.mark(dve.reciprocal(rinv[:, g:g + 1], rsum[:, g:g + 1]))
                        if g >= 2:
                            dve.wait_ge(pv_done, g - 1)
                        dve.tensor_copy(prob_t[:, g % 2, 0:(i + 1) * P],
                                        ps[:, 2 + g % 2, 0:(i + 1) * P]).then_inc(pt_ev, 1)
                    if r >= 2:
                        own.settle(dve)
                        values_out(16 * c + r - 2)
            own.settle(dve)
            tail(1)
            router(1)
            experts(1)


def one_hots4(dve, e, dst, done, ranks, slot1):
    T = ranks.shape[1]
    for s in range(T):
        ptr = ranks[:, s, e:e + 1] if isinstance(e, int) else ranks[:, s, bass.ds(e, 1)]
        ins = dve.tensor_scalar(dst[:, s * P:(s + 1) * P], slot1[:, :], ptr, None, ALU.is_equal)
    ins.then_inc(done, 1)


_INS = ["x", "gla_w_in", "gla_w_gk", "gla_b_gk", "gla_norm_g", "gla_w_out", "kv_w", "forget_bias", "fox_w_qg",
        "fox_w_out", "router_w", "router_bias", "moe_w_gate", "moe_w_up", "moe_w_down", "ln_g", "ln_b"]
_OUTS = [((1, 512, 1024), "float32")]


def kernel(**inputs):
    import numpy as _np
    import concourse.bacc as _bacc
    from concourse import mybir as _mybir
    from concourse.bass_utils import run_bass_kernel_spmd as _run

    nc = _bacc.Bacc("TRN2", target_bir_lowering=False, num_devices=1)
    arrays, args = {}, []
    for name in _INS:
        a = _np.ascontiguousarray(inputs[name])
        arrays[f"in_{name}_dram"] = a
        args.append(nc.dram_tensor(f"in_{name}_dram", a.shape, _mybir.dt.from_np(a.dtype), kind="ExternalInput").ap())
    for i, (shape, dtype) in enumerate(_OUTS):
        dt = _mybir.dt.from_np(_np.dtype(dtype))
        args.append(nc.dram_tensor(f"out_{i}_dram", shape, dt, kind="ExternalOutput").ap())
    yoco_trunk(nc, *args)
    r = _run(nc, [arrays], core_ids=[0])
    return r.results[0]["out_0_dram"]
```

```python
from contextlib import ExitStack

import concourse.bass as bass
from concourse import mybir

F32 = mybir.dt.float32
F32R = mybir.dt.float32r
BF16 = mybir.dt.bfloat16
I32 = mybir.dt.int32
U32 = mybir.dt.uint32
ALU = mybir.AluOpType
ACT = mybir.ActivationFunctionType
AX = mybir.AxisListType

P = 128
BANK = 512


class Steps:

    def __init__(self, sem):
        self.sem, self.n = sem, 0

    def mark(self, ins):
        self.n += 1
        ins.then_inc(self.sem, 1)

    def settle(self, eng):
        eng.wait_ge(self.sem, self.n)


def yoco_trunk(nc, x, gla_w_in, gla_w_gk, gla_b_gk, gla_norm_g, gla_w_out, kv_w, forget_bias, fox_w_qg,
               fox_w_out, router_w, router_bias, moe_w_gate, moe_w_up, moe_w_down, ln_g, ln_b, out):
    _, S, D = x.shape
    DEPTH, E, _, DE = moe_w_gate.shape
    RANK, HK = gla_w_gk.shape[1:]
    DV = gla_norm_g.shape[1]
    HV = gla_w_out.shape[1]
    H_A = HV // DV
    DK = HK // H_A
    H_B = forget_bias.shape[0]
    DH = fox_w_out.shape[1] // H_B
    CH = 64
    GROUPS = 4
    EPG = E // GROUPS
    T = S // P
    K = D // P
    KE = DE // P
    CPT = P // CH
    ALPHA = float((2 * DEPTH) ** 0.25)
    LN_EPS, RMS_EPS, GATE_NORM = 1e-5, 1e-6, 16.0
    BIG = float(4 * S)
    NEG = -1e37
    LOW = -3e38
    assert DEPTH == 2 and T == 4 and K == 8 and DK == P and S == BANK and DE == BANK and DH == 64

    h_rows = nc.dram_tensor("h_rows", [S, D], F32).ap()
    cum_rows = nc.dram_tensor("cum_rows", [2, 16, S], F32).ap()
    y_rows = nc.dram_tensor("y_rows", [2 * S, D], F32).ap()

    RING, PAIRED = 6, 5
    CHUNKS = 4
    GLA_PIECES = 8
    FOX_PIECES = 10
    MOE_PIECES = 3 * E
    gla0, fox0 = 0, GLA_PIECES
    BODY = 4
    before_mix = [0, GLA_PIECES + MOE_PIECES]
    before_moe = [GLA_PIECES, GLA_PIECES + MOE_PIECES + FOX_PIECES]
    seen = [0] * RING
    landed, slot_base = [], []
    for pieces_ in (GLA_PIECES, FOX_PIECES):
        for p_ in range(pieces_):
            seen[2 * p_ % PAIRED] += 1
            landed.append(seen[2 * p_ % PAIRED])
        slot_base.append(list(seen))
        seen = [n_ + MOE_PIECES // RING for n_ in seen]

    def mix_piece(n):
        L, p = (0, n) if n < fox0 else (1, n - fox0)
        return L, p, 2 * p % PAIRED, (2 * p + 1) % PAIRED

    def released_for(n, high):
        L, p, lo_slot, hi_slot = mix_piece(n)
        turn = p + high - 2
        if p + high >= 2 + (not high):
            return before_mix[L] + turn
        if L == 0:
            return 0
        return before_mix[1] - (3 if (hi_slot if high else lo_slot) < 3 else 0)

    ctx = ExitStack()
    with ctx:
        def sb(name, shape, dt=F32):
            return ctx.enter_context(nc.sbuf_tensor(name, shape, dt))

        def sem(name):
            return ctx.enter_context(nc.semaphore(name))

        ring_at = -(-nc.sbuf_base // 32) * 32
        ring = sb("ring", [P, RING, K * BANK])
        ring_r = nc.alloc_sbuf_tensor_at("ring_r", [P, RING, K * BANK], F32R, offset=ring_at)
        H = sb("resid", [P, T, D])
        hT_hi = sb("featT", [P, K, S], F32R)
        hT_lo = ring_r[:, RING - 1, :].rearrange("p (k n) -> p k n", k=K)
        arena = sb("arena", [P, 18624])
        ident = sb("ident", [P, P])
        chunk_sums = sb("chunk_sums", [P, 2 * P])
        upto = sb("upto", [P, P])
        one = sb("one", [P, 1])
        causal = sb("causal", [P, P])
        slot1 = sb("slot1", [P, P])
        rw = sb("rw", [P, K, 2, E], F32R)
        gkf = sb("gkf", [P, K, 2, RANK], F32R)
        rbias = sb("rbias", [P, E])
        fbias = sb("fbias", [P, H_B])
        iota_e = sb("iota_e", [P, E])
        row_id = sb("row_id", [P, T])
        counts = sb("counts", [1, E], I32)
        parts = sb("parts", [1, E], I32)
        scan = sb("scan", [1, 2, 8 + E])
        part3 = sb("part3", [1, E])
        carry = sb("carry", [1, 1])
        ln_mv = sb("ln_mv", [P, T, 2])
        ln_bn = sb("ln_bn", [P, T, 2, 6])
        ln_r = sb("ln_r", [P, T, 3])
        half = sb("half", [P, T * H_A])
        tokv = sb("tokv", [P, 4, 2], U32)
        tokg = sb("tokg", [P, 4])
        cold_rows = sb("cold_rows", [P, 2], U32)
        cold_gate = sb("cold_gate", [P, 1])
        cold_rank = sb("cold_rank", [P, T])
        upto_b = sb("upto_b", [P, P], BF16)
        ones_b = sb("ones_b", [P, P], BF16)
        picked_b = sb("picked_b", [P, T, E], BF16)
        ranks = sb("ranks", [P, T, E + 3])
        ps = ctx.enter_context(nc.psum_tensor("ps", [P, 8, BANK], F32))

        def at(off, *dims):
            n = 1
            for d in dims:
                n *= d
            v = arena[:, off:off + n]
            if len(dims) == 2:
                v = v.rearrange("p (a b) -> p a b", a=dims[0])
            if len(dims) == 3:
                v = v.rearrange("p (a b c) -> p a b c", a=dims[0], b=dims[1])
            return v

        ln_p = at(0, 2, D)
        q_a, k_a, gk = at(0, H_A, S), at(2048, H_A, S), at(4096, T, HK)
        mix = at(6144, T, HV)
        e_bc, k_inv, k_end = at(10240, 2, S), at(11264, 2, S), at(12288, 2, S)
        k_tok, att, states = at(13312, T, P), at(13824, T, P), at(14336, 2 * T, DV)
        gr_in, wgk = at(16384, S)[0:RANK + 1, :], at(16896, HK)[0:RANK + 1, :]
        normg = at(17536, DV)
        narrow_raw = at(10240, 3, K * E)
        ssq = at(17792, T * H_A)
        rms = at(17808, T * H_A)
        squares = at(17824, DV)
        gate_a = at(10240, 2, BANK)
        qa, ka = at(0, 2, 4, S), at(4096, 2, 4, S)
        v_b = at(8192, T, D)
        o_b = at(12288, T, D)
        prob, prob_t = at(16384, 2, S), at(17408, 2, S)
        nmax = at(18432, 64)
        rsum = at(18496, 64)
        rinv = at(18560, 64)
        f_log, f_tmp = nmax, rinv
        cumT = at(16384, 2, S)
        gate_b = at(16384, 2, BANK)
        xg, xgT = at(2048, 2, D), at(4096, 2, D)
        hid, hidT, silu = at(6144, BANK), at(6656, BANK), at(7168, BANK)
        yb = at(7680, 2, D)
        cxg, cxgT, cyb = at(10752, D), at(11776, D), at(12800, D)
        spare = hT_hi[:, :, :].rearrange("p k s -> p (k s)")
        onehot = spare[:, 0:2 * BANK].rearrange("p (a n) -> p a n", a=2)
        coneh = spare[:, 2 * BANK:3 * BANK]
        info = spare[:, 3 * BANK:3 * BANK + T * (E + 2) * 4].rearrange("p (t e c) -> p t e c", t=T, c=4)
        ysum = at(2048, 2, 2 * D)
        rt = [at(14656 + 64 * n, T, E) for n in range(12)]
        rs = [at(14656 + 64 * 12 + 16 * n, T, GROUPS) for n in range(8)]
        rv = [at(14656 + 64 * 14 + 4 * n, T) for n in range(8)]

        w_loaded = [sem(f"w_loaded{n}") for n in range(RING)]
        w_free = sem("w_free")
        w_high, w_low = sem("w_high"), sem("w_low")
        par_high, par_low = sem("par_high"), sem("par_low")
        x_loaded = [sem(f"x_loaded{n}") for n in range(T)]
        par_loaded = sem("par_loaded")
        consts = sem("consts")
        one_rows = sem("one_rows")
        tp_done, tp_act, tp_dve = sem("tp_done"), sem("tp_act"), sem("tp_dve")
        proj_done = sem("proj_done")
        ev_act, ev_dve = sem("ev_act"), sem("ev_dve")
        dve_step, act_step, pool_step = sem("dve_step"), sem("act_step"), sem("pool_step")
        gr_done, gr_ev, z_done, z_min, z_abs, z_ln, gk_ready = (
            sem(n) for n in ("gr_done", "gr_ev", "z_done", "z_min", "z_abs", "z_ln", "gk_ready"))
        bc_done, bc_exp, decayed = sem("bc_done"), sem("bc_exp"), sem("decayed")
        kt_done, kt_ev, att_done, att_ev = sem("kt_done"), sem("kt_ev"), sem("att_done"), sem("att_ev")
        kv_done, st_done, o_done, o_ev, sq_done = (
            sem(n) for n in ("kv_done", "st_done", "o_done", "o_ev", "sq_done"))
        rms_in, rms_out, normed = sem("rms_in"), sem("rms_out"), sem("normed")
        gate_done, gated = sem("gate_done"), sem("gated")
        lnp_loaded = sem("lnp_loaded")
        ln_stats, ln_rstd, ln_bias, ln_norm, ln_scaled, ln_ready = (
            sem(n) for n in ("ln_stats", "ln_rstd", "ln_bias", "ln_norm", "ln_scaled", "ln_ready"))
        h_stored = sem("h_stored")
        rt_logits, rt_in, rt_exp, rt_picked, rt_ranks, rt_ready = (
            sem(n) for n in ("rt_logits", "rt_in", "rt_exp", "rt_picked", "rt_ranks", "rt_ready"))
        pads_clear = sem("pads_clear")
        moves = sem("moves")
        hot, tbl_done, tbl_ev = sem("hot"), sem("tbl_done"), sem("tbl_ev")
        gathered = [sem("gathered0"), sem("gathered1")]
        scattered = [sem("scattered0"), sem("scattered1")]
        xt_done, xt_ev = sem("xt_done"), sem("xt_ev")
        gate_mm, up_mm, silu_done, hid_done = sem("gate_mm"), sem("up_mm"), sem("silu_done"), sem("hid_done")
        ht_done, ht_ev, y_mm, y_act, y_dve = (sem(n) for n in ("ht_done", "ht_ev", "y_mm", "y_act", "y_dve"))
        c_copy, c_rank, c_hot, c_tbl, c_idx, c_gat, c_xt, c_xe, c_gu, c_silu, c_hid, c_ht, c_he, c_y, c_ya, c_yd, c_sca = (
            sem("cold_" + n) for n in ("copy", "rank", "hot", "tbl", "idx", "gathered", "xt", "xt_ev", "gate_up", "silu",
                                       "hid", "ht", "ht_ev", "y", "y_act", "y_dve", "scattered"))
        y_loaded = [sem("y_loaded0"), sem("y_loaded1")]
        fl_done, fl_z, fl_abs, fl_ln, f_ready, cum_done, cum_ev, cum_stored = (
            sem(n) for n in ("fl_done", "fl_z", "fl_abs", "fl_ln", "f_ready", "cum_done", "cum_ev", "cum_stored"))
        cum_put = [sem("cum_put0"), sem("cum_put1")]
        sc_done, sc_masked, sc_max, p_done, pt_done, pt_ev, pv_done, pv_ev = (
            sem(n) for n in ("sc_done", "sc_masked", "sc_max", "p_done", "pt_done", "pt_ev", "pv_done", "pv_ev"))
        stored = sem("stored")

        KV_BANKS = (4, 2)

        units = []

        def plan(kind, piece, block, engine):
            units.append((kind, piece, block, engine))

        for f in range(H_A):
            plan("qa", gla0, f, "act")
        for f in range(H_A):
            plan("ka", gla0 + 1, f, "dve")
        for p in range(2):
            for t in range(T):
                plan("va", gla0 + 2 + p, (p, t), "act" if t % 2 else "dve")
        U_GLA_TAIL = len(units)
        for p in range(2):
            for t in range(T):
                plan("ga", gla0 + 4 + p, (p, t), "act")
        for t in range(T):
            for p in range(2):
                plan("oa", gla0 + 6 + p, (p, t), "dve")
        U_FOX = len(units)
        for p in range(2):
            for t in range(T):
                plan("vb", fox0 + p, (p, t), "act" if t % 2 else "dve")
        U_QUARTERS = len(units)
        for c in range(4):
            for f in range(2):
                plan("kb", fox0 + 2 + 2 * (c // 2), (c, f), "dve")
            for f in range(2):
                plan("qb", fox0 + 3 + 2 * (c // 2), (c, f), "act")
        U_FOX_TAIL = len(units)
        for p in range(2):
            for t in range(T):
                plan("gb", fox0 + 6 + p, (p, t), "act")
        for t in range(T):
            for p in range(2):
                plan("ob", fox0 + 8 + p, (p, t), "dve")
        U_END = len(units)

        def taken(u):
            e = units[u][3]
            return (ev_act if e == "act" else ev_dve), sum(1 for x_ in units[:u + 1] if x_[3] == e)

        tails = [(U_GLA_TAIL, mix, gate_a, ACT.Silu), (U_FOX_TAIL, o_b, gate_b, ACT.Sigmoid)]
        TP_X, TP_MIX, TP_RT, TP_L0 = 0, [1, 4], [2, 5], 3

        def split_chunk(n, q):
            _, _, lo_slot, hi_slot = mix_piece(n)
            c = slice(q * (K * BANK // CHUNKS), (q + 1) * (K * BANK // CHUNKS))
            return ring[:, lo_slot, c], ring_r[:, hi_slot, c], ring_r[:, lo_slot, c]

        block = ctx.enter_context(nc.Block())

        @block.sync
        def _(sp):
            for t in range(T):
                sp.dma_start(H[:, t, :], x[0, t * P:(t + 1) * P, :]).then_inc(x_loaded[t], 16)

            def load(slot, src):
                dst = ring[:, slot, :].rearrange("p (k n) -> p k n", k=src.shape[1])
                sp.dma_start(dst, src).then_inc(w_loaded[slot], 16)

            def cols(w, c):
                return w[:, c * BANK:(c + 1) * BANK].rearrange("(k p) n -> p k n", p=P)

            def straight(n0, srcs):
                for m, src in enumerate(srcs):
                    n = n0 + m
                    if n == 1:
                        sp.wait_ge(par_loaded, 16 * 8)
                    if n == fox0 + 2:
                        for done in y_loaded:
                            sp.wait_ge(done, 32)
                    if released_for(n, False):
                        sp.wait_ge(w_free, released_for(n, False))
                    load(mix_piece(n)[2], src)

            def experts(L):
                sp.wait_ge(w_free, before_moe[L])
                with sp.Fori(0, E // BODY) as i:
                    for j in range(BODY):
                        e = i * BODY + j
                        for m, w in enumerate((moe_w_gate, moe_w_up, moe_w_down)):
                            n = 3 * j + m
                            src = w[L][bass.ds(e, 1), :, :].rearrange("e (k p) f -> p (e k) f", p=P)
                            if n % RING == RING - 1:
                                sp.wait_ge(rt_logits, L + 1)
                            sp.wait_ge(w_free, i * (3 * BODY) + before_moe[L] + n - RING + 1)
                            load(n % RING, src)

            w_in, w_out, w_qg, w_o2 = gla_w_in[0], gla_w_out[0], fox_w_qg[0], fox_w_out[0]
            straight(gla0, [cols(w_in, c) for c in range(6)] + [cols(w_out, c) for c in range(2)])
            experts(0)
            straight(fox0, [cols(kv_w, 2), cols(kv_w, 3), cols(kv_w, 0), cols(w_qg, 0), cols(kv_w, 1),
                            cols(w_qg, 1), cols(w_qg, 2), cols(w_qg, 3), cols(w_o2, 0), cols(w_o2, 1)])
            experts(1)

        @block.gpsimd
        def _(pool):
            own = Steps(pool_step)
            last_row = [pool.to_reg(S - 1), pool.to_reg(2 * S - 1)]
            n_const = [0]

            def const(ins):
                n_const[0] += 1
                ins.then_inc(consts, 1)

            def settle():
                pool.wait_ge(consts, n_const[0])

            const(pool.memset(ident[:, :], 0.0))
            const(pool.memset(chunk_sums[:, :], 1.0 / GATE_NORM))
            const(pool.memset(upto[:, :], 1.0))
            const(pool.memset(one[:, :], 1.0))
            const(pool.memset(causal[:, :], 0.0))
            const(pool.memset(half[:, :], -0.5))
            const(pool.memset(att[:, :, :], 0.0))
            const(pool.iota(slot1[:, :], pattern=[[1, P]], base=1, channel_multiplier=0,
                            allow_small_or_imprecise_dtypes=True))
            const(pool.iota(iota_e[:, :], pattern=[[1, E]], base=0, channel_multiplier=0,
                            allow_small_or_imprecise_dtypes=True))
            const(pool.iota(row_id[:, :], pattern=[[P, T]], base=-int(BIG), channel_multiplier=1,
                            allow_small_or_imprecise_dtypes=True))
            settle()
            const(pool.affine_select(out=ident[:, :], in_=ident[:, :], compare_op=ALU.not_equal, fill=1.0,
                                     base=0, pattern=[[-1, P]], channel_multiplier=1))
            const(pool.affine_select(out=upto[:, :], in_=upto[:, :], compare_op=ALU.is_ge, fill=0.0,
                                     base=0, pattern=[[1, P]], channel_multiplier=-1))
            const(pool.affine_select(out=causal[:, :], in_=causal[:, :], compare_op=ALU.is_ge, fill=NEG,
                                     base=0, pattern=[[-1, P]], channel_multiplier=1))
            const(pool.affine_select(out=chunk_sums[:, 0:P], in_=chunk_sums[:, 0:P], compare_op=ALU.is_ge,
                                     fill=0.0, base=0, pattern=[[1, P]], channel_multiplier=-1))
            const(pool.affine_select(out=chunk_sums[:, P:2 * P], in_=chunk_sums[:, P:2 * P],
                                     compare_op=ALU.is_gt, fill=0.0, base=0, pattern=[[-1, P]],
                                     channel_multiplier=1))
            settle()
            const(pool.affine_select(out=chunk_sums[:, CH:P], in_=chunk_sums[:, CH:P], compare_op=ALU.is_ge,
                                     fill=0.0, base=-CH, pattern=[[0, P - CH]], channel_multiplier=1))
            const(pool.affine_select(out=chunk_sums[:, P:P + CH], in_=chunk_sums[:, P:P + CH],
                                     compare_op=ALU.is_gt, fill=0.0, base=CH, pattern=[[0, CH]],
                                     channel_multiplier=-1))

            def layer_norm(N):
                for s in range(T + 2):
                    if s < T:
                        pool.wait_ge(ln_stats, N * T + s + 1)
                        pool.tensor_tensor(ln_r[:, s, 1:2], ln_r[:, s, 0:1], half[:, 0:1],
                                           ALU.pow).then_inc(ln_rstd, 1)
                    if s >= 2:
                        t = s - 2
                        pool.wait_ge(ln_scaled, N * T + t + 1)
                        pool.wait_ge(lnp_loaded, 32 * (N + 1))
                        pool.tensor_tensor(H[:, t, :], H[:, t, :], ln_p[:, 1, :], ALU.add).then_inc(ln_ready, 1)

            def load_ln(N):
                L, which = divmod(N, 2)
                for m, w in enumerate((ln_g, ln_b)):
                    pool.dma_start(ln_p[:, m, :], w[L, which:which + 1, :].to_broadcast([P, D])
                                   ).then_inc(lnp_loaded, 16)

            def store_rows(N, dst):
                for t in range(T):
                    pool.wait_ge(ln_ready, N * T + t + 1)
                    pool.dma_start(dst[t * P:(t + 1) * P, :], H[:, t, :]).then_inc(
                        h_stored if dst is h_rows else stored, 16)

            def gather(dst, rows, done):
                pool.sem_inc(moves, 1)
                pool.indirect_dma_start(out=dst, out_offset=None, in_=h_rows,
                                        in_offset=bass.IndirectOffsetOnAxis(ap=rows, axis=0),
                                        bounds_check=last_row[0], oob_is_err=False).then_inc(done, 16)

            def scatter(src, rows, done):
                pool.sem_inc(moves, 1)
                pool.indirect_dma_start(out=y_rows, out_offset=bass.IndirectOffsetOnAxis(ap=rows, axis=0),
                                        in_=src, in_offset=None,
                                        bounds_check=last_row[1], oob_is_err=False).then_inc(done, 16)

            def experts(L):
                TB, XT, EX, SC = 18 * L, 17 * L + 1, 16 * L + 1, 8 * L + 1
                if L == 0:
                    for dst, done in ((yb[0:1, 0, 0:P], scattered[0]), (yb[0:1, 1, 0:P], scattered[1]),
                                      (cyb[0:1, 0:P], c_sca)):
                        pool.dma_start(dst, x[0, 0:1, 0:P]).then_inc(done, 16)
                for n in range(2):
                    pool.memset(xg[:, n, :], 0.0).then_inc(pads_clear, 1)
                pool.memset(cxg, 0.0).then_inc(pads_clear, 1)
                pool.wait_ge(pads_clear, 3 * (L + 1))
                pool.wait_ge(h_stored, 64 * (L + 1))
                for e in range(2):
                    pool.wait_ge(tbl_ev, 2 * (TB + e + 1))
                    gather(xg[:, e, :], tokv[:, e, 0:1], gathered[e])
                with pool.Fori(0, E // BODY) as i:
                    for j in range(BODY):
                        e = i * BODY + j
                        n = pool.value_load(counts[0:1, bass.ds(e, 1)], min_val=0, max_val=S)
                        pool.wait_ge(tbl_ev, (e + TB + 3) * 2)
                        pool.wait_ge(xt_done, (e + XT + 1) * 2)
                        gather(xg[:, j % 2, :], tokv[:, (j + 2) % 4, 0:1], gathered[j % 2])
                        pool.wait_ge(y_act, e + EX + 1)
                        pool.wait_ge(y_dve, e + EX + 1)
                        scatter(yb[:, j % 2, :], tokv[:, j % 4, 1:2], scattered[j % 2])
                        with pool.If(n > P):
                            before = pool.value_load(parts[0:1, bass.ds(e, 1)], min_val=0, max_val=6 * E + 1)
                            with pool.Fori(0, 3) as m:
                                c = before + m
                                pool.wait_ge(c_sca, c * 16)
                                pool.wait_ge(c_idx, (c + 1) * 2)
                                gather(cxg, cold_rows[:, 0:1], c_gat)
                                pool.wait_ge(c_ya, c + 1)
                                pool.wait_ge(c_yd, c + 1)
                                scatter(cyb, cold_rows[:, 1:2], c_sca)
                            pool.wait_ge(c_sca, (before + 3) * 16)
                            pool.nop()
                        with pool.Else():
                            pool.nop()
                        pool.nop()
                for n in range(2):
                    pool.wait_ge(gathered[n], 16 * 9 * (L + 1))
                    pool.wait_ge(scattered[n], 16 * (SC + 8))
                y_by_choice = y_rows.rearrange("(c t p) d -> t p c d", c=2, p=P)
                for t in range(T):
                    if t >= 2:
                        pool.wait_ge(ln_stats, (2 * L + 1) * T + t - 1)
                    pool.dma_start(ysum[:, t % 2, :].rearrange("p (c d) -> p c d", c=2),
                                   y_by_choice[t]).then_inc(y_loaded[t % 2], 16)

            pool.wait_ge(sq_done, T * H_A)
            pool.wait_ge(rms_in, 1)
            pool.tensor_tensor(rms, ssq, half[:, 0:T * H_A], ALU.pow).then_inc(rms_out, 1)
            pool.wait_ge(normed, 1)
            load_ln(0)
            layer_norm(0)
            store_rows(0, h_rows)
            load_ln(1)
            experts(0)
            layer_norm(1)
            pool.wait_ge(ln_ready, 2 * T)
            for buf in (qa, ka):
                pool.memset(buf[DH:DH + 2, :, :, :], 1.0).then_inc(one_rows, 1)
            pool.wait_ge(one_rows, 2)
            pool.wait_ge(cum_ev, 2)
            pool.dma_start(cum_rows.rearrange("a h s -> h a s"), cumT[0:H_B, :, :]).then_inc(cum_stored, 16)
            pool.wait_ge(cum_stored, 16)
            for c in range(4):
                if c >= 2:
                    pool.wait_ge(pv_done, 16 * (c - 1))
                for buf, row, src in ((qa, DH + 1, 0), (ka, DH, 1)):
                    pool.dma_start(buf[row:row + 1, c % 2, :, :], cum_rows[src:src + 1, 4 * c:4 * c + 4, :]
                                   ).then_inc(cum_put[c % 2], 16)
            pool.wait_ge(pv_ev, 64)
            load_ln(2)
            layer_norm(2)
            store_rows(2, h_rows)
            load_ln(3)
            experts(1)
            layer_norm(3)
            store_rows(3, out[0])
            pool.wait_ge(stored, 16 * T)

        @block.tensor
        def _(pe):
            def transpose_tile(turn, t, src):
                for kk in range(2):
                    if 4 * turn + t:
                        pe.wait_ge(tp_dve, 2 * (4 * turn + t) - 1 + kk)
                    for j in range(4):
                        mm = pe.transpose(ps[:, kk, j * P:(j + 1) * P],
                                          src[:, t, (4 * kk + j) * P:(4 * kk + j + 1) * P], ident[:, :])
                    mm.then_inc(tp_done, 1)

            def products(o, left, right, k):
                pe.matmul(o, left[0], right[0], start=k == 0, stop=False)
                pe.matmul(o, left[0], right[1], start=False, stop=False)
                return pe.matmul(o, left[1], right[0], start=False, stop=k == K - 1)

            def hT_block(k, cols):
                return hT_hi[:, k, cols], hT_lo[:, k, cols]

            def unit(u, frees=0):
                kind, piece, blk, _ = units[u]
                if u >= 4:
                    pe.wait_ge(*taken(u - 4))
                o = ps[:, 2 + u % 4, :]
                _, _, lo_slot, hi_slot = mix_piece(piece)
                w_hi, w_lo = (ring_r[:, slot, :].rearrange("p (k n) -> p k n", k=K)
                              for slot in (hi_slot, lo_slot))
                first = u == 0 or all(x_[1] != piece for x_ in units[:u])
                for k in range(K):
                    if first and k % (K // CHUNKS) == 0:
                        pe.wait_ge(w_low, CHUNKS * piece + k // (K // CHUNKS) + 1)
                    if kind in ("qa", "ka", "qb", "kb"):
                        f = blk if kind in ("qa", "ka") else 2 * (blk[0] % 2) + blk[1]
                        f = slice(f * P, (f + 1) * P)
                        mm = products(o, (w_hi[:, k, f], w_lo[:, k, f]), hT_block(k, slice(0, S)), k)
                    else:
                        t = blk[1]
                        mm = products(o, hT_block(k, slice(t * P, (t + 1) * P)), (w_hi[:, k, :], w_lo[:, k, :]), k)
                mm.then_inc(proj_done, 1)
                if frees:
                    marker(frees)

            def marker(frees):
                pe.matmul(ps[:, 7, BANK - 2:BANK], ident[:, :], ident[:, 0:2], start=True, stop=True
                          ).then_inc(w_free, frees)

            def narrow(t, w):
                n = 2 * w.shape[3]
                for k in range(K):
                    for m, part in enumerate(hT_block(k, slice(t * P, (t + 1) * P))):
                        mm = pe.matmul(ps[:, 6, t * n:(t + 1) * n], part,
                                       w[:, k, :, :].rearrange("p a n -> p (a n)"),
                                       start=k == 0 and m == 0, stop=k == K - 1 and m == 1)
                return mm

            def tail(L):
                u0, src, _, _ = tails[L]
                for s in range(T):
                    unit(u0 + s, frees=1 if s == T - 1 else 0)
                for s in range(T + 1):
                    if s < T:
                        unit(u0 + T + s, frees=1 if s == T - 1 else 0)
                    if s >= 1:
                        pe.wait_ge(gated, 8 * L + T + s)
                        transpose_tile(TP_MIX[L], s - 1, src)
                for t in range(T):
                    pe.wait_ge(tp_dve, 2 * (4 * TP_MIX[L] + t + 1))
                    unit(u0 + 8 + 2 * t)
                    unit(u0 + 9 + 2 * t, frees=2 if t == T - 1 else 0)
                for s in range(T + 1):
                    if s < T:
                        pe.wait_ge(ln_ready, 2 * L * T + s + 1)
                        transpose_tile(TP_RT[L], s, H)
                    if s >= 1:
                        t = s - 1
                        pe.wait_ge(tp_dve, 2 * (4 * TP_RT[L] + t + 1))
                        mm = narrow(t, rw)
                mm.then_inc(rt_logits, 1)

            def router(L):
                pe.wait_ge(rt_picked, L + 1)
                for t in range(T):
                    for s in range(t + 1):
                        pe.matmul(ps[:, 6, t * E:(t + 1) * E], (upto_b if s == t else ones_b)[:, :], picked_b[:, s, :],
                                  start=s == 0, stop=s == t)
                for s in range(T):
                    mm = pe.matmul(ps[:, 6, T * E:(T + 1) * E], ones_b[:, :], picked_b[:, s, :],
                                   start=s == 0, stop=s == T - 1)
                mm.then_inc(rt_ranks, 1)

            def experts(L):
                TB, HB, XT, EX = 18 * L, 19 * L, 17 * L + 1, 16 * L + 1
                if L == 0:
                    for s, n in ((xt_done, 2), (gate_mm, 1), (up_mm, 1), (ht_done, 1), (y_mm, 1), (c_tbl, 1),
                                 (c_xt, 2), (c_gu, 1), (c_ht, 1), (c_y, 1)):
                        pe.sem_inc(s, n)

                def table(e, hots):
                    for s in range(T):
                        mm = pe.matmul(ps[:, 7, 0:4], hots[:, s * P:(s + 1) * P],
                                       info[:, s, bass.ds(e, 1), :].rearrange("p e c -> p (e c)")
                                       if not isinstance(e, int) else info[:, s, e, :],
                                       start=s == 0, stop=s == T - 1)
                    return mm

                def turn_rows(src, done, halves=range(2)):
                    for kk in halves:
                        for j in range(4):
                            mm = pe.transpose(ps[:, kk, j * P:(j + 1) * P],
                                              src[:, (4 * kk + j) * P:(4 * kk + j + 1) * P], ident[:, :])
                        mm.then_inc(done, 1)

                def w_of(n, k):
                    return ring[:, n % RING, :].rearrange("p (k n) -> p k n", k=k)

                def gate_up(xT, n, bank):
                    for k in range(K):
                        mm = pe.matmul(ps[:, bank, :], xT[:, k * P:(k + 1) * P], w_of(n, K)[:, k, :],
                                       start=k == 0, stop=k == K - 1)
                    return mm

                def down(n):
                    w = w_of(n, KE)
                    for b in range(2):
                        for k in range(KE):
                            mm = pe.matmul(ps[:, 4 + b, :], hidT[:, k * P:(k + 1) * P],
                                           w[:, k, b * BANK:(b + 1) * BANK], start=k == 0, stop=k == KE - 1)
                    return mm

                def turn_hidden():
                    for k in range(KE):
                        mm = pe.transpose(ps[:, 6, k * P:(k + 1) * P], hid[:, k * P:(k + 1) * P], ident[:, :])
                    return mm

                pe.wait_ge(rt_ready, L + 1)
                for e in range(2):
                    pe.wait_ge(hot, HB + e + 1)
                    if e:
                        pe.wait_ge(tbl_ev, 2 * (TB + e))
                    table(e, onehot[:, e, :]).then_inc(tbl_done, 1)
                pe.wait_ge(gathered[0], 16 * (9 * L + 1))
                turn_rows(xg[:, 0, :], xt_done)
                pe.wait_ge(tbl_ev, 2 * (TB + 2))
                with pe.Fori(0, E // BODY) as i:
                    for j in range(BODY):
                        e = i * BODY + j
                        n0 = 3 * j

                        def piece(n):
                            pe.wait_ge(w_loaded[n % RING], i * (16 * 3 * BODY // RING)
                                       + 16 * (slot_base[L][n % RING] + n // RING + 1))

                        xT = xgT[:, j % 2, :]
                        pe.wait_ge(hot, e + HB + 3)
                        table(e + 2, onehot[:, j % 2, :]).then_inc(tbl_done, 1)
                        piece(n0)
                        pe.wait_ge(xt_ev, (e + XT + 1) * 2)
                        gate_up(xT, n0, 2).then_inc(gate_mm, 1)
                        piece(n0 + 1)
                        gate_up(xT, n0 + 1, 3).then_inc(up_mm, 1)
                        n_rows = pe.value_load(counts[0:1, bass.ds(e, 1)], min_val=0, max_val=S)
                        b = (j + 1) % 2
                        pe.wait_ge(gathered[b], (i * 2 + 9 * L + (j + 1) // 2 + 1) * 16)
                        turn_rows(xg[:, b, :], xt_done, range(1))
                        pe.wait_ge(hid_done, e + EX + 1)
                        turn_hidden().then_inc(ht_done, 1)
                        turn_rows(xg[:, b, :], xt_done, range(1, 2))
                        piece(n0 + 2)
                        pe.wait_ge(ht_ev, e + EX + 1)
                        pe.wait_ge(y_act, e + EX)
                        pe.wait_ge(y_dve, e + EX)
                        down(n0 + 2).then_inc(y_mm, 1)
                        with pe.If(n_rows > P):
                            before = pe.value_load(parts[0:1, bass.ds(e, 1)], min_val=0, max_val=6 * E + 1)
                            with pe.Fori(0, 3) as m:
                                c = before + m
                                pe.wait_ge(tbl_ev, (e + TB + 3) * 2)
                                pe.wait_ge(xt_ev, (e + XT + 2) * 2)
                                pe.wait_ge(y_act, e + EX + 1)
                                pe.wait_ge(y_dve, e + EX + 1)
                                pe.wait_ge(c_ya, c)
                                pe.wait_ge(c_yd, c)
                                pe.wait_ge(c_hot, c + 1)
                                table(e, coneh).then_inc(c_tbl, 1)
                                pe.wait_ge(c_gat, c * 16)
                                turn_rows(cxg, c_xt)
                                pe.wait_ge(c_xe, (c + 1) * 2)
                                gate_up(cxgT, n0, 2)
                                gate_up(cxgT, n0 + 1, 3).then_inc(c_gu, 1)
                                pe.wait_ge(c_hid, c + 1)
                                turn_hidden().then_inc(c_ht, 1)
                                pe.wait_ge(c_he, c + 1)
                                down(n0 + 2).then_inc(c_y, 1)
                            pe.wait_ge(c_ya, before + 3)
                            pe.wait_ge(c_yd, before + 3)
                            pe.matmul(ps[:, 7, 0:2], ident[:, :], ident[:, 0:2], start=True, stop=True)
                        with pe.Else():
                            pe.nop()
                        pe.wait_ge(tbl_ev, (e + TB + 3) * 2)
                        marker(3)

            pe.wait_ge(consts, 17)
            for t in range(T):
                pe.wait_ge(x_loaded[t], 16)
                transpose_tile(TP_X, t, H)
            pe.wait_ge(par_loaded, 16 * 8)
            pe.wait_ge(par_low, 1)
            pe.wait_ge(tp_dve, 2 * T)
            for k in range(K):
                mm = products(ps[0:RANK, 6, :], (gkf[:, k, 0, :], gkf[:, k, 1, :]), hT_block(k, slice(0, S)), k)
            mm.then_inc(gr_done, 1)
            for f in range(H_A):
                unit(f, frees=1 if f == H_A - 1 else 0)
            pe.wait_ge(gr_ev, 2)
            for t in range(T):
                if t >= 1:
                    pe.wait_ge(z_abs, t)
                pe.matmul(ps[:, 6, :], gr_in[:, t * P:(t + 1) * P], wgk, start=True, stop=True).then_inc(z_done, 1)
            for u in range(H_A, 2 * H_A):
                unit(u, frees=1 if u == 2 * H_A - 1 else 0)
            for u in range(2 * H_A, U_GLA_TAIL):
                unit(u, frees=1 if u % T == T - 1 else 0)

            def decay_sums(h):
                pe.wait_ge(gk_ready, T) if h == 0 else pe.wait_ge(bc_exp, 6 * h)
                for t in range(T):
                    mm = pe.matmul(ps[:, t // 2, (t % 2) * 2 * P:(t % 2 + 1) * 2 * P],
                                   gk[:, t, h * DK:(h + 1) * DK], chunk_sums[:, :], start=True, stop=True)
                    if t % 2:
                        mm.then_inc(bc_done, 1)

            for s in (ev_act, ev_dve):
                pe.wait_ge(s, sum(1 for x_ in units[:U_GLA_TAIL] if x_[3] == ("act" if s is ev_act else "dve")))
            decay_sums(0)
            for h in range(H_A):
                b = h % 2
                pe.wait_ge(decayed, 3 * (h + 1))
                if h:
                    pe.wait_ge(kt_ev, h)
                for t in range(T):
                    mm = pe.transpose(ps[:, 2, t * P:(t + 1) * P], k_end[:, b, t * P:(t + 1) * P], ident[:, :])
                mm.then_inc(kt_done, 1)
                if h:
                    pe.wait_ge(att_ev, h)
                for t in range(T):
                    mm = pe.matmul(ps[:, 3, t * P:(t + 1) * P], k_inv[:, b, t * P:(t + 1) * P],
                                   q_a[:, h, t * P:(t + 1) * P], start=True, stop=True)
                mm.then_inc(att_done, 1)
                if h + 1 < H_A:
                    decay_sums(h + 1)
                pe.wait_ge(kt_ev, h + 1)
                for t in range(T):
                    if t == 1:
                        pe.wait_ge(att_ev, h + 1)
                    elif 2 * h + t >= 2:
                        pe.wait_ge(st_done, 7 * h + 2 * t - 2 if t else 7 * h - 1)
                    for c in range(CPT if t < T - 1 else 1):
                        mm = pe.matmul(ps[:, KV_BANKS[t % 2] + c, 0:DV],
                                       k_tok[c * CH:(c + 1) * CH, t, :],
                                       mix[c * CH:(c + 1) * CH, t, h * DV:(h + 1) * DV], start=True, stop=True)
                    mm.then_inc(kv_done, 1)
                pe.wait_ge(att_ev, h + 1)
                for t in range(T):
                    if 4 * h + t >= 2:
                        pe.wait_ge(o_ev, 4 * h + t - 1)
                    pe.wait_ge(st_done, 7 * h + 2 * t + 1)
                    bank = ps[:, 6 + t % 2, 0:DV]
                    mm = pe.matmul(bank, att[:, t, :], mix[:, t, h * DV:(h + 1) * DV], start=True, stop=False,
                                   skip_group_check=True)
                    for c in range(CPT):
                        n = CPT * t + c
                        if n:
                            mm = pe.matmul(ps[c * CH:(c + 1) * CH, 6 + t % 2, 0:DV],
                                           q_a[:, h, n * CH:(n + 1) * CH], states[:, n, :],
                                           start=False, stop=True, skip_group_check=True)
                    mm.then_inc(o_done, 1)
            pe.wait_ge(o_ev, 4 * H_A)
            tail(0)
            router(0)
            experts(0)
            for t in range(T):
                pe.wait_ge(ln_ready, T + t + 1)
                transpose_tile(TP_L0, t, H)
            pe.wait_ge(tp_dve, 2 * 4 * (TP_L0 + 1))
            for t in range(T):
                mm = narrow(t, gkf)
            mm.then_inc(fl_done, 1)
            for u in range(U_FOX, U_QUARTERS):
                unit(u, frees=1 if (u - U_FOX) % T == T - 1 else 0)
            pe.wait_ge(f_ready, 1)
            for t in range(T):
                for s in range(t + 1):
                    mm = pe.matmul(ps[0:H_B, 7, t * P:(t + 1) * P], f_log[:, s * H_B:(s + 1) * H_B],
                                   upto[:, :] if s == t else one[:, :].to_broadcast([P, P]),
                                   start=s == 0, stop=s == t)
            mm.then_inc(cum_done, 1)
            pe.wait_ge(cum_ev, 2)
            for c in range(4):
                for m in range(4):
                    last = c % 2 == 1 and m in (1, 3)
                    unit(U_QUARTERS + 4 * c + m, frees=1 if last else 0)
                b = c % 2
                pe.wait_ge(cum_put[c % 2], 32 * (c // 2 + 1))
                pe.wait_ge(*taken(U_QUARTERS + 4 * c + 1))
                pe.wait_ge(*taken(U_QUARTERS + 4 * c + 3))

                def scores(r):
                    g, (s, i) = 16 * c + r, divmod(r, T)
                    if g >= 2:
                        pe.wait_ge(p_done, g - 1)
                    pe.matmul(ps[:, g % 2, 0:(i + 1) * P], qa[0:DH + 2, b, s, i * P:(i + 1) * P],
                              ka[0:DH + 2, b, s, 0:(i + 1) * P], start=True, stop=True).then_inc(sc_done, 1)

                def turn(r):
                    g, i = 16 * c + r, r % T
                    pe.wait_ge(p_done, g + 1)
                    if g >= 2:
                        pe.wait_ge(pt_ev, g - 1)
                    for n in range(i + 1):
                        mm = pe.transpose(ps[:, 2 + g % 2, n * P:(n + 1) * P], prob[:, g % 2, n * P:(n + 1) * P],
                                          ident[:, :])
                    mm.then_inc(pt_done, 1)

                def values(r):
                    g, (s, i) = 16 * c + r, divmod(r, T)
                    hd = 4 * c + s
                    pe.wait_ge(pt_ev, g + 1)
                    if g >= 2:
                        pe.wait_ge(pv_ev, g - 1)
                    for n in range(i + 1):
                        mm = pe.matmul(ps[:, 4 + g % 2, 0:DH], prob_t[:, g % 2, n * P:(n + 1) * P],
                                       v_b[:, n, hd * DH:(hd + 1) * DH], start=n == 0, stop=n == i)
                    mm.then_inc(pv_done, 1)

                for r in range(16 + 2):
                    if r < 16:
                        scores(r)
                    if 1 <= r <= 16:
                        turn(r - 1)
                    if r >= 2:
                        values(r - 2)
                pe.wait_ge(pv_ev, 16 * (c + 1))
            tail(1)
            router(1)
            experts(1)

        @block.scalar
        def _(act):
            own = Steps(act_step)
            w_in = gla_w_in[0]
            raw = [narrow_raw[:, m, :].rearrange("p (k n) -> p k n", k=K) for m in range(3)]
            act.dma_start(raw[0], w_in[:, 2 * HK + 2 * HV:].rearrange("(k p) n -> p k n", p=P)).then_inc(par_loaded, 16)
            act.dma_start(wgk[0:RANK, :], gla_w_gk[0]).then_inc(par_loaded, 16)
            act.dma_start(wgk[RANK:RANK + 1, :], gla_b_gk).then_inc(par_loaded, 16)
            act.dma_start(normg, gla_norm_g.to_broadcast([P, DV])).then_inc(par_loaded, 16)
            act.dma_start(raw[1], router_w.rearrange("(k p) n -> p k n", p=P)).then_inc(par_loaded, 16)
            act.dma_start(rbias[:, :], router_bias.rearrange("(a e) -> a e", a=1).to_broadcast([P, E])
                          ).then_inc(par_loaded, 16)
            act.dma_start(fbias[:, :], forget_bias.rearrange("(a e) -> a e", a=1).to_broadcast([P, H_B])
                          ).then_inc(par_loaded, 16)
            act.dma_start(raw[2], kv_w[:, 2 * D:].rearrange("(k p) n -> p k n", p=P)).then_inc(par_loaded, 16)

            def split_narrow(m):
                act.wait_ge(par_loaded, 16 * 8)
                if m == 2:
                    act.wait_ge(gr_done, 1)
                act.copy((gkf, rw, gkf)[m][:, :, 0, :], raw[m]).then_inc(par_high, 1)

            def split(n, chunks=range(CHUNKS)):
                L, p, lo_slot, _ = mix_piece(n)
                for q in chunks:
                    if q == 0:
                        act.wait_ge(w_loaded[lo_slot], 16 * landed[n])
                        if released_for(n, True):
                            act.wait_ge(w_free, released_for(n, True))
                    w, high, _ = split_chunk(n, q)
                    act.copy(high, w).then_inc(w_high, 1)

            def take_tile(turn, t):
                for kk in range(2):
                    act.wait_ge(tp_done, 8 * turn + 2 * t + kk + 1)
                    act.copy(hT_hi[:, 4 * kk:4 * kk + 4, t * P:(t + 1) * P],
                             ps[:, kk, :].rearrange("p (k n) -> p k n", k=4)).then_inc(tp_act, 1)

            def take(u):
                kind, _, blk, engine = units[u]
                if engine != "act":
                    return
                act.wait_ge(proj_done, u + 1)
                src = ps[:, 2 + u % 4, :]
                if kind == "qa":
                    ins = act.copy(q_a[:, blk, :], src)
                elif kind == "va":
                    ins = act.copy(mix[:, blk[1], blk[0] * BANK:(blk[0] + 1) * BANK], src)
                elif kind == "vb":
                    ins = act.copy(v_b[:, blk[1], blk[0] * BANK:(blk[0] + 1) * BANK], src)
                elif kind == "qb":
                    c, f = blk
                    if f == 0 and c >= 2:
                        act.wait_ge(pv_done, 16 * (c - 1))
                    own.mark(act.mul(qa[0:DH, c % 2, 2 * f, :], ps[0:DH, 2 + u % 4, :], float(DH) ** -0.5))
                    ins = act.mul(qa[0:DH, c % 2, 2 * f + 1, :], ps[DH:P, 2 + u % 4, :], float(DH) ** -0.5)
                ins.then_inc(ev_act, 1)

            def tail(L):
                u0, _, gate, func = tails[L]
                out_piece = units[u0 + 8][1]

                def gate_unit(m):
                    u = u0 + m
                    act.wait_ge(proj_done, u + 1)
                    if m >= 2:
                        act.wait_ge(gated, 8 * L + m - 1)
                    act.activation(gate[:, m % 2, :], ps[:, 2 + u % 4, :], func).then_inc(ev_act, 1)

                for m in range(T):
                    gate_unit(m)
                split(out_piece)
                for s in range(T + 1):
                    if s < T:
                        gate_unit(T + s)
                    if s >= 1:
                        take_tile(TP_MIX[L], s - 1)
                split(out_piece + 1)
                layer_norm(2 * L)
                for t in range(T):
                    take_tile(TP_RT[L], t)

            def layer_norm(N):
                for t in range(T):
                    act.wait_ge(ln_bias, N * T + t + 1)
                    act.activation(H[:, t, :], H[:, t, :], ACT.Identity, bias=ln_r[:, t, 2:3],
                                   scale=ln_r[:, t, 1:2]).then_inc(ln_norm, 1)

            def router(L):
                act.wait_ge(rt_in, L + 1)
                act.activation(rt[1], rt[0], ACT.Exp).then_inc(rt_exp, 1)

            def experts(L):
                XT, EX = 17 * L + 1, 16 * L + 1
                if L == 0:
                    for s, n in ((xt_ev, 2), (silu_done, 1), (y_act, 1), (c_xe, 2), (c_silu, 1), (c_ya, 1)):
                        act.sem_inc(s, n)

                def take_rows(dst, at_done, base):
                    for kk in range(2):
                        act.wait_ge(at_done, base + kk + 1)
                        yield act.copy(dst[:, kk * BANK:(kk + 1) * BANK], ps[:, kk, :])

                for ins in take_rows(xgT[:, 0, :], xt_done, 2 * XT):
                    ins.then_inc(xt_ev, 1)
                with act.Fori(0, E // BODY) as i:
                    for j in range(BODY):
                        e = i * BODY + j
                        n_rows = act.value_load(counts[0:1, bass.ds(e, 1)], min_val=0, max_val=S)
                        act.wait_ge(gate_mm, e + EX + 1)
                        act.wait_ge(hid_done, e + EX)
                        act.activation(silu, ps[:, 2, :], ACT.Silu).then_inc(silu_done, 1)
                        for ins in take_rows(xgT[:, (j + 1) % 2, :], xt_done, (e + XT + 1) * 2):
                            ins.then_inc(xt_ev, 1)
                        act.wait_ge(y_mm, e + EX + 1)
                        act.wait_ge(scattered[j % 2], (i * 2 + 8 * L + 1 + j // 2) * 16)
                        act.copy(yb[:, j % 2, 0:BANK], ps[:, 4, :]).then_inc(y_act, 1)
                        with act.If(n_rows > P):
                            before = act.value_load(parts[0:1, bass.ds(e, 1)], min_val=0, max_val=6 * E + 1)
                            with act.Fori(0, 3) as m:
                                c = before + m
                                for ins in take_rows(cxgT, c_xt, c * 2):
                                    ins.then_inc(c_xe, 1)
                                act.wait_ge(c_gu, c + 1)
                                act.wait_ge(hid_done, e + EX + 1)
                                act.wait_ge(c_hid, c)
                                act.activation(silu, ps[:, 2, :], ACT.Silu).then_inc(c_silu, 1)
                                act.wait_ge(c_y, c + 1)
                                act.wait_ge(c_sca, c * 16)
                                act.copy(cyb[:, 0:BANK], ps[:, 4, :]).then_inc(c_ya, 1)
                        with act.Else():
                            act.nop()
                        act.nop()

            for t in range(T):
                take_tile(TP_X, t)
            split_narrow(0)
            split_narrow(1)
            split(gla0)
            split(gla0 + 1)
            for u in range(H_A):
                take(u)
            split_narrow(2)
            split(gla0 + 2)
            z_t = states.rearrange("p a b -> p (a b)").rearrange("p (t n) -> p t n", t=T)
            for t in range(T):
                act.wait_ge(z_min, t + 1)
                act.activation(z_t[:, t, :], ps[:, 6, :], ACT.Abs).then_inc(z_abs, 1)
            for t in range(T):
                act.wait_ge(z_abs, t + 1)
                own.mark(act.activation(z_t[:, t, :], z_t[:, t, :], ACT.Exp, scale=-1.0))
            for t in range(T):
                own.settle(act)
                act.activation(z_t[:, t, :], z_t[:, t, :], ACT.Ln, bias=1.0).then_inc(z_ln, 1)
            split(gla0 + 3)
            for u in range(2 * H_A, 2 * H_A + T):
                take(u)
            split(gla0 + 4)
            for u in range(2 * H_A + T, U_GLA_TAIL):
                take(u)

            def exps(h):
                b = h % 2
                for m in range(2):
                    act.wait_ge(bc_done, 2 * h + m + 1)
                    if h >= 2 and m == 0:
                        act.wait_ge(o_ev, 4 * (h - 1))
                    src = ps[:, m, :].rearrange("p (t c n) -> p t c n", t=2, c=2)
                    cols = slice(m * 2 * P, (m + 1) * 2 * P)
                    for dst, part, sign in ((e_bc, 0, 1.0), (k_inv, 0, -1.0), (k_end, 1, 1.0)):
                        act.activation(dst[:, b, cols].rearrange("p (t n) -> p t n", t=2), src[:, :, part, :],
                                       ACT.Exp, scale=sign).then_inc(bc_exp, 1)

            exps(0)
            for h in range(H_A):
                if h + 1 < H_A:
                    exps(h + 1)
                split(gla0 + 5, range(h, h + 1))
                for t in range(T):
                    act.wait_ge(o_ev, 4 * h + t + 1)
                    if 4 * h + t:
                        act.wait_ge(sq_done, 4 * h + t)
                    act.activation(squares, mix[:, t, h * DV:(h + 1) * DV], ACT.Square,
                                   accum_out=ssq[:, t * H_A + h:t * H_A + h + 1]).then_inc(sq_done, 1)
            tail(0)
            router(0)
            experts(0)
            split(fox0)
            split(fox0 + 1)
            layer_norm(1)
            for t in range(T):
                take_tile(TP_L0, t)
            act.wait_ge(fl_z, 1)
            own.mark(act.activation(f_tmp, f_tmp, ACT.Abs))
            own.settle(act)
            own.mark(act.activation(f_tmp, f_tmp, ACT.Exp, scale=-1.0))
            own.settle(act)
            act.activation(f_tmp, f_tmp, ACT.Ln, bias=1.0).then_inc(fl_ln, 1)
            for p in range(2):
                for t in range(T):
                    take(U_FOX + T * p + t)
                split(fox0 + 2 + p)
            for c in range(4):
                for m in range(4):
                    take(U_QUARTERS + 4 * c + m)
                for r in range(16):
                    if c % 2 and r % 2 == 0:
                        q = r // 2
                        split(fox0 + 4 + c - 1 + q // CHUNKS, range(q % CHUNKS, q % CHUNKS + 1))
                    g, i = 16 * c + r, r % T
                    act.wait_ge(sc_max, g + 1)
                    if g >= 2:
                        act.wait_ge(pt_done, g - 1)
                    if g == 0:
                        act.wait_ge(cum_stored, 16)
                    act.activation(prob[:, g % 2, 0:(i + 1) * P], ps[:, g % 2, 0:(i + 1) * P], ACT.Exp,
                                   bias=nmax[:, g:g + 1], accum_out=rsum[:, g:g + 1]).then_inc(p_done, 1)
            tail(1)
            router(1)
            experts(1)
            layer_norm(3)

        @block.vector
        def _(dve):
            own = Steps(dve_step)

            def do(ins):
                own.mark(ins)
                own.settle(dve)

            def split_narrow(m):
                w = (gkf, rw, gkf)[m]
                dve.wait_ge(par_high, m + 1)
                dve.tensor_tensor(w[:, :, 1, :], narrow_raw[:, m, :].rearrange("p (k n) -> p k n", k=K),
                                  w[:, :, 0, :].bitcast(F32), ALU.subtract).then_inc(par_low, 1)

            def split(n, chunks=range(CHUNKS)):
                for q in chunks:
                    dve.wait_ge(w_high, CHUNKS * n + q + 1)
                    w, high, low = split_chunk(n, q)
                    dve.tensor_tensor(low, w, high.bitcast(F32), ALU.subtract).then_inc(w_low, 1)

            def take_tile(turn, t):
                for kk in range(2):
                    dve.wait_ge(tp_act, 2 * (4 * turn + t) + kk + 1)
                    block = slice(4 * kk, 4 * kk + 4), slice(t * P, (t + 1) * P)
                    dve.tensor_tensor(hT_lo[:, block[0], block[1]], ps[:, kk, :].rearrange("p (k n) -> p k n", k=4),
                                      hT_hi[:, block[0], block[1]].bitcast(F32), ALU.subtract).then_inc(tp_dve, 1)

            def take(u):
                kind, _, blk, engine = units[u]
                if engine != "dve":
                    return
                dve.wait_ge(proj_done, u + 1)
                src = ps[:, 2 + u % 4, :]
                if kind == "ka":
                    ins = dve.tensor_copy(k_a[:, blk, :], src)
                elif kind == "va":
                    ins = dve.tensor_copy(mix[:, blk[1], blk[0] * BANK:(blk[0] + 1) * BANK], src)
                elif kind == "vb":
                    ins = dve.tensor_copy(v_b[:, blk[1], blk[0] * BANK:(blk[0] + 1) * BANK], src)
                elif kind == "kb":
                    c, f = blk
                    if f == 0 and c >= 2:
                        dve.wait_ge(pv_done, 16 * (c - 1))
                    own.mark(dve.tensor_copy(ka[0:DH, c % 2, 2 * f, :], ps[0:DH, 2 + u % 4, :]))
                    ins = dve.tensor_copy(ka[0:DH, c % 2, 2 * f + 1, :], ps[DH:P, 2 + u % 4, :])
                ins.then_inc(ev_dve, 1)

            def layer_norm(N, add):
                for s in range(T + 2):
                    if s < T:
                        add(s)
                        for p in range(2):
                            own.mark(dve.bn_stats(ln_bn[:, s, p, :], H[:, s, p * BANK:(p + 1) * BANK]))
                        own.settle(dve)
                        do(dve.bn_aggr(ln_mv[:, s, :], ln_bn[:, s, :, :].rearrange("p a b -> p (a b)")))
                        dve.tensor_scalar(ln_r[:, s, 0:1], ln_mv[:, s, 1:2], LN_EPS, None,
                                          ALU.add).then_inc(ln_stats, 1)
                    if 1 <= s <= T:
                        t = s - 1
                        dve.wait_ge(ln_rstd, N * T + t + 1)
                        dve.scalar_tensor_tensor(out=ln_r[:, t, 2:3], in0=ln_mv[:, t, 0:1], scalar=-1.0,
                                                 in1=ln_r[:, t, 1:2], op0=ALU.mult,
                                                 op1=ALU.mult).then_inc(ln_bias, 1)
                    if s >= 2:
                        t = s - 2
                        dve.wait_ge(ln_norm, N * T + t + 1)
                        dve.wait_ge(lnp_loaded, 32 * (N + 1))
                        dve.tensor_tensor(H[:, t, :], H[:, t, :], ln_p[:, 0, :], ALU.mult).then_inc(ln_scaled, 1)

            def tail(L):
                u0, src, gate, _ = tails[L]
                out_piece = units[u0 + 8][1]

                def gate_heads(m):
                    p, t = units[u0 + m][2]
                    dve.wait_ge(*taken(u0 + m))
                    v = src[:, t, p * BANK:(p + 1) * BANK]
                    dve.tensor_tensor(v, v, gate[:, m % 2, :], ALU.mult).then_inc(gated, 1)

                for m in range(T):
                    gate_heads(m)
                split(out_piece)
                for s in range(T + 1):
                    if s < T:
                        gate_heads(T + s)
                    if s >= 1:
                        take_tile(TP_MIX[L], s - 1)
                split(out_piece + 1)

                def add(t):
                    for p in range(2):
                        u = u0 + 8 + 2 * t + p
                        dve.wait_ge(proj_done, u + 1)
                        hp = H[:, t, p * BANK:(p + 1) * BANK]
                        dve.scalar_tensor_tensor(out=hp, in0=hp, scalar=ALPHA, in1=ps[:, 2 + u % 4, :],
                                                 op0=ALU.mult, op1=ALU.add).then_inc(ev_dve, 1)
                    dve.wait_ge(*taken(u0 + 8 + 2 * t + 1))

                layer_norm(2 * L, add)
                for t in range(T):
                    take_tile(TP_RT[L], t)

            def router(L):
                def over_e(v):
                    return v.unsqueeze(2).to_broadcast([P, T, E])

                def each_t(v, n):
                    return v.unsqueeze(1).to_broadcast([P, T, n])

                halves = ps[:, 6, 0:2 * T * E].rearrange("p (t a e) -> p t a e", t=T, a=2)
                logits = rt[11]
                dve.wait_ge(rt_logits, L + 1)
                do(dve.tensor_copy(logits, halves[:, :, 1, :]))
                do(dve.tensor_tensor(logits, halves[:, :, 0, :], logits, ALU.add))
                do(dve.tensor_reduce(rv[0], logits, AX.X, ALU.max))
                dve.tensor_tensor(rt[0], logits, over_e(rv[0]), ALU.subtract).then_inc(rt_in, 1)
                dve.wait_ge(rt_exp, L + 1)
                do(dve.tensor_reduce(rv[1], rt[1], AX.X, ALU.add))
                do(dve.reciprocal(rv[2], rv[1]))
                scores, sel = rt[2], rt[3]
                do(dve.tensor_tensor(scores, rt[1], over_e(rv[2]), ALU.mult))
                do(dve.tensor_tensor(sel, scores, each_t(rbias[:, :], E), ALU.add))
                pair = sel.rearrange("p t (g a b) -> p (t g) a b", g=GROUPS, a=2)
                big = rt[4].rearrange("p t e -> p (t e)")[:, 0:2 * T * GROUPS].rearrange("p (n a) -> p n a", a=2)
                small = rt[5].rearrange("p t e -> p (t e)")[:, 0:2 * T * GROUPS].rearrange("p (n a) -> p n a", a=2)
                own.mark(dve.tensor_tensor(big, pair[:, :, :, 0], pair[:, :, :, 1], ALU.max))
                do(dve.tensor_tensor(small, pair[:, :, :, 0], pair[:, :, :, 1], ALU.min))
                flat = [v.rearrange("p t g -> p (t g)") for v in rs]
                own.mark(dve.tensor_tensor(flat[0], big[:, :, 0], big[:, :, 1], ALU.max))
                own.mark(dve.tensor_tensor(flat[1], big[:, :, 0], big[:, :, 1], ALU.min))
                do(dve.tensor_tensor(flat[2], small[:, :, 0], small[:, :, 1], ALU.max))
                do(dve.tensor_tensor(flat[1], flat[1], flat[2], ALU.max))
                do(dve.tensor_tensor(rs[3], rs[0], rs[1], ALU.add))

                def first_largest(v, iota, n, hit, key, most, low):
                    def wide(a):
                        return a.unsqueeze(2).to_broadcast([P, T, n])
                    do(dve.tensor_reduce(most, v, AX.X, ALU.max))
                    do(dve.tensor_tensor(hit, v, wide(most), ALU.is_equal))
                    do(dve.tensor_scalar(hit, hit, -float(n), None, ALU.mult))
                    do(dve.tensor_tensor(key, hit, each_t(iota, n), ALU.add))
                    do(dve.tensor_reduce(low, key, AX.X, ALU.min))
                    do(dve.tensor_tensor(hit, key, wide(low), ALU.is_equal))

                first_largest(rs[3], iota_e[:, 0:GROUPS], GROUPS, rs[4], rs[5], rv[3], rv[4])
                in_group = rs[4].unsqueeze(3).to_broadcast([P, T, GROUPS, EPG])
                four = [v.rearrange("p t (g e) -> p t g e", g=GROUPS) for v in rt]
                do(dve.tensor_scalar(rs[5], rs[4], -LOW, LOW, ALU.mult, ALU.add))
                outside = rs[5].unsqueeze(3).to_broadcast([P, T, GROUPS, EPG])
                do(dve.tensor_tensor(four[4], four[3], in_group, ALU.mult))
                do(dve.tensor_tensor(four[4], four[4], outside, ALU.add))
                first_largest(rt[4], iota_e[:, :], E, rt[5], rt[6], rv[3], rv[4])
                do(dve.scalar_tensor_tensor(out=rt[4], in0=rt[5], scalar=LOW, in1=rt[4], op0=ALU.mult, op1=ALU.add))
                first_largest(rt[4], iota_e[:, :], E, rt[7], rt[6], rv[3], rv[4])
                dve.tensor_tensor(picked_b[:, :, :], rt[5], rt[7], ALU.add).then_inc(rt_picked, 1)
                do(dve.tensor_tensor(rt[8], rt[5], rt[7], ALU.add))
                do(dve.tensor_tensor(rt[9], scores, rt[8], ALU.mult))
                do(dve.tensor_reduce(rv[5], rt[9], AX.X, ALU.add))
                do(dve.reciprocal(rv[6], rv[5]))
                own.mark(dve.tensor_scalar(info[:, :, E:E + 2, :], rt[9][:, :, 0:8].rearrange("p t (e c) -> p t e c", c=4), 0.0,
                                           None, ALU.mult))
                own.mark(dve.memset(ranks[:, :, E:E + 3], 0.0))
                own.mark(dve.tensor_copy(info[:, :, 0:E, 0], over_e(row_id[:, :])))
                own.mark(dve.scalar_tensor_tensor(out=info[:, :, 0:E, 1], in0=rt[7], scalar=float(S),
                                                  in1=over_e(row_id[:, :]), op0=ALU.mult, op1=ALU.add))
                do(dve.tensor_tensor(rt[10], rt[9], over_e(rv[6]), ALU.mult))
                do(dve.tensor_copy(info[:, :, 0:E, 2], rt[10]))
                do(dve.tensor_tensor(info[:, :, 0:E, 3], rt[10], info[:, :, 0:E, 2].bitcast(F32), ALU.subtract))
                dve.wait_ge(rt_ranks, L + 1)
                do(dve.tensor_tensor(ranks[:, :, 0:E], ps[:, 6, 0:T * E].rearrange("p (t e) -> p t e", t=T),
                                     rt[8], ALU.mult))
                total = ps[0:1, 6, T * E:(T + 1) * E]
                own.mark(dve.tensor_copy(counts[:, :], total))
                if L == 0:
                    do(dve.memset(scan[:, :, :], 0.0))
                    do(dve.memset(scan[:, 1, 0:1], 1.0))
                else:
                    do(dve.tensor_copy(scan[:, 1, 0:1], scan[:, 0, E + 7:E + 8]))
                    do(dve.memset(scan[:, :, 1:8], 0.0))
                    do(dve.memset(scan[:, 0, 0:1], 0.0))
                do(dve.tensor_scalar(scan[:, 0, 8:], total, float(P), 3.0, ALU.is_gt, ALU.mult))
                do(dve.tensor_copy(part3[:, :], scan[:, 0, 8:]))
                for m, d in enumerate((1, 2, 4, 8)):
                    a, b = scan[:, m % 2, :], scan[:, 1 - m % 2, :]
                    if m == 0:
                        do(dve.tensor_copy(carry[:, :], scan[:, 1, 0:1]))
                        do(dve.memset(scan[:, 1, 0:1], 0.0))
                    do(dve.tensor_tensor(b[:, 8:], a[:, 8:], a[:, 8 - d:8 - d + E], ALU.add))
                do(dve.tensor_scalar(scan[:, 0, 8:], scan[:, 0, 8:], carry[:, 0:1], None, ALU.add))
                dve.tensor_tensor(parts[:, :], scan[:, 0, 8:], part3[:, :], ALU.subtract).then_inc(rt_ready, 1)
                dve.wait_ge(rt_ready, L + 1)

            def experts(L):
                TB, EX, SC = 18 * L, 16 * L + 1, 8 * L + 1
                if L == 0:
                    for s, n in ((hid_done, 1), (ht_ev, 1), (y_dve, 1), (c_copy, 1), (c_rank, 1), (c_hot, 1), (c_idx, 2),
                                 (c_hid, 1), (c_he, 1), (c_yd, 1)):
                        dve.sem_inc(s, n)

                def take_table(rows, gate, done):
                    dve.tensor_scalar(rows, ps[:, 7, 0:2], BIG, None, ALU.add).then_inc(done, 1)
                    dve.tensor_reduce(gate, ps[:, 7, 2:4], AX.X, ALU.add).then_inc(done, 1)

                def hidden(gate):
                    return dve.scalar_tensor_tensor(out=hid, in0=silu, scalar=gate, in1=ps[:, 3, :],
                                                    op0=ALU.mult, op1=ALU.mult)

                for e in range(2):
                    one_hots4(dve, e, onehot[:, e, :], hot, ranks, slot1)
                for e in range(2):
                    dve.wait_ge(tbl_done, TB + e + 1)
                    take_table(tokv[:, e, :], tokg[:, e:e + 1], tbl_ev)
                    if e == 0:
                        one_hots4(dve, 2, onehot[:, 0, :], hot, ranks, slot1)
                with dve.Fori(0, E // BODY) as i:
                    for j in range(BODY):
                        e = i * BODY + j
                        dve.wait_ge(tbl_done, e + TB + 3)
                        dve.wait_ge(scattered[j % 2], (i * 2 + SC + j // 2) * 16)
                        take_table(tokv[:, (j + 2) % 4, :], tokg[:, (j + 2) % 4:(j + 2) % 4 + 1], tbl_ev)
                        one_hots4(dve, e + 3, onehot[:, (j + 1) % 2, :], hot, ranks, slot1)
                        n_rows = dve.value_load(counts[0:1, bass.ds(e, 1)], min_val=0, max_val=S)
                        dve.wait_ge(tbl_ev, (e + TB + 1) * 2)
                        dve.wait_ge(silu_done, e + EX + 1)
                        dve.wait_ge(up_mm, e + EX + 1)
                        dve.wait_ge(ht_done, e + EX)
                        hidden(tokg[:, j:j + 1]).then_inc(hid_done, 1)
                        dve.wait_ge(ht_done, e + EX + 1)
                        dve.wait_ge(y_mm, e + EX)
                        dve.tensor_copy(hidT, ps[:, 6, :]).then_inc(ht_ev, 1)
                        dve.wait_ge(y_mm, e + EX + 1)
                        dve.tensor_copy(yb[:, j % 2, BANK:2 * BANK], ps[:, 5, :]).then_inc(y_dve, 1)
                        with dve.If(n_rows > P):
                            before = dve.value_load(parts[0:1, bass.ds(e, 1)], min_val=0, max_val=6 * E + 1)
                            dve.tensor_copy(cold_rank[:, :].unsqueeze(2), ranks[:, :, bass.ds(e, 1)]
                                            ).then_inc(c_copy, 3)
                            with dve.Fori(0, 3) as m:
                                c = before + m
                                dve.wait_ge(c_copy, before + 3)
                                dve.wait_ge(c_hot, c)
                                dve.tensor_scalar(cold_rank[:, :], cold_rank[:, :], -float(P), None,
                                                  ALU.add).then_inc(c_rank, 1)
                                dve.wait_ge(c_rank, c + 1)
                                for s in range(T - 1):
                                    dve.tensor_scalar(coneh[:, s * P:(s + 1) * P], slot1[:, :],
                                                      cold_rank[:, s:s + 1], None, ALU.is_equal)
                                s = T - 1
                                dve.tensor_scalar(coneh[:, s * P:(s + 1) * P], slot1[:, :],
                                                  cold_rank[:, s:s + 1], None, ALU.is_equal).then_inc(c_hot, 1)
                                dve.wait_ge(c_tbl, c + 1)
                                dve.wait_ge(c_sca, c * 16)
                                take_table(cold_rows[:, :], cold_gate[:, :], c_idx)
                                dve.wait_ge(c_silu, c + 1)
                                dve.wait_ge(c_idx, (c + 1) * 2)
                                hidden(cold_gate[:, 0:1]).then_inc(c_hid, 1)
                                dve.wait_ge(c_ht, c + 1)
                                dve.tensor_copy(hidT, ps[:, 6, :]).then_inc(c_he, 1)
                                dve.wait_ge(c_y, c + 1)
                                dve.tensor_copy(cyb[:, BANK:2 * BANK], ps[:, 5, :]).then_inc(c_yd, 1)
                        with dve.Else():
                            dve.nop()
                        dve.nop()

                def add(t):
                    dve.wait_ge(y_loaded[t % 2], 16 * (2 * L + t // 2 + 1))
                    do(dve.scalar_tensor_tensor(out=H[:, t, :], in0=H[:, t, :], scalar=ALPHA,
                                                in1=ysum[:, t % 2, 0:D], op0=ALU.mult, op1=ALU.add))
                    do(dve.tensor_tensor(H[:, t, :], H[:, t, :], ysum[:, t % 2, D:2 * D], ALU.add))

                if L == 0:
                    split(fox0)
                    split(fox0 + 1)
                layer_norm(2 * L + 1, add)

            dve.wait_ge(consts, 17)
            own.mark(dve.tensor_copy(upto_b[:, :], upto[:, :]))
            own.mark(dve.tensor_copy(ones_b[:, :], one[:, :].to_broadcast([P, P])))
            dve.memset(gr_in, 1.0).then_inc(gr_ev, 1)
            for t in range(T):
                take_tile(TP_X, t)
            split_narrow(0)
            split_narrow(1)
            split(gla0)
            split(gla0 + 1)
            dve.wait_ge(gr_done, 1)
            dve.wait_ge(gr_ev, 1)
            dve.tensor_copy(gr_in[0:RANK, :], ps[0:RANK, 6, :]).then_inc(gr_ev, 1)
            for t in range(T):
                dve.wait_ge(z_done, t + 1)
                dve.tensor_scalar(gk[:, t, :], ps[:, 6, :], 0.0, None, ALU.min).then_inc(z_min, 1)
            z_t = states.rearrange("p a b -> p (a b)").rearrange("p (t n) -> p t n", t=T)
            split_narrow(2)
            split(gla0 + 2)
            for u in range(H_A, 2 * H_A):
                take(u)
            split(gla0 + 3)
            for t in range(T):
                dve.wait_ge(z_ln, t + 1)
                dve.tensor_tensor(gk[:, t, :], gk[:, t, :], z_t[:, t, :], ALU.subtract).then_inc(gk_ready, 1)
            for u in range(2 * H_A, 2 * H_A + T):
                take(u)
            split(gla0 + 4)
            for u in range(2 * H_A + T, U_GLA_TAIL):
                take(u)

            def decay(h):
                b = h % 2
                dve.wait_ge(bc_exp, 6 * (h + 1))
                dve.scalar_tensor_tensor(out=q_a[:, h, :], in0=q_a[:, h, :], scalar=float(DK) ** -0.5,
                                         in1=e_bc[:, b, :], op0=ALU.mult, op1=ALU.mult).then_inc(decayed, 1)
                for v in (k_inv, k_end):
                    dve.tensor_tensor(v[:, b, :], v[:, b, :], k_a[:, h, :], ALU.mult).then_inc(decayed, 1)

            dve.wait_ge(*taken(H_A - 1))
            dve.wait_ge(*taken(2 * H_A - 1))
            dve.wait_ge(consts, 17)
            dve.wait_ge(par_loaded, 16 * 8)
            decay(0)
            for h in range(H_A):
                b = h % 2
                dve.wait_ge(kt_done, h + 1)
                dve.tensor_copy(k_tok.rearrange("p t n -> p (t n)"), ps[:, 2, :]).then_inc(kt_ev, 1)
                dve.wait_ge(att_done, h + 1)
                mask = chunk_sums[:, 0:P].bitcast(U32).unsqueeze(1).to_broadcast([P, T, P])
                dve.copy_predicated(att, mask, ps[:, 3, :].rearrange("p (t n) -> p t n", t=T)).then_inc(att_ev, 1)
                for n in range(2 * T - 1):
                    t, c = divmod(n, CPT)
                    if c == 0:
                        dve.wait_ge(kv_done, 4 * h + t + 1)
                    kv = ps[:, KV_BANKS[t % 2] + c, 0:DV]
                    if n == 0:
                        dve.tensor_copy(states[:, 1, :], kv).then_inc(st_done, 1)
                    else:
                        dve.wait_ge(st_done, 7 * h + n)
                        last = n * CH + CH - 1
                        dve.scalar_tensor_tensor(out=states[:, n + 1, :], in0=states[:, n, :],
                                                 scalar=e_bc[:, b, last:last + 1], in1=kv,
                                                 op0=ALU.mult, op1=ALU.add).then_inc(st_done, 1)
                if h + 1 < H_A:
                    decay(h + 1)
                split(gla0 + 5, range(h, h + 1))
                for t in range(T):
                    dve.wait_ge(o_done, 4 * h + t + 1)
                    dve.tensor_copy(mix[:, t, h * DV:(h + 1) * DV], ps[:, 6 + t % 2, 0:DV]).then_inc(o_ev, 1)
            dve.wait_ge(sq_done, T * H_A)
            dve.tensor_scalar(ssq, ssq, 1.0 / DV, RMS_EPS, ALU.mult, ALU.add).then_inc(rms_in, 1)
            dve.wait_ge(rms_out, 1)
            for t in range(T):
                for h in range(H_A):
                    v = mix[:, t, h * DV:(h + 1) * DV]
                    own.mark(dve.scalar_tensor_tensor(out=v, in0=v, scalar=rms[:, t * H_A + h:t * H_A + h + 1],
                                                      in1=normg, op0=ALU.mult, op1=ALU.mult))
            own.settle(dve)
            dve.tensor_copy(ssq, rms).then_inc(normed, 1)
            dve.wait_ge(normed, 1)
            tail(0)
            router(0)
            experts(0)
            for t in range(T):
                take_tile(TP_L0, t)
            dve.wait_ge(fl_done, 1)
            f3 = f_tmp.rearrange("p (t h) -> p t h", t=T)
            halves = ps[:, 6, 0:2 * T * H_B].rearrange("p (t a h) -> p t a h", t=T, a=2)
            do(dve.tensor_tensor(f3, halves[:, :, 1, :], fbias[:, :].unsqueeze(1).to_broadcast([P, T, H_B]), ALU.add))
            do(dve.tensor_tensor(f3, halves[:, :, 0, :], f3, ALU.add))
            dve.tensor_scalar(f_log, f_tmp, 0.0, None, ALU.min).then_inc(fl_z, 1)
            dve.wait_ge(fl_ln, 1)
            dve.tensor_tensor(f_log, f_log, f_tmp, ALU.subtract).then_inc(f_ready, 1)
            for p in range(2):
                for t in range(T):
                    take(U_FOX + T * p + t)
                split(fox0 + 2 + p)
            dve.wait_ge(cum_done, 1)
            dve.tensor_copy(cumT[0:H_B, 0, :], ps[0:H_B, 7, :]).then_inc(cum_ev, 1)
            dve.tensor_scalar(cumT[0:H_B, 1, :], ps[0:H_B, 7, :], -1.0, None, ALU.mult).then_inc(cum_ev, 1)

            def values_out(g):
                hd, i = divmod(g, T)
                dve.wait_ge(pv_done, g + 1)
                dve.tensor_scalar(o_b[:, i, hd * DH:(hd + 1) * DH], ps[:, 4 + g % 2, 0:DH], rinv[:, g:g + 1],
                                  None, ALU.mult).then_inc(pv_ev, 1)

            for c in range(4):
                for m in range(4):
                    take(U_QUARTERS + 4 * c + m)
                for r in range(16 + 2):
                    if c % 2 and r < 16 and r % 2 == 0:
                        q = r // 2
                        split(fox0 + 4 + c - 1 + q // CHUNKS, range(q % CHUNKS, q % CHUNKS + 1))
                    if r < 16:
                        g, i = 16 * c + r, r % T
                        dve.wait_ge(sc_done, g + 1)
                        diag = ps[:, g % 2, i * P:(i + 1) * P]
                        dve.tensor_tensor(diag, diag, causal[:, :], ALU.add).then_inc(sc_masked, 1)
                        dve.wait_ge(sc_masked, g + 1)
                        dve.tensor_reduce(nmax[:, g:g + 1], ps[:, g % 2, 0:(i + 1) * P], AX.X, ALU.max,
                                          negate=True).then_inc(sc_max, 1)
                    if 1 <= r <= 16:
                        g, i = 16 * c + r - 1, (r - 1) % T
                        dve.wait_ge(pt_done, g + 1)
                        own.mark(dve.reciprocal(rinv[:, g:g + 1], rsum[:, g:g + 1]))
                        if g >= 2:
                            dve.wait_ge(pv_done, g - 1)
                        dve.tensor_copy(prob_t[:, g % 2, 0:(i + 1) * P],
                                        ps[:, 2 + g % 2, 0:(i + 1) * P]).then_inc(pt_ev, 1)
                    if r >= 2:
                        own.settle(dve)
                        values_out(16 * c + r - 2)
            own.settle(dve)
            tail(1)
            router(1)
            experts(1)


def one_hots4(dve, e, dst, done, ranks, slot1):
    T = ranks.shape[1]
    for s in range(T):
        ptr = ranks[:, s, e:e + 1] if isinstance(e, int) else ranks[:, s, bass.ds(e, 1)]
        ins = dve.tensor_scalar(dst[:, s * P:(s + 1) * P], slot1[:, :], ptr, None, ALU.is_equal)
    ins.then_inc(done, 1)


_INS = ["x", "gla_w_in", "gla_w_gk", "gla_b_gk", "gla_norm_g", "gla_w_out", "kv_w", "forget_bias", "fox_w_qg",
        "fox_w_out", "router_w", "router_bias", "moe_w_gate", "moe_w_up", "moe_w_down", "ln_g", "ln_b"]
_OUTS = [((1, 512, 1024), "float32")]


def kernel(**inputs):
    import numpy as _np
    import concourse.bacc as _bacc
    from concourse import mybir as _mybir
    from concourse.bass_utils import run_bass_kernel_spmd as _run

    nc = _bacc.Bacc("TRN2", target_bir_lowering=False, num_devices=1)
    arrays, args = {}, []
    for name in _INS:
        a = _np.ascontiguousarray(inputs[name])
        arrays[f"in_{name}_dram"] = a
        args.append(nc.dram_tensor(f"in_{name}_dram", a.shape, _mybir.dt.from_np(a.dtype), kind="ExternalInput").ap())
    for i, (shape, dtype) in enumerate(_OUTS):
        dt = _mybir.dt.from_np(_np.dtype(dtype))
        args.append(nc.dram_tensor(f"out_{i}_dram", shape, dt, kind="ExternalOutput").ap())
    yoco_trunk(nc, *args)
    r = _run(nc, [arrays], core_ids=[0])
    return r.results[0]["out_0_dram"]
```

```python
from contextlib import ExitStack

import concourse.bass as bass
from concourse import mybir

F32 = mybir.dt.float32
F32R = mybir.dt.float32r
BF16 = mybir.dt.bfloat16
I32 = mybir.dt.int32
U32 = mybir.dt.uint32
ALU = mybir.AluOpType
ACT = mybir.ActivationFunctionType
AX = mybir.AxisListType

P = 128
BANK = 512




class Steps:

    def __init__(self, sem):
        self.sem, self.n = sem, 0

    def mark(self, ins):
        self.n += 1
        ins.then_inc(self.sem, 1)

    def settle(self, eng):
        eng.wait_ge(self.sem, self.n)


def yoco_trunk(nc, x, gla_w_in, gla_w_gk, gla_b_gk, gla_norm_g, gla_w_out, kv_w, forget_bias, fox_w_qg,
               fox_w_out, router_w, router_bias, moe_w_gate, moe_w_up, moe_w_down, ln_g, ln_b, out):
    _, S, D = x.shape
    DEPTH, E, _, DE = moe_w_gate.shape
    RANK, HK = gla_w_gk.shape[1:]
    DV = gla_norm_g.shape[1]
    HV = gla_w_out.shape[1]
    H_A = HV // DV
    DK = HK // H_A
    H_B = forget_bias.shape[0]
    DH = fox_w_out.shape[1] // H_B
    CH = 64
    GROUPS = 4
    EPG = E // GROUPS
    T = S // P
    K = D // P
    KE = DE // P
    CPT = P // CH
    ALPHA = float((2 * DEPTH) ** 0.25)
    LN_EPS, RMS_EPS, GATE_NORM = 1e-5, 1e-6, 16.0
    BIG = float(4 * S)
    NEG = -1e37
    LOW = -3e38
    assert DEPTH == 2 and T == 4 and K == 8 and DK == P and S == BANK and DE == BANK and DH == 64

    h_rows = nc.dram_tensor("h_rows", [S, D], F32).ap()
    cum_rows = nc.dram_tensor("cum_rows", [2, 16, S], F32).ap()
    y_rows = nc.dram_tensor("y_rows", [2 * S, D], F32).ap()

    RING, PAIRED = 6, 5
    CHUNKS = 4
    GLA_PIECES = 8
    FOX_PIECES = 10
    MOE_PIECES = 3 * E
    gla0, fox0 = 0, GLA_PIECES
    BODY = 4
    before_mix = [0, GLA_PIECES + MOE_PIECES]
    before_moe = [GLA_PIECES, GLA_PIECES + MOE_PIECES + FOX_PIECES]
    seen = [0] * RING
    landed, slot_base = [], []
    for pieces_ in (GLA_PIECES, FOX_PIECES):
        for p_ in range(pieces_):
            seen[2 * p_ % PAIRED] += 1
            landed.append(seen[2 * p_ % PAIRED])
        slot_base.append(list(seen))
        seen = [n_ + MOE_PIECES // RING for n_ in seen]

    def mix_piece(n):
        L, p = (0, n) if n < fox0 else (1, n - fox0)
        return L, p, 2 * p % PAIRED, (2 * p + 1) % PAIRED

    def released_for(n, high):
        L, p, lo_slot, hi_slot = mix_piece(n)
        if p >= (1 if high else 3):
            return before_mix[L] + p - (1 if high else 2)
        if L == 0:
            return 0
        return before_mix[1] - (3 if (hi_slot if high else lo_slot) < 3 else 0)

    ctx = ExitStack()
    with ctx:
        def sb(name, shape, dt=F32):
            return ctx.enter_context(nc.sbuf_tensor(name, shape, dt))

        def sem(name):
            return ctx.enter_context(nc.semaphore(name))

        ring_at = -(-nc.sbuf_base // 32) * 32
        ring = sb("ring", [P, RING, K * BANK])
        ring_r = nc.alloc_sbuf_tensor_at("ring_r", [P, RING, K * BANK], F32R, offset=ring_at)
        H = sb("resid", [P, T, D])
        hT_hi = sb("featT", [P, K, S], F32R)
        hT_lo = ring_r[:, RING - 1, :].rearrange("p (k n) -> p k n", k=K)
        arena = sb("arena", [P, 18624])
        ident = sb("ident", [P, P])
        chunk_sums = sb("chunk_sums", [P, 2 * P])
        upto = sb("upto", [P, P])
        one = sb("one", [P, 1])
        causal = sb("causal", [P, P])
        slot1 = sb("slot1", [P, P])
        rw = sb("rw", [P, K, 2, E], F32R)
        gkf = sb("gkf", [P, K, 2, RANK], F32R)
        rbias = sb("rbias", [P, E])
        fbias = sb("fbias", [P, H_B])
        iota_e = sb("iota_e", [P, E])
        row_id = sb("row_id", [P, T])
        counts = sb("counts", [1, E], I32)
        parts = sb("parts", [1, E], I32)
        scan = sb("scan", [1, 2, 8 + E])
        part3 = sb("part3", [1, E])
        carry = sb("carry", [1, 1])
        ln_mv = sb("ln_mv", [P, T, 2])
        ln_bn = sb("ln_bn", [P, T, 2, 6])
        ln_r = sb("ln_r", [P, T, 3])
        half = sb("half", [P, T * H_A])
        tokv = sb("tokv", [P, 4, 2], U32)
        tokg = sb("tokg", [P, 4])
        cold_rows = sb("cold_rows", [P, 2], U32)
        cold_gate = sb("cold_gate", [P, 1])
        cold_rank = sb("cold_rank", [P, T])
        upto_b = sb("upto_b", [P, P], BF16)
        ones_b = sb("ones_b", [P, P], BF16)
        picked_b = sb("picked_b", [P, T, E], BF16)
        ranks = sb("ranks", [P, T, E + 3])
        ps = ctx.enter_context(nc.psum_tensor("ps", [P, 8, BANK], F32))

        def at(off, *dims):
            n = 1
            for d in dims:
                n *= d
            v = arena[:, off:off + n]
            if len(dims) == 2:
                v = v.rearrange("p (a b) -> p a b", a=dims[0])
            if len(dims) == 3:
                v = v.rearrange("p (a b c) -> p a b c", a=dims[0], b=dims[1])
            return v

        ln_p = at(0, 2, D)
        q_a, k_a, gk = at(0, H_A, S), at(2048, H_A, S), at(4096, T, HK)
        mix = at(6144, T, HV)
        e_bc, k_inv, k_end = at(10240, 2, S), at(11264, 2, S), at(12288, 2, S)
        k_tok, att, states = at(13312, T, P), at(13824, T, P), at(14336, 2 * T, DV)
        gr_in, wgk = at(16384, S)[0:RANK + 1, :], at(16896, HK)[0:RANK + 1, :]
        normg = at(17536, DV)
        narrow_raw = at(10240, 3, K * E)
        ssq = at(17792, T * H_A)
        rms = at(17808, T * H_A)
        squares = at(17824, DV)
        gate_a = at(10240, 2, BANK)
        qa, ka = at(0, 2, 4, S), at(4096, 2, 4, S)
        v_b = at(8192, T, D)
        o_b = at(12288, T, D)
        prob, prob_t = at(16384, 2, S), at(17408, 2, S)
        nmax = at(18432, 64)
        rsum = at(18496, 64)
        rinv = at(18560, 64)
        f_log, f_tmp = nmax, rinv
        cumT = at(16384, 2, S)
        gate_b = at(16384, 2, BANK)
        xg, xgT = at(2048, 2, D), at(4096, 2, D)
        hid, hidT, silu = at(6144, BANK), at(6656, BANK), at(7168, BANK)
        yb = at(7680, 2, D)
        cxg, cxgT, cyb = at(10752, D), at(11776, D), at(12800, D)
        spare = hT_hi[:, :, :].rearrange("p k s -> p (k s)")
        onehot = spare[:, 0:2 * BANK].rearrange("p (a n) -> p a n", a=2)
        coneh = spare[:, 2 * BANK:3 * BANK]
        info = spare[:, 3 * BANK:3 * BANK + T * (E + 3) * 4].rearrange("p (t e c) -> p t e c", t=T, c=4)
        ysum = at(2048, 2, 2 * D)
        rt = [at(14656 + 64 * n, T, E) for n in range(12)]
        rs = [at(14656 + 64 * 12 + 16 * n, T, GROUPS) for n in range(8)]
        rv = [at(14656 + 64 * 14 + 4 * n, T) for n in range(8)]
        total = at(14656 + 64 * 14 + 32, E)[0:1, :]

        w_loaded = [sem(f"w_loaded{n}") for n in range(RING)]
        w_free = sem("w_free")
        w_high, w_low = sem("w_high"), sem("w_low")
        par_high, par_low = sem("par_high"), sem("par_low")
        x_loaded = [sem(f"x_loaded{n}") for n in range(T)]
        par_loaded = sem("par_loaded")
        consts = sem("consts")
        one_rows = sem("one_rows")
        tp_done, tp_act, tp_dve = sem("tp_done"), sem("tp_act"), sem("tp_dve")
        proj_done = sem("proj_done")
        ev_act, ev_dve = sem("ev_act"), sem("ev_dve")
        dve_step, act_step, pool_step = sem("dve_step"), sem("act_step"), sem("pool_step")
        gr_done, gr_ev, z_done, z_min, z_abs, z_ln, gk_ready = (
            sem(n) for n in ("gr_done", "gr_ev", "z_done", "z_min", "z_abs", "z_ln", "gk_ready"))
        bc_done, bc_exp, decayed = sem("bc_done"), sem("bc_exp"), sem("decayed")
        kt_done, kt_ev, att_done, att_ev = sem("kt_done"), sem("kt_ev"), sem("att_done"), sem("att_ev")
        kv_done, st_done, o_done, o_ev, sq_done = (
            sem(n) for n in ("kv_done", "st_done", "o_done", "o_ev", "sq_done"))
        rms_in, rms_out, normed = sem("rms_in"), sem("rms_out"), sem("normed")
        gated = sem("gated")
        lnp_loaded = sem("lnp_loaded")
        ln_stats, ln_rstd, ln_bias, ln_norm, ln_scaled, ln_ready = (
            sem(n) for n in ("ln_stats", "ln_rstd", "ln_bias", "ln_norm", "ln_scaled", "ln_ready"))
        h_stored = sem("h_stored")
        counted = sem("counted")
        rt_logits, rt_in, rt_exp, rt_picked, rt_ranks, rt_ready = (
            sem(n) for n in ("rt_logits", "rt_in", "rt_exp", "rt_picked", "rt_ranks", "rt_ready"))
        pads_clear = sem("pads_clear")
        moves = sem("moves")
        hot, tbl_done, tbl_ev = sem("hot"), sem("tbl_done"), sem("tbl_ev")
        gathered = [sem("gathered0"), sem("gathered1")]
        scattered = [sem("scattered0"), sem("scattered1")]
        xt_done, xt_ev = sem("xt_done"), sem("xt_ev")
        gate_mm, up_mm, silu_done, hid_done = sem("gate_mm"), sem("up_mm"), sem("silu_done"), sem("hid_done")
        ht_done, ht_ev, y_mm, y_act, y_dve = (sem(n) for n in ("ht_done", "ht_ev", "y_mm", "y_act", "y_dve"))
        c_copy, c_rank, c_hot, c_tbl, c_idx, c_gat, c_xt, c_xe = (
            sem("cold_" + n) for n in ("copy", "rank", "hot", "tbl", "idx", "gathered", "xt", "xt_ev"))
        c_gu, c_silu, c_hid, c_ht, c_he, c_y, c_ya, c_yd, c_sca = (
            sem("cold_" + n) for n in ("gate_up", "silu", "hid", "ht", "ht_ev", "y", "y_act", "y_dve", "scattered"))
        y_loaded = [sem("y_loaded0"), sem("y_loaded1")]
        fl_done, fl_z, fl_ln, f_ready, cum_done, cum_ev, cum_stored = (
            sem(n) for n in ("fl_done", "fl_z", "fl_ln", "f_ready", "cum_done", "cum_ev", "cum_stored"))
        cum_put = [sem("cum_put0"), sem("cum_put1")]
        sc_done, sc_masked, sc_max, p_done, pt_done, pt_ev, pv_done, pv_ev = (
            sem(n) for n in ("sc_done", "sc_masked", "sc_max", "p_done", "pt_done", "pt_ev", "pv_done", "pv_ev"))
        stored = sem("stored")

        SCORE_BANKS = (0, 1, 6, 7)
        KV_BANKS = (4, 2)

        units = []

        def plan(kind, piece, block, engine):
            units.append((kind, piece, block, engine))

        for f in range(H_A):
            plan("qa", gla0, f, "act")
        for f in range(H_A):
            plan("ka", gla0 + 1, f, "dve")
        for p in range(2):
            for t in range(T):
                plan("va", gla0 + 2 + p, (p, t), "act" if t % 2 else "dve")
        U_GLA_TAIL = len(units)
        for p in range(2):
            for t in range(T):
                plan("ga", gla0 + 4 + p, (p, t), "act")
        for t in range(T):
            for p in range(2):
                plan("oa", gla0 + 6 + p, (p, t), "dve")
        U_FOX = len(units)
        for p in range(2):
            for t in range(T):
                plan("vb", fox0 + p, (p, t), "act" if t % 2 else "dve")
        U_QUARTERS = len(units)
        for c in range(4):
            for f in range(2):
                plan("kb", fox0 + 2 + 2 * (c // 2), (c, f), "dve")
            for f in range(2):
                plan("qb", fox0 + 3 + 2 * (c // 2), (c, f), "act")
        U_FOX_TAIL = len(units)
        for p in range(2):
            for t in range(T):
                plan("gb", fox0 + 6 + p, (p, t), "act")
        for t in range(T):
            for p in range(2):
                plan("ob", fox0 + 8 + p, (p, t), "dve")

        def taken(u):
            e = units[u][3]
            return (ev_act if e == "act" else ev_dve), sum(1 for x_ in units[:u + 1] if x_[3] == e)

        tails = [(U_GLA_TAIL, mix, gate_a, ACT.Silu), (U_FOX_TAIL, o_b, gate_b, ACT.Sigmoid)]
        TP_X, TP_MIX, TP_RT, TP_L0 = 0, [1, 4], [2, 5], 3

        def split_chunk(n, q):
            _, _, lo_slot, hi_slot = mix_piece(n)
            c = slice(q * (K * BANK // CHUNKS), (q + 1) * (K * BANK // CHUNKS))
            return ring[:, lo_slot, c], ring_r[:, hi_slot, c], ring_r[:, lo_slot, c]

        block = ctx.enter_context(nc.Block())

        @block.sync
        def _(sp):
            for t in range(T):
                sp.dma_start(H[:, t, :], x[0, t * P:(t + 1) * P, :]).then_inc(x_loaded[t], 16)

            def load(slot, src):
                dst = ring[:, slot, :].rearrange("p (k n) -> p k n", k=src.shape[1])
                sp.dma_start(dst, src).then_inc(w_loaded[slot], 16)

            def cols(w, c):
                return w[:, c * BANK:(c + 1) * BANK].rearrange("(k p) n -> p k n", p=P)

            def straight(n0, srcs):
                for m, src in enumerate(srcs):
                    n = n0 + m
                    if n == 1:
                        sp.wait_ge(par_loaded, 16 * 8)
                    if n == fox0 + 2:
                        for done in y_loaded:
                            sp.wait_ge(done, 32)
                    if released_for(n, False):
                        sp.wait_ge(w_free, released_for(n, False))
                    load(mix_piece(n)[2], src)

            def experts(L):
                sp.wait_ge(w_free, before_moe[L])
                with sp.Fori(0, E // BODY) as i:
                    for j in range(BODY):
                        e = i * BODY + j
                        for m, w in enumerate((moe_w_gate, moe_w_up, moe_w_down)):
                            n = 3 * j + m
                            src = w[L][bass.ds(e, 1), :, :].rearrange("e (k p) f -> p (e k) f", p=P)
                            if n == 3:
                                sp.wait_ge(gathered[1], 16 * (9 * L + 1))
                            sp.wait_ge(w_free, i * (3 * BODY) + before_moe[L] + n - RING + 1)
                            load(n % RING, src)

            w_in, w_out, w_qg, w_o2 = gla_w_in[0], gla_w_out[0], fox_w_qg[0], fox_w_out[0]
            straight(gla0, [cols(w_in, c) for c in range(6)] + [cols(w_out, c) for c in range(2)])
            experts(0)
            straight(fox0, [cols(kv_w, 2), cols(kv_w, 3), cols(kv_w, 0), cols(w_qg, 0), cols(kv_w, 1),
                            cols(w_qg, 1), cols(w_qg, 2), cols(w_qg, 3), cols(w_o2, 0), cols(w_o2, 1)])
            experts(1)

        @block.gpsimd
        def _(pool):
            own = Steps(pool_step)
            last_row = [pool.to_reg(S - 1), pool.to_reg(2 * S - 1)]
            n_const = [0]

            def const(ins):
                n_const[0] += 1
                ins.then_inc(consts, 1)

            def settle():
                pool.wait_ge(consts, n_const[0])

            const(pool.memset(ident[:, :], 0.0))
            const(pool.memset(chunk_sums[:, :], 1.0 / GATE_NORM))
            const(pool.memset(upto[:, :], 1.0))
            const(pool.memset(one[:, :], 1.0))
            const(pool.memset(causal[:, :], 0.0))
            const(pool.memset(half[:, :], -0.5))
            const(pool.memset(att[:, :, :], 0.0))
            const(pool.iota(slot1[:, :], pattern=[[1, P]], base=1, channel_multiplier=0,
                            allow_small_or_imprecise_dtypes=True))
            const(pool.iota(iota_e[:, :], pattern=[[1, E]], base=0, channel_multiplier=0,
                            allow_small_or_imprecise_dtypes=True))
            const(pool.iota(row_id[:, :], pattern=[[P, T]], base=-int(BIG), channel_multiplier=1,
                            allow_small_or_imprecise_dtypes=True))
            settle()
            const(pool.affine_select(out=ident[:, :], in_=ident[:, :], compare_op=ALU.not_equal, fill=1.0,
                                     base=0, pattern=[[-1, P]], channel_multiplier=1))
            const(pool.affine_select(out=upto[:, :], in_=upto[:, :], compare_op=ALU.is_ge, fill=0.0,
                                     base=0, pattern=[[1, P]], channel_multiplier=-1))
            const(pool.affine_select(out=causal[:, :], in_=causal[:, :], compare_op=ALU.is_ge, fill=NEG,
                                     base=0, pattern=[[-1, P]], channel_multiplier=1))
            const(pool.affine_select(out=chunk_sums[:, 0:P], in_=chunk_sums[:, 0:P], compare_op=ALU.is_ge,
                                     fill=0.0, base=0, pattern=[[1, P]], channel_multiplier=-1))
            const(pool.affine_select(out=chunk_sums[:, P:2 * P], in_=chunk_sums[:, P:2 * P],
                                     compare_op=ALU.is_gt, fill=0.0, base=0, pattern=[[-1, P]],
                                     channel_multiplier=1))
            settle()
            const(pool.affine_select(out=chunk_sums[:, CH:P], in_=chunk_sums[:, CH:P], compare_op=ALU.is_ge,
                                     fill=0.0, base=-CH, pattern=[[0, P - CH]], channel_multiplier=1))
            const(pool.affine_select(out=chunk_sums[:, P:P + CH], in_=chunk_sums[:, P:P + CH],
                                     compare_op=ALU.is_gt, fill=0.0, base=CH, pattern=[[0, CH]],
                                     channel_multiplier=-1))

            def inverse_deviation(N, t):
                pool.wait_ge(ln_stats, N * T + t + 1)
                pool.tensor_tensor(ln_r[:, t, 1:2], ln_r[:, t, 0:1], half[:, 0:1], ALU.pow).then_inc(ln_rstd, 1)

            def layer_norm_rows(N):
                for s in range(T + 1):
                    if s < T:
                        inverse_deviation(N, s)
                    if s >= 1:
                        pool.wait_ge(ln_ready, N * T + s)
                        pool.dma_start(h_rows[(s - 1) * P:s * P, :], H[:, s - 1, :]).then_inc(h_stored, 16)

            def load_results(t):
                pool.dma_start(ysum[:, t % 2, :].rearrange("p (c d) -> p c d", c=2),
                               y_rows.rearrange("(c t p) d -> t p c d", c=2, p=P)[t]).then_inc(y_loaded[t % 2], 16)

            def layer_norm_shift(N):
                for s in range(T + 1):
                    if s < T:
                        inverse_deviation(N, s)
                    if s + 2 < T:
                        load_results(s + 2)
                    if s >= 1:
                        t = s - 1
                        pool.wait_ge(ln_scaled, (N // 2) * T + t + 1)
                        pool.wait_ge(lnp_loaded, 32 * (N + 1))
                        pool.tensor_tensor(H[:, t, :], H[:, t, :], ln_p[:, 1, :], ALU.add).then_inc(ln_ready, 1)

            def load_ln(N):
                L, which = divmod(N, 2)
                for m, w in enumerate((ln_g, ln_b)):
                    pool.dma_start(ln_p[:, m, :], w[L, which:which + 1, :].to_broadcast([P, D])
                                   ).then_inc(lnp_loaded, 16)

            def gather(dst, rows, done):
                pool.sem_inc(moves, 1)
                pool.indirect_dma_start(out=dst, out_offset=None, in_=h_rows,
                                        in_offset=bass.IndirectOffsetOnAxis(ap=rows, axis=0),
                                        bounds_check=last_row[0], oob_is_err=False).then_inc(done, 16)

            def scatter(src, rows, done):
                pool.sem_inc(moves, 1)
                pool.indirect_dma_start(out=y_rows, out_offset=bass.IndirectOffsetOnAxis(ap=rows, axis=0),
                                        in_=src, in_offset=None,
                                        bounds_check=last_row[1], oob_is_err=False).then_inc(done, 16)

            def experts(L):
                TB, XT, EX, SC = 19 * L, 17 * L + 1, 16 * L + 1, 8 * L + 1
                if L == 0:
                    for dst, done in ((yb[0:1, 0, 0:P], scattered[0]), (yb[0:1, 1, 0:P], scattered[1]),
                                      (cyb[0:1, 0:P], c_sca)):
                        pool.dma_start(dst, x[0, 0:1, 0:P]).then_inc(done, 16)
                for n in range(2):
                    pool.memset(xg[:, n, :], 0.0).then_inc(pads_clear, 1)
                pool.memset(cxg, 0.0).then_inc(pads_clear, 1)
                pool.wait_ge(pads_clear, 3 * (L + 1))
                pool.wait_ge(h_stored, 64 * (L + 1))
                for e in range(2):
                    pool.wait_ge(tbl_ev, 2 * (TB + e + 1))
                    gather(xg[:, e, :], tokv[:, e, 0:1], gathered[e])
                pool.wait_ge(counted, L + 1)
                with pool.Fori(0, E // BODY) as i:
                    for j in range(BODY):
                        e = i * BODY + j
                        n = pool.value_load(counts[0:1, bass.ds(e, 1)], min_val=0, max_val=S)
                        pool.wait_ge(tbl_ev, (e + TB + 3) * 2)
                        pool.wait_ge(xt_done, (e + XT + 1) * 2)
                        gather(xg[:, j % 2, :], tokv[:, (j + 2) % 4, 0:1], gathered[j % 2])
                        pool.wait_ge(y_act, e + EX + 1)
                        pool.wait_ge(y_dve, e + EX + 1)
                        scatter(yb[:, j % 2, :], tokv[:, j % 4, 1:2], scattered[j % 2])
                        with pool.If(n > P):
                            before = pool.value_load(parts[0:1, bass.ds(e, 1)], min_val=0, max_val=6 * E + 1)
                            with pool.Fori(0, 3) as m:
                                c = before + m
                                pool.wait_ge(c_sca, c * 16)
                                pool.wait_ge(c_idx, (c + 1) * 2)
                                gather(cxg, cold_rows[:, 0:1], c_gat)
                                pool.wait_ge(c_ya, c + 1)
                                pool.wait_ge(c_yd, c + 1)
                                scatter(cyb, cold_rows[:, 1:2], c_sca)
                            pool.wait_ge(c_sca, (before + 3) * 16)
                            pool.nop()
                        with pool.Else():
                            pool.nop()
                        pool.nop()
                for n in range(2):
                    pool.wait_ge(gathered[n], 16 * 9 * (L + 1))
                    pool.wait_ge(scattered[n], 16 * (SC + 8))
                for t in range(2):
                    load_results(t)

            pool.wait_ge(sq_done, T * H_A)
            pool.wait_ge(rms_in, 1)
            pool.tensor_tensor(rms, ssq, half[:, 0:T * H_A], ALU.pow).then_inc(rms_out, 1)
            pool.wait_ge(normed, 1)
            load_ln(0)
            layer_norm_rows(0)
            load_ln(1)
            experts(0)
            layer_norm_shift(1)
            pool.wait_ge(ln_ready, 2 * T)
            for buf in (qa, ka):
                pool.memset(buf[DH:DH + 2, :, :, :], 1.0).then_inc(one_rows, 1)
            pool.wait_ge(one_rows, 2)
            pool.wait_ge(cum_ev, 2)
            pool.dma_start(cum_rows.rearrange("a h s -> h a s"), cumT[0:H_B, :, :]).then_inc(cum_stored, 16)
            pool.wait_ge(cum_stored, 16)
            for c in range(4):
                if c >= 2:
                    pool.wait_ge(pv_done, 16 * (c - 1))
                for buf, row, src in ((qa, DH + 1, 0), (ka, DH, 1)):
                    pool.dma_start(buf[row:row + 1, c % 2, :, :], cum_rows[src:src + 1, 4 * c:4 * c + 4, :]
                                   ).then_inc(cum_put[c % 2], 16)
            pool.wait_ge(pv_ev, 64)
            load_ln(2)
            layer_norm_rows(2)
            load_ln(3)
            experts(1)
            layer_norm_shift(3)
            for t in range(T):
                pool.wait_ge(ln_ready, 3 * T + t + 1)
                pool.dma_start(out[0][t * P:(t + 1) * P, :], H[:, t, :]).then_inc(stored, 16)
            pool.wait_ge(stored, 16 * T)

        @block.tensor
        def _(pe):
            def transpose_tile(turn, t, src):
                for kk in range(2):
                    if 4 * turn + t:
                        pe.wait_ge(tp_dve, 2 * (4 * turn + t) - 1 + kk)
                    for j in range(4):
                        mm = pe.transpose(ps[:, kk, j * P:(j + 1) * P],
                                          src[:, t, (4 * kk + j) * P:(4 * kk + j + 1) * P], ident[:, :])
                    mm.then_inc(tp_done, 1)

            def products(o, left, right, k):
                pe.matmul(o, left[0], right[0], start=k == 0, stop=False)
                pe.matmul(o, left[0], right[1], start=False, stop=False)
                return pe.matmul(o, left[1], right[0], start=False, stop=k == K - 1)

            def hT_block(k, cols):
                return hT_hi[:, k, cols], hT_lo[:, k, cols]

            def unit(u, frees=0):
                kind, piece, blk, _ = units[u]
                if u >= 4:
                    pe.wait_ge(*taken(u - 4))
                o = ps[:, 2 + u % 4, :]
                _, _, lo_slot, hi_slot = mix_piece(piece)
                w_hi, w_lo = (ring_r[:, slot, :].rearrange("p (k n) -> p k n", k=K)
                              for slot in (hi_slot, lo_slot))
                first = u == 0 or all(x_[1] != piece for x_ in units[:u])
                for k in range(K):
                    if first and k % (K // CHUNKS) == 0:
                        pe.wait_ge(w_low, CHUNKS * piece + k // (K // CHUNKS) + 1)
                    if kind in ("qa", "ka", "qb", "kb"):
                        f = blk if kind in ("qa", "ka") else 2 * (blk[0] % 2) + blk[1]
                        f = slice(f * P, (f + 1) * P)
                        mm = products(o, (w_hi[:, k, f], w_lo[:, k, f]), hT_block(k, slice(0, S)), k)
                    else:
                        t = blk[1]
                        mm = products(o, hT_block(k, slice(t * P, (t + 1) * P)), (w_hi[:, k, :], w_lo[:, k, :]), k)
                mm.then_inc(proj_done, 1)
                if frees:
                    marker(frees)

            def marker(frees):
                pe.matmul(ps[:, 7, BANK - 2:BANK], ident[:, :], ident[:, 0:2], start=True, stop=True
                          ).then_inc(w_free, frees)

            def narrow(t, w):
                n = 2 * w.shape[3]
                for k in range(K):
                    for m, part in enumerate(hT_block(k, slice(t * P, (t + 1) * P))):
                        mm = pe.matmul(ps[:, 6, t * n:(t + 1) * n], part,
                                       w[:, k, :, :].rearrange("p a n -> p (a n)"),
                                       start=k == 0 and m == 0, stop=k == K - 1 and m == 1)
                return mm

            def tail(L):
                u0, src, _, _ = tails[L]
                for s in range(T):
                    unit(u0 + s, frees=1 if s == T - 1 else 0)
                for s in range(T + 1):
                    if s < T:
                        unit(u0 + T + s, frees=1 if s == T - 1 else 0)
                    if s >= 1:
                        pe.wait_ge(gated, 8 * L + T + s)
                        transpose_tile(TP_MIX[L], s - 1, src)
                for s in range(T + 2):
                    if s < T:
                        pe.wait_ge(tp_dve, 2 * (4 * TP_MIX[L] + s + 1))
                        unit(u0 + 8 + 2 * s)
                        unit(u0 + 9 + 2 * s, frees=2 if s == T - 1 else 0)
                    if 1 <= s <= T:
                        pe.wait_ge(ln_ready, 2 * L * T + s)
                        transpose_tile(TP_RT[L], s - 1, H)
                    if s >= 2:
                        pe.wait_ge(tp_dve, 2 * (4 * TP_RT[L] + s - 1))
                        mm = narrow(s - 2, rw)
                mm.then_inc(rt_logits, 1)

            def router(L):
                pe.wait_ge(rt_picked, L + 1)
                for t in range(T):
                    for s in range(t + 1):
                        before = upto_b if s == t else ones_b
                        pe.matmul(ps[:, 6, t * E:(t + 1) * E], before[:, :], picked_b[:, s, :],
                                  start=s == 0, stop=s == t)
                for s in range(T):
                    mm = pe.matmul(ps[:, 6, T * E:(T + 1) * E], ones_b[:, :], picked_b[:, s, :],
                                   start=s == 0, stop=s == T - 1)
                mm.then_inc(rt_ranks, 1)

            def experts(L):
                TB, XT, EX = 19 * L, 17 * L + 1, 16 * L + 1
                if L == 0:
                    for s, n in ((xt_done, 2), (gate_mm, 1), (up_mm, 1), (ht_done, 1), (y_mm, 1), (c_tbl, 1),
                                 (c_xt, 2), (c_gu, 1), (c_ht, 1), (c_y, 1)):
                        pe.sem_inc(s, n)

                def table(e, hots):
                    for s in range(T):
                        mm = pe.matmul(ps[:, 7, 0:4], hots[:, s * P:(s + 1) * P],
                                       info[:, s, bass.ds(e, 1), :].rearrange("p e c -> p (e c)")
                                       if not isinstance(e, int) else info[:, s, e, :],
                                       start=s == 0, stop=s == T - 1)
                    return mm

                def turn_rows(src, done):
                    for kk in range(2):
                        for j in range(4):
                            mm = pe.transpose(ps[:, kk, j * P:(j + 1) * P],
                                              src[:, (4 * kk + j) * P:(4 * kk + j + 1) * P], ident[:, :])
                        mm.then_inc(done, 1)

                def w_of(n, k):
                    return ring[:, n % RING, :].rearrange("p (k n) -> p k n", k=k)

                def gate_up(xT, n, bank):
                    for k in range(K):
                        mm = pe.matmul(ps[:, bank, :], xT[:, k * P:(k + 1) * P], w_of(n, K)[:, k, :],
                                       start=k == 0, stop=k == K - 1)
                    return mm

                def down(n, rest=None):
                    w = w_of(n, KE)
                    for b in range(2):
                        for k in range(KE):
                            if rest is not None and b == 0 and k == 1:
                                pe.wait_ge(ht_ev, rest)
                            mm = pe.matmul(ps[:, 4 + b, :], hidT[:, k * P:(k + 1) * P],
                                           w[:, k, b * BANK:(b + 1) * BANK], start=k == 0, stop=k == KE - 1)
                    return mm

                def turn_hidden():
                    for k in range(KE):
                        mm = pe.transpose(ps[:, 6, k * P:(k + 1) * P], hid[:, k * P:(k + 1) * P], ident[:, :])
                    return mm

                pe.wait_ge(rt_ready, L + 1)
                for e in range(3):
                    pe.wait_ge(hot, TB + e + 1)
                    if e:
                        pe.wait_ge(tbl_ev, 2 * (TB + e))
                    table(e, onehot[:, e % 2, :]).then_inc(tbl_done, 1)
                pe.wait_ge(counted, L + 1)
                pe.wait_ge(gathered[0], 16 * (9 * L + 1))
                turn_rows(xg[:, 0, :], xt_done)
                pe.wait_ge(tbl_ev, 2 * (TB + 3))
                with pe.Fori(0, E // BODY) as i:
                    for j in range(BODY):
                        e = i * BODY + j
                        n0 = 3 * j

                        def piece(n):
                            pe.wait_ge(w_loaded[n % RING], i * (16 * 3 * BODY // RING)
                                       + 16 * (slot_base[L][n % RING] + n // RING + 1))

                        xT = xgT[:, j % 2, :]
                        piece(n0)
                        pe.wait_ge(xt_ev, (e + XT + 1) * 2)
                        gate_up(xT, n0, 2).then_inc(gate_mm, 1)
                        piece(n0 + 1)
                        gate_up(xT, n0 + 1, 3).then_inc(up_mm, 1)
                        n_rows = pe.value_load(counts[0:1, bass.ds(e, 1)], min_val=0, max_val=S)
                        b = (j + 1) % 2
                        pe.wait_ge(gathered[b], (i * 2 + 9 * L + (j + 1) // 2 + 1) * 16)
                        turn_rows(xg[:, b, :], xt_done)
                        pe.wait_ge(hid_done, e + EX + 1)
                        turn_hidden().then_inc(ht_done, 1)
                        piece(n0 + 2)
                        pe.wait_ge(y_act, e + EX)
                        pe.wait_ge(y_dve, e + EX)
                        pe.wait_ge(hot, e + TB + 4)
                        table(e + 3, onehot[:, b, :]).then_inc(tbl_done, 1)
                        pe.wait_ge(ht_ev, (e + EX) * 2 + 1)
                        down(n0 + 2, rest=(e + EX + 1) * 2).then_inc(y_mm, 1)
                        with pe.If(n_rows > P):
                            before = pe.value_load(parts[0:1, bass.ds(e, 1)], min_val=0, max_val=6 * E + 1)
                            with pe.Fori(0, 3) as m:
                                c = before + m
                                pe.wait_ge(tbl_ev, (e + TB + 4) * 2)
                                pe.wait_ge(xt_ev, (e + XT + 2) * 2)
                                pe.wait_ge(y_act, e + EX + 1)
                                pe.wait_ge(y_dve, e + EX + 1)
                                pe.wait_ge(c_ya, c)
                                pe.wait_ge(c_yd, c)
                                pe.wait_ge(c_hot, c + 1)
                                table(e, coneh).then_inc(c_tbl, 1)
                                pe.wait_ge(c_gat, c * 16)
                                turn_rows(cxg, c_xt)
                                pe.wait_ge(c_xe, (c + 1) * 2)
                                gate_up(cxgT, n0, 2)
                                gate_up(cxgT, n0 + 1, 3).then_inc(c_gu, 1)
                                pe.wait_ge(c_hid, c + 1)
                                turn_hidden().then_inc(c_ht, 1)
                                pe.wait_ge(c_he, c + 1)
                                down(n0 + 2).then_inc(c_y, 1)
                            pe.wait_ge(c_ya, before + 3)
                            pe.wait_ge(c_yd, before + 3)
                            pe.matmul(ps[:, 7, 0:2], ident[:, :], ident[:, 0:2], start=True, stop=True)
                        with pe.Else():
                            pe.nop()
                        pe.wait_ge(tbl_ev, (e + TB + 4) * 2)
                        marker(3)

            pe.wait_ge(consts, 17)
            for t in range(T):
                pe.wait_ge(x_loaded[t], 16)
                transpose_tile(TP_X, t, H)
            pe.wait_ge(par_loaded, 16 * 8)
            pe.wait_ge(par_low, 1)
            pe.wait_ge(tp_dve, 2 * T)
            for k in range(K):
                mm = products(ps[0:RANK, 6, :], (gkf[:, k, 0, :], gkf[:, k, 1, :]), hT_block(k, slice(0, S)), k)
            mm.then_inc(gr_done, 1)
            for f in range(H_A):
                unit(f, frees=1 if f == H_A - 1 else 0)
            pe.wait_ge(gr_ev, 2)
            for t in range(T):
                if t >= 1:
                    pe.wait_ge(z_abs, t)
                pe.matmul(ps[:, 6, :], gr_in[:, t * P:(t + 1) * P], wgk, start=True, stop=True).then_inc(z_done, 1)
            for u in range(H_A, 2 * H_A):
                unit(u, frees=1 if u == 2 * H_A - 1 else 0)
            for u in range(2 * H_A, U_GLA_TAIL):
                unit(u, frees=1 if u % T == T - 1 else 0)

            def decay_sums(h):
                pe.wait_ge(gk_ready, T) if h == 0 else pe.wait_ge(bc_exp, 6 * h)
                for t in range(T):
                    mm = pe.matmul(ps[:, t // 2, (t % 2) * 2 * P:(t % 2 + 1) * 2 * P],
                                   gk[:, t, h * DK:(h + 1) * DK], chunk_sums[:, :], start=True, stop=True)
                    if t % 2:
                        mm.then_inc(bc_done, 1)

            for s in (ev_act, ev_dve):
                pe.wait_ge(s, sum(1 for x_ in units[:U_GLA_TAIL] if x_[3] == ("act" if s is ev_act else "dve")))
            decay_sums(0)
            for h in range(H_A):
                b = h % 2
                if h + 1 < H_A:
                    decay_sums(h + 1)
                pe.wait_ge(decayed, 3 * (h + 1))
                if h:
                    pe.wait_ge(kt_ev, h)
                for t in range(T):
                    mm = pe.transpose(ps[:, 2, t * P:(t + 1) * P], k_end[:, b, t * P:(t + 1) * P], ident[:, :])
                mm.then_inc(kt_done, 1)
                if h:
                    pe.wait_ge(att_ev, h)
                for t in range(T):
                    mm = pe.matmul(ps[:, 3, t * P:(t + 1) * P], k_inv[:, b, t * P:(t + 1) * P],
                                   q_a[:, h, t * P:(t + 1) * P], start=True, stop=True)
                mm.then_inc(att_done, 1)
                pe.wait_ge(kt_ev, h + 1)
                for t in range(T):
                    if t == 1:
                        pe.wait_ge(att_ev, h + 1)
                    elif 2 * h + t >= 2:
                        pe.wait_ge(st_done, 7 * h + 2 * t - 2 if t else 7 * h - 1)
                    for c in range(CPT if t < T - 1 else 1):
                        mm = pe.matmul(ps[:, KV_BANKS[t % 2] + c, 0:DV],
                                       k_tok[c * CH:(c + 1) * CH, t, :],
                                       mix[c * CH:(c + 1) * CH, t, h * DV:(h + 1) * DV], start=True, stop=True)
                    mm.then_inc(kv_done, 1)
                pe.wait_ge(att_ev, h + 1)
                for t in range(T):
                    if 4 * h + t >= 2:
                        pe.wait_ge(o_ev, 4 * h + t - 1)
                    pe.wait_ge(st_done, 7 * h + 2 * t + 1)
                    bank = ps[:, 6 + t % 2, 0:DV]
                    mm = pe.matmul(bank, att[:, t, :], mix[:, t, h * DV:(h + 1) * DV], start=True, stop=False,
                                   skip_group_check=True)
                    for c in range(CPT):
                        n = CPT * t + c
                        if n:
                            mm = pe.matmul(ps[c * CH:(c + 1) * CH, 6 + t % 2, 0:DV],
                                           q_a[:, h, n * CH:(n + 1) * CH], states[:, n, :],
                                           start=False, stop=True, skip_group_check=True)
                    mm.then_inc(o_done, 1)
            pe.wait_ge(o_ev, 4 * H_A)
            tail(0)
            router(0)
            experts(0)
            for s in range(T + 1):
                if s < T:
                    pe.wait_ge(ln_ready, T + s + 1)
                    transpose_tile(TP_L0, s, H)
                if s >= 1:
                    pe.wait_ge(tp_dve, 2 * (4 * TP_L0 + s))
                    mm = narrow(s - 1, gkf)
                    if s == T:
                        mm.then_inc(fl_done, 1)
                    unit(U_FOX + s - 1, frees=1 if s == T else 0)
            for u in range(U_FOX + T, U_QUARTERS):
                unit(u, frees=1 if (u - U_FOX) % T == T - 1 else 0)
            pe.wait_ge(f_ready, 1)
            for t in range(T):
                for s in range(t + 1):
                    mm = pe.matmul(ps[0:H_B, 7, t * P:(t + 1) * P], f_log[:, s * H_B:(s + 1) * H_B],
                                   upto[:, :] if s == t else one[:, :].to_broadcast([P, P]),
                                   start=s == 0, stop=s == t)
            mm.then_inc(cum_done, 1)
            pe.wait_ge(cum_ev, 2)
            for c in range(4):
                for m in range(4):
                    last = c % 2 == 1 and m in (1, 3)
                    unit(U_QUARTERS + 4 * c + m, frees=1 if last else 0)
                b = c % 2
                pe.wait_ge(cum_put[c % 2], 32 * (c // 2 + 1))
                pe.wait_ge(*taken(U_QUARTERS + 4 * c + 1))
                pe.wait_ge(*taken(U_QUARTERS + 4 * c + 3))

                def scores(r):
                    g, (s, i) = 16 * c + r, divmod(r, T)
                    if g >= 4:
                        pe.wait_ge(p_done, g - 3)
                    pe.matmul(ps[:, SCORE_BANKS[g % 4], 0:(i + 1) * P], qa[0:DH + 2, b, s, i * P:(i + 1) * P],
                              ka[0:DH + 2, b, s, 0:(i + 1) * P], start=True, stop=True).then_inc(sc_done, 1)

                def turn(r):
                    g, i = 16 * c + r, r % T
                    pe.wait_ge(p_done, g + 1)
                    if g >= 2:
                        pe.wait_ge(pt_ev, g - 1)
                    for n in range(i + 1):
                        mm = pe.transpose(ps[:, 2 + g % 2, n * P:(n + 1) * P], prob[:, g % 2, n * P:(n + 1) * P],
                                          ident[:, :])
                    mm.then_inc(pt_done, 1)

                def values(r):
                    g, (s, i) = 16 * c + r, divmod(r, T)
                    hd = 4 * c + s
                    pe.wait_ge(pt_ev, g + 1)
                    if g >= 2:
                        pe.wait_ge(pv_ev, g - 1)
                    for n in range(i + 1):
                        mm = pe.matmul(ps[:, 4 + g % 2, 0:DH], prob_t[:, g % 2, n * P:(n + 1) * P],
                                       v_b[:, n, hd * DH:(hd + 1) * DH], start=n == 0, stop=n == i)
                    mm.then_inc(pv_done, 1)

                for r in range(16 + 3):
                    if r < 16:
                        scores(r)
                    if 2 <= r <= 17:
                        turn(r - 2)
                    if r >= 3:
                        values(r - 3)
                pe.wait_ge(pv_ev, 16 * (c + 1))
            tail(1)
            router(1)
            experts(1)

        @block.scalar
        def _(act):
            own = Steps(act_step)
            w_in = gla_w_in[0]
            raw = [narrow_raw[:, m, :].rearrange("p (k n) -> p k n", k=K) for m in range(3)]
            act.dma_start(raw[0], w_in[:, 2 * HK + 2 * HV:].rearrange("(k p) n -> p k n", p=P)
                          ).then_inc(par_loaded, 16)
            act.dma_start(wgk[0:RANK, :], gla_w_gk[0]).then_inc(par_loaded, 16)
            act.dma_start(wgk[RANK:RANK + 1, :], gla_b_gk).then_inc(par_loaded, 16)
            act.dma_start(normg, gla_norm_g.to_broadcast([P, DV])).then_inc(par_loaded, 16)
            act.dma_start(raw[1], router_w.rearrange("(k p) n -> p k n", p=P)).then_inc(par_loaded, 16)
            act.dma_start(rbias[:, :], router_bias.rearrange("(a e) -> a e", a=1).to_broadcast([P, E])
                          ).then_inc(par_loaded, 16)
            act.dma_start(fbias[:, :], forget_bias.rearrange("(a e) -> a e", a=1).to_broadcast([P, H_B])
                          ).then_inc(par_loaded, 16)
            act.dma_start(raw[2], kv_w[:, 2 * D:].rearrange("(k p) n -> p k n", p=P)).then_inc(par_loaded, 16)

            def split_narrow(m):
                act.wait_ge(par_loaded, 16 * 8)
                if m == 2:
                    act.wait_ge(gr_done, 1)
                act.copy((gkf, rw, gkf)[m][:, :, 0, :], raw[m]).then_inc(par_high, 1)

            def split(n, chunks=range(CHUNKS)):
                L, p, lo_slot, _ = mix_piece(n)
                for q in chunks:
                    if q == 0:
                        act.wait_ge(w_loaded[lo_slot], 16 * landed[n])
                        if released_for(n, True):
                            act.wait_ge(w_free, released_for(n, True))
                    w, high, _ = split_chunk(n, q)
                    act.copy(high, w).then_inc(w_high, 1)

            def take_tile(turn, t):
                for kk in range(2):
                    act.wait_ge(tp_done, 8 * turn + 2 * t + kk + 1)
                    act.copy(hT_hi[:, 4 * kk:4 * kk + 4, t * P:(t + 1) * P],
                             ps[:, kk, :].rearrange("p (k n) -> p k n", k=4)).then_inc(tp_act, 1)

            def take(u):
                kind, _, blk, engine = units[u]
                if engine != "act":
                    return
                act.wait_ge(proj_done, u + 1)
                src = ps[:, 2 + u % 4, :]
                if kind == "qa":
                    ins = act.copy(q_a[:, blk, :], src)
                elif kind == "va":
                    ins = act.copy(mix[:, blk[1], blk[0] * BANK:(blk[0] + 1) * BANK], src)
                elif kind == "vb":
                    ins = act.copy(v_b[:, blk[1], blk[0] * BANK:(blk[0] + 1) * BANK], src)
                elif kind == "qb":
                    c, f = blk
                    if f == 0 and c >= 2:
                        act.wait_ge(pv_done, 16 * (c - 1))
                    own.mark(act.mul(qa[0:DH, c % 2, 2 * f, :], ps[0:DH, 2 + u % 4, :], float(DH) ** -0.5))
                    ins = act.mul(qa[0:DH, c % 2, 2 * f + 1, :], ps[DH:P, 2 + u % 4, :], float(DH) ** -0.5)
                ins.then_inc(ev_act, 1)

            def tail(L):
                u0, _, gate, func = tails[L]
                out_piece = units[u0 + 8][1]

                def gate_unit(m):
                    u = u0 + m
                    act.wait_ge(proj_done, u + 1)
                    if m >= 2:
                        act.wait_ge(gated, 8 * L + m - 1)
                    act.activation(gate[:, m % 2, :], ps[:, 2 + u % 4, :], func).then_inc(ev_act, 1)

                for m in range(T):
                    gate_unit(m)
                split(out_piece)
                for s in range(T + 1):
                    if s < T:
                        gate_unit(T + s)
                    if s >= 1:
                        take_tile(TP_MIX[L], s - 1)
                split(out_piece + 1)
                for s in range(T + 1):
                    if s >= 1:
                        take_tile(TP_RT[L], s - 1)
                    if s < T:
                        normalise(2 * L, s)

            def normalise(N, t):
                act.wait_ge(ln_bias, N * T + t + 1)
                act.activation(H[:, t, :], H[:, t, :], ACT.Identity, bias=ln_r[:, t, 2:3],
                               scale=ln_r[:, t, 1:2]).then_inc(ln_norm, 1)

            def router(L):
                act.wait_ge(rt_in, L + 1)
                act.activation(rt[1], rt[0], ACT.Exp).then_inc(rt_exp, 1)

            def experts(L):
                XT, EX = 17 * L + 1, 16 * L + 1
                if L == 0:
                    for s, n in ((xt_ev, 2), (silu_done, 1), (y_act, 1), (c_xe, 2), (c_silu, 1), (c_ya, 1)):
                        act.sem_inc(s, n)

                def take_rows(dst, at_done, base):
                    for kk in range(2):
                        act.wait_ge(at_done, base + kk + 1)
                        yield act.copy(dst[:, kk * BANK:(kk + 1) * BANK], ps[:, kk, :])

                act.wait_ge(counted, L + 1)
                for ins in take_rows(xgT[:, 0, :], xt_done, 2 * XT):
                    ins.then_inc(xt_ev, 1)
                with act.Fori(0, E // BODY) as i:
                    for j in range(BODY):
                        e = i * BODY + j
                        n_rows = act.value_load(counts[0:1, bass.ds(e, 1)], min_val=0, max_val=S)
                        act.wait_ge(gate_mm, e + EX + 1)
                        act.wait_ge(hid_done, e + EX)
                        act.activation(silu, ps[:, 2, :], ACT.Silu).then_inc(silu_done, 1)
                        for ins in take_rows(xgT[:, (j + 1) % 2, :], xt_done, (e + XT + 1) * 2):
                            ins.then_inc(xt_ev, 1)
                        act.wait_ge(y_mm, e + EX + 1)
                        act.wait_ge(scattered[j % 2], (i * 2 + 8 * L + 1 + j // 2) * 16)
                        act.copy(yb[:, j % 2, 0:BANK], ps[:, 4, :]).then_inc(y_act, 1)
                        with act.If(n_rows > P):
                            before = act.value_load(parts[0:1, bass.ds(e, 1)], min_val=0, max_val=6 * E + 1)
                            with act.Fori(0, 3) as m:
                                c = before + m
                                for ins in take_rows(cxgT, c_xt, c * 2):
                                    ins.then_inc(c_xe, 1)
                                act.wait_ge(c_gu, c + 1)
                                act.wait_ge(hid_done, e + EX + 1)
                                act.wait_ge(c_hid, c)
                                act.activation(silu, ps[:, 2, :], ACT.Silu).then_inc(c_silu, 1)
                                act.wait_ge(c_y, c + 1)
                                act.wait_ge(c_sca, c * 16)
                                act.copy(cyb[:, 0:BANK], ps[:, 4, :]).then_inc(c_ya, 1)
                        with act.Else():
                            act.nop()
                        act.nop()

            for t in range(T):
                take_tile(TP_X, t)
            split_narrow(0)
            split_narrow(1)
            split(gla0)
            split(gla0 + 1)
            for u in range(H_A):
                take(u)
            split_narrow(2)
            split(gla0 + 2)
            z_t = states.rearrange("p a b -> p (a b)").rearrange("p (t n) -> p t n", t=T)
            for t in range(T):
                act.wait_ge(z_min, t + 1)
                act.activation(z_t[:, t, :], ps[:, 6, :], ACT.Abs).then_inc(z_abs, 1)
            for t in range(T):
                act.wait_ge(z_abs, t + 1)
                own.mark(act.activation(z_t[:, t, :], z_t[:, t, :], ACT.Exp, scale=-1.0))
            for t in range(T):
                own.settle(act)
                act.activation(z_t[:, t, :], z_t[:, t, :], ACT.Ln, bias=1.0).then_inc(z_ln, 1)
            split(gla0 + 3)
            for u in range(2 * H_A, 2 * H_A + T):
                take(u)
            split(gla0 + 4)
            for u in range(2 * H_A + T, U_GLA_TAIL):
                take(u)

            def exps(h):
                b = h % 2
                for m in range(2):
                    act.wait_ge(bc_done, 2 * h + m + 1)
                    if h >= 2 and m == 0:
                        act.wait_ge(o_ev, 4 * (h - 1))
                    src = ps[:, m, :].rearrange("p (t c n) -> p t c n", t=2, c=2)
                    cols = slice(m * 2 * P, (m + 1) * 2 * P)
                    for dst, part, sign in ((e_bc, 0, 1.0), (k_inv, 0, -1.0), (k_end, 1, 1.0)):
                        act.activation(dst[:, b, cols].rearrange("p (t n) -> p t n", t=2), src[:, :, part, :],
                                       ACT.Exp, scale=sign).then_inc(bc_exp, 1)

            exps(0)
            for h in range(H_A):
                if h + 1 < H_A:
                    exps(h + 1)
                split(gla0 + 5, range(h, h + 1))
                for t in range(T):
                    act.wait_ge(o_ev, 4 * h + t + 1)
                    if 4 * h + t:
                        act.wait_ge(sq_done, 4 * h + t)
                    act.activation(squares, mix[:, t, h * DV:(h + 1) * DV], ACT.Square,
                                   accum_out=ssq[:, t * H_A + h:t * H_A + h + 1]).then_inc(sq_done, 1)
            tail(0)
            router(0)
            experts(0)
            split(fox0)
            split(fox0 + 1)
            for s in range(T + 1):
                if s < T:
                    normalise(1, s)
                if s >= 1:
                    take_tile(TP_L0, s - 1)
            act.wait_ge(fl_z, 1)
            own.mark(act.activation(f_tmp, f_tmp, ACT.Abs))
            own.settle(act)
            own.mark(act.activation(f_tmp, f_tmp, ACT.Exp, scale=-1.0))
            own.settle(act)
            act.activation(f_tmp, f_tmp, ACT.Ln, bias=1.0).then_inc(fl_ln, 1)
            for p in range(2):
                for t in range(T):
                    take(U_FOX + T * p + t)
                split(fox0 + 2 + p)
            for c in range(4):
                for m in range(4):
                    take(U_QUARTERS + 4 * c + m)
                for r in range(16):
                    if c % 2 and r % 2 == 0:
                        q = r // 2
                        split(fox0 + 4 + c - 1 + q // CHUNKS, range(q % CHUNKS, q % CHUNKS + 1))
                    g, i = 16 * c + r, r % T
                    act.wait_ge(sc_max, g + 1)
                    if g >= 2:
                        act.wait_ge(pt_done, g - 1)
                    if g == 0:
                        act.wait_ge(cum_stored, 16)
                    act.activation(prob[:, g % 2, 0:(i + 1) * P], ps[:, SCORE_BANKS[g % 4], 0:(i + 1) * P], ACT.Exp,
                                   bias=nmax[:, g:g + 1], accum_out=rsum[:, g:g + 1]).then_inc(p_done, 1)
            tail(1)
            router(1)
            experts(1)
            for t in range(T):
                normalise(3, t)

        @block.vector
        def _(dve):
            own = Steps(dve_step)

            def do(ins):
                own.mark(ins)
                own.settle(dve)

            def split_narrow(m):
                w = (gkf, rw, gkf)[m]
                dve.wait_ge(par_high, m + 1)
                dve.tensor_tensor(w[:, :, 1, :], narrow_raw[:, m, :].rearrange("p (k n) -> p k n", k=K),
                                  w[:, :, 0, :].bitcast(F32), ALU.subtract).then_inc(par_low, 1)

            def split(n, chunks=range(CHUNKS)):
                for q in chunks:
                    dve.wait_ge(w_high, CHUNKS * n + q + 1)
                    w, high, low = split_chunk(n, q)
                    dve.tensor_tensor(low, w, high.bitcast(F32), ALU.subtract).then_inc(w_low, 1)

            def take_tile(turn, t):
                for kk in range(2):
                    dve.wait_ge(tp_act, 2 * (4 * turn + t) + kk + 1)
                    block = slice(4 * kk, 4 * kk + 4), slice(t * P, (t + 1) * P)
                    dve.tensor_tensor(hT_lo[:, block[0], block[1]], ps[:, kk, :].rearrange("p (k n) -> p k n", k=4),
                                      hT_hi[:, block[0], block[1]].bitcast(F32), ALU.subtract).then_inc(tp_dve, 1)

            def take(u):
                kind, _, blk, engine = units[u]
                if engine != "dve":
                    return
                dve.wait_ge(proj_done, u + 1)
                src = ps[:, 2 + u % 4, :]
                if kind == "ka":
                    ins = dve.tensor_copy(k_a[:, blk, :], src)
                elif kind == "va":
                    ins = dve.tensor_copy(mix[:, blk[1], blk[0] * BANK:(blk[0] + 1) * BANK], src)
                elif kind == "vb":
                    ins = dve.tensor_copy(v_b[:, blk[1], blk[0] * BANK:(blk[0] + 1) * BANK], src)
                elif kind == "kb":
                    c, f = blk
                    if f == 0 and c >= 2:
                        dve.wait_ge(pv_done, 16 * (c - 1))
                    own.mark(dve.tensor_copy(ka[0:DH, c % 2, 2 * f, :], ps[0:DH, 2 + u % 4, :]))
                    ins = dve.tensor_copy(ka[0:DH, c % 2, 2 * f + 1, :], ps[DH:P, 2 + u % 4, :])
                ins.then_inc(ev_dve, 1)

            def statistics(N, t):
                for p in range(2):
                    own.mark(dve.bn_stats(ln_bn[:, t, p, :], H[:, t, p * BANK:(p + 1) * BANK]))
                own.settle(dve)
                do(dve.bn_aggr(ln_mv[:, t, :], ln_bn[:, t, :, :].rearrange("p a b -> p (a b)")))
                dve.tensor_scalar(ln_r[:, t, 0:1], ln_mv[:, t, 1:2], LN_EPS, None, ALU.add).then_inc(ln_stats, 1)

            def bias(N, t):
                dve.wait_ge(ln_rstd, N * T + t + 1)
                dve.scalar_tensor_tensor(out=ln_r[:, t, 2:3], in0=ln_mv[:, t, 0:1], scalar=-1.0,
                                         in1=ln_r[:, t, 1:2], op0=ALU.mult, op1=ALU.mult).then_inc(ln_bias, 1)

            def gain(N, t):
                dve.wait_ge(ln_norm, N * T + t + 1)
                dve.wait_ge(lnp_loaded, 32 * (N + 1))
                return dve.tensor_tensor(H[:, t, :], H[:, t, :], ln_p[:, 0, :], ALU.mult)

            def tail(L):
                u0, src, gate, _ = tails[L]
                out_piece = units[u0 + 8][1]

                def gate_heads(m):
                    p, t = units[u0 + m][2]
                    dve.wait_ge(*taken(u0 + m))
                    v = src[:, t, p * BANK:(p + 1) * BANK]
                    dve.tensor_tensor(v, v, gate[:, m % 2, :], ALU.mult).then_inc(gated, 1)

                for m in range(T):
                    gate_heads(m)
                split(out_piece)
                for s in range(T + 1):
                    if s < T:
                        gate_heads(T + s)
                    if s >= 1:
                        take_tile(TP_MIX[L], s - 1)
                split(out_piece + 1)

                def add(t):
                    for p in range(2):
                        u = u0 + 8 + 2 * t + p
                        dve.wait_ge(proj_done, u + 1)
                        hp = H[:, t, p * BANK:(p + 1) * BANK]
                        dve.scalar_tensor_tensor(out=hp, in0=hp, scalar=ALPHA, in1=ps[:, 2 + u % 4, :],
                                                 op0=ALU.mult, op1=ALU.add).then_inc(ev_dve, 1)
                    dve.wait_ge(*taken(u0 + 8 + 2 * t + 1))

                for s in range(T + 1):
                    if s < T:
                        add(s)
                        statistics(2 * L, s)
                        bias(2 * L, s)
                        do(gain(2 * L, s))
                        dve.tensor_tensor(H[:, s, :], H[:, s, :], ln_p[:, 1, :], ALU.add).then_inc(ln_ready, 1)
                    if s >= 1:
                        take_tile(TP_RT[L], s - 1)

            def router(L):
                def over_e(v):
                    return v.unsqueeze(2).to_broadcast([P, T, E])

                def each_t(v, n):
                    return v.unsqueeze(1).to_broadcast([P, T, n])

                halves = ps[:, 6, 0:2 * T * E].rearrange("p (t a e) -> p t a e", t=T, a=2)
                logits = rt[11]
                dve.wait_ge(rt_logits, L + 1)
                do(dve.tensor_copy(logits, halves[:, :, 1, :]))
                do(dve.tensor_tensor(logits, halves[:, :, 0, :], logits, ALU.add))
                do(dve.tensor_reduce(rv[0], logits, AX.X, ALU.max))
                dve.tensor_tensor(rt[0], logits, over_e(rv[0]), ALU.subtract).then_inc(rt_in, 1)
                dve.wait_ge(rt_exp, L + 1)
                do(dve.tensor_reduce(rv[1], rt[1], AX.X, ALU.add))
                do(dve.reciprocal(rv[2], rv[1]))
                scores, sel = rt[2], rt[3]
                do(dve.tensor_tensor(scores, rt[1], over_e(rv[2]), ALU.mult))
                do(dve.tensor_tensor(sel, scores, each_t(rbias[:, :], E), ALU.add))
                pair = sel.rearrange("p t (g a b) -> p (t g) a b", g=GROUPS, a=2)
                big = rt[4].rearrange("p t e -> p (t e)")[:, 0:2 * T * GROUPS].rearrange("p (n a) -> p n a", a=2)
                small = rt[5].rearrange("p t e -> p (t e)")[:, 0:2 * T * GROUPS].rearrange("p (n a) -> p n a", a=2)
                own.mark(dve.tensor_tensor(big, pair[:, :, :, 0], pair[:, :, :, 1], ALU.max))
                do(dve.tensor_tensor(small, pair[:, :, :, 0], pair[:, :, :, 1], ALU.min))
                flat = [v.rearrange("p t g -> p (t g)") for v in rs]
                own.mark(dve.tensor_tensor(flat[0], big[:, :, 0], big[:, :, 1], ALU.max))
                own.mark(dve.tensor_tensor(flat[1], big[:, :, 0], big[:, :, 1], ALU.min))
                do(dve.tensor_tensor(flat[2], small[:, :, 0], small[:, :, 1], ALU.max))
                do(dve.tensor_tensor(flat[1], flat[1], flat[2], ALU.max))
                do(dve.tensor_tensor(rs[3], rs[0], rs[1], ALU.add))

                def first_largest(v, iota, n, hit, key, most, low):
                    def wide(a):
                        return a.unsqueeze(2).to_broadcast([P, T, n])
                    do(dve.tensor_reduce(most, v, AX.X, ALU.max))
                    do(dve.tensor_tensor(hit, v, wide(most), ALU.is_equal))
                    do(dve.tensor_scalar(hit, hit, -float(n), None, ALU.mult))
                    do(dve.tensor_tensor(key, hit, each_t(iota, n), ALU.add))
                    do(dve.tensor_reduce(low, key, AX.X, ALU.min))
                    do(dve.tensor_tensor(hit, key, wide(low), ALU.is_equal))

                first_largest(rs[3], iota_e[:, 0:GROUPS], GROUPS, rs[4], rs[5], rv[3], rv[4])
                in_group = rs[4].unsqueeze(3).to_broadcast([P, T, GROUPS, EPG])
                four = [v.rearrange("p t (g e) -> p t g e", g=GROUPS) for v in rt]
                do(dve.tensor_scalar(rs[5], rs[4], -LOW, LOW, ALU.mult, ALU.add))
                outside = rs[5].unsqueeze(3).to_broadcast([P, T, GROUPS, EPG])
                do(dve.tensor_tensor(four[4], four[3], in_group, ALU.mult))
                do(dve.tensor_tensor(four[4], four[4], outside, ALU.add))
                first_largest(rt[4], iota_e[:, :], E, rt[5], rt[6], rv[3], rv[4])
                do(dve.scalar_tensor_tensor(out=rt[4], in0=rt[5], scalar=LOW, in1=rt[4], op0=ALU.mult, op1=ALU.add))
                first_largest(rt[4], iota_e[:, :], E, rt[7], rt[6], rv[3], rv[4])
                dve.tensor_tensor(picked_b[:, :, :], rt[5], rt[7], ALU.add).then_inc(rt_picked, 1)
                do(dve.tensor_tensor(rt[8], rt[5], rt[7], ALU.add))
                do(dve.tensor_tensor(rt[9], scores, rt[8], ALU.mult))
                do(dve.tensor_reduce(rv[5], rt[9], AX.X, ALU.add))
                do(dve.reciprocal(rv[6], rv[5]))
                pads = rt[9][:, :, 0:12].rearrange("p t (e c) -> p t e c", c=4)
                own.mark(dve.tensor_scalar(info[:, :, E:E + 3, :], pads, 0.0, None, ALU.mult))
                own.mark(dve.memset(ranks[:, :, E:E + 3], 0.0))
                own.mark(dve.tensor_copy(info[:, :, 0:E, 0], over_e(row_id[:, :])))
                own.mark(dve.scalar_tensor_tensor(out=info[:, :, 0:E, 1], in0=rt[7], scalar=float(S),
                                                  in1=over_e(row_id[:, :]), op0=ALU.mult, op1=ALU.add))
                do(dve.tensor_tensor(rt[10], rt[9], over_e(rv[6]), ALU.mult))
                do(dve.tensor_copy(info[:, :, 0:E, 2], rt[10]))
                do(dve.tensor_tensor(info[:, :, 0:E, 3], rt[10], info[:, :, 0:E, 2].bitcast(F32), ALU.subtract))
                dve.wait_ge(rt_ranks, L + 1)
                do(dve.tensor_tensor(ranks[:, :, 0:E], ps[:, 6, 0:T * E].rearrange("p (t e) -> p t e", t=T),
                                     rt[8], ALU.mult))
                own.mark(dve.tensor_copy(total[:, :], ps[0:1, 6, T * E:(T + 1) * E]))
                dve.tensor_copy(rv[7], rv[6]).then_inc(rt_ready, 1)
                dve.wait_ge(rt_ready, L + 1)

            def count_parts(L):
                own.mark(dve.tensor_copy(counts[:, :], total[:, :]))
                if L == 0:
                    do(dve.memset(scan[:, :, :], 0.0))
                    do(dve.memset(scan[:, 1, 0:1], 1.0))
                else:
                    do(dve.tensor_copy(scan[:, 1, 0:1], scan[:, 0, E + 7:E + 8]))
                    do(dve.memset(scan[:, :, 1:8], 0.0))
                    do(dve.memset(scan[:, 0, 0:1], 0.0))
                do(dve.tensor_scalar(scan[:, 0, 8:], total[:, :], float(P), 3.0, ALU.is_gt, ALU.mult))
                do(dve.tensor_copy(part3[:, :], scan[:, 0, 8:]))
                for m, d in enumerate((1, 2, 4, 8)):
                    a, b = scan[:, m % 2, :], scan[:, 1 - m % 2, :]
                    if m == 0:
                        do(dve.tensor_copy(carry[:, :], scan[:, 1, 0:1]))
                        do(dve.memset(scan[:, 1, 0:1], 0.0))
                    do(dve.tensor_tensor(b[:, 8:], a[:, 8:], a[:, 8 - d:8 - d + E], ALU.add))
                do(dve.tensor_scalar(scan[:, 0, 8:], scan[:, 0, 8:], carry[:, 0:1], None, ALU.add))
                dve.tensor_tensor(parts[:, :], scan[:, 0, 8:], part3[:, :], ALU.subtract).then_inc(counted, 1)
                dve.wait_ge(counted, L + 1)

            def experts(L):
                TB, EX, SC = 19 * L, 16 * L + 1, 8 * L + 1
                if L == 0:
                    for s, n in ((hid_done, 1), (ht_ev, 2), (y_dve, 1), (c_copy, 1), (c_rank, 1), (c_hot, 1),
                                 (c_idx, 2), (c_hid, 1), (c_he, 1), (c_yd, 1)):
                        dve.sem_inc(s, n)

                def take_table(rows, gate, done):
                    dve.tensor_scalar(rows, ps[:, 7, 0:2], BIG, None, ALU.add).then_inc(done, 1)
                    dve.tensor_reduce(gate, ps[:, 7, 2:4], AX.X, ALU.add).then_inc(done, 1)

                def hidden(gate):
                    return dve.scalar_tensor_tensor(out=hid, in0=silu, scalar=gate, in1=ps[:, 3, :],
                                                    op0=ALU.mult, op1=ALU.mult)

                for e in range(2):
                    one_hots4(dve, e, onehot[:, e, :], hot, ranks, slot1)
                for e in range(3):
                    dve.wait_ge(tbl_done, TB + e + 1)
                    take_table(tokv[:, e, :], tokg[:, e:e + 1], tbl_ev)
                    if e == 0:
                        one_hots4(dve, 2, onehot[:, 0, :], hot, ranks, slot1)
                    if e == 1:
                        count_parts(L)
                with dve.Fori(0, E // BODY) as i:
                    for j in range(BODY):
                        e = i * BODY + j
                        dve.wait_ge(tbl_done, e + TB + 2)
                        one_hots4(dve, e + 3, onehot[:, (j + 1) % 2, :], hot, ranks, slot1)
                        n_rows = dve.value_load(counts[0:1, bass.ds(e, 1)], min_val=0, max_val=S)
                        dve.wait_ge(tbl_ev, (e + TB + 1) * 2)
                        dve.wait_ge(silu_done, e + EX + 1)
                        dve.wait_ge(up_mm, e + EX + 1)
                        dve.wait_ge(ht_done, e + EX)
                        hidden(tokg[:, j:j + 1]).then_inc(hid_done, 1)
                        dve.wait_ge(ht_done, e + EX + 1)
                        dve.wait_ge(y_mm, e + EX)
                        dve.tensor_copy(hidT[:, 0:P], ps[:, 6, 0:P]).then_inc(ht_ev, 1)
                        dve.tensor_copy(hidT[:, P:BANK], ps[:, 6, P:BANK]).then_inc(ht_ev, 1)
                        dve.wait_ge(tbl_done, e + TB + 4)
                        dve.wait_ge(scattered[(j + 1) % 2], (i * 2 + SC + (j + 1) // 2) * 16)
                        take_table(tokv[:, (j + 3) % 4, :], tokg[:, (j + 3) % 4:(j + 3) % 4 + 1], tbl_ev)
                        dve.wait_ge(y_mm, e + EX + 1)
                        dve.tensor_copy(yb[:, j % 2, BANK:2 * BANK], ps[:, 5, :]).then_inc(y_dve, 1)
                        with dve.If(n_rows > P):
                            before = dve.value_load(parts[0:1, bass.ds(e, 1)], min_val=0, max_val=6 * E + 1)
                            dve.tensor_copy(cold_rank[:, :].unsqueeze(2), ranks[:, :, bass.ds(e, 1)]
                                            ).then_inc(c_copy, 3)
                            with dve.Fori(0, 3) as m:
                                c = before + m
                                dve.wait_ge(c_copy, before + 3)
                                dve.wait_ge(c_hot, c)
                                dve.tensor_scalar(cold_rank[:, :], cold_rank[:, :], -float(P), None,
                                                  ALU.add).then_inc(c_rank, 1)
                                dve.wait_ge(c_rank, c + 1)
                                for s in range(T - 1):
                                    dve.tensor_scalar(coneh[:, s * P:(s + 1) * P], slot1[:, :],
                                                      cold_rank[:, s:s + 1], None, ALU.is_equal)
                                s = T - 1
                                dve.tensor_scalar(coneh[:, s * P:(s + 1) * P], slot1[:, :],
                                                  cold_rank[:, s:s + 1], None, ALU.is_equal).then_inc(c_hot, 1)
                                dve.wait_ge(c_tbl, c + 1)
                                dve.wait_ge(c_sca, c * 16)
                                take_table(cold_rows[:, :], cold_gate[:, :], c_idx)
                                dve.wait_ge(c_silu, c + 1)
                                dve.wait_ge(c_idx, (c + 1) * 2)
                                hidden(cold_gate[:, 0:1]).then_inc(c_hid, 1)
                                dve.wait_ge(c_ht, c + 1)
                                dve.tensor_copy(hidT, ps[:, 6, :]).then_inc(c_he, 1)
                                dve.wait_ge(c_y, c + 1)
                                dve.tensor_copy(cyb[:, BANK:2 * BANK], ps[:, 5, :]).then_inc(c_yd, 1)
                        with dve.Else():
                            dve.nop()
                        dve.nop()

                def add(t):
                    dve.wait_ge(y_loaded[t % 2], 16 * (2 * L + t // 2 + 1))
                    do(dve.scalar_tensor_tensor(out=H[:, t, :], in0=H[:, t, :], scalar=ALPHA,
                                                in1=ysum[:, t % 2, 0:D], op0=ALU.mult, op1=ALU.add))
                    do(dve.tensor_tensor(H[:, t, :], H[:, t, :], ysum[:, t % 2, D:2 * D], ALU.add))

                if L == 0:
                    split(fox0)
                    split(fox0 + 1)
                N = 2 * L + 1
                for s in range(T + 2):
                    if s < T:
                        add(s)
                    if 1 <= s <= T:
                        bias(N, s - 1)
                    if s < T:
                        statistics(N, s)
                    if 1 <= s <= T:
                        gain(N, s - 1).then_inc(ln_scaled, 1)
                    if s >= 2 and L == 0:
                        take_tile(TP_L0, s - 2)

            dve.wait_ge(consts, 17)
            own.mark(dve.tensor_copy(upto_b[:, :], upto[:, :]))
            own.mark(dve.tensor_copy(ones_b[:, :], one[:, :].to_broadcast([P, P])))
            dve.memset(gr_in, 1.0).then_inc(gr_ev, 1)
            for t in range(T):
                take_tile(TP_X, t)
            split_narrow(0)
            split_narrow(1)
            split(gla0)
            split(gla0 + 1)
            dve.wait_ge(gr_done, 1)
            dve.wait_ge(gr_ev, 1)
            dve.tensor_copy(gr_in[0:RANK, :], ps[0:RANK, 6, :]).then_inc(gr_ev, 1)
            for t in range(T):
                dve.wait_ge(z_done, t + 1)
                dve.tensor_scalar(gk[:, t, :], ps[:, 6, :], 0.0, None, ALU.min).then_inc(z_min, 1)
            z_t = states.rearrange("p a b -> p (a b)").rearrange("p (t n) -> p t n", t=T)
            split_narrow(2)
            split(gla0 + 2)
            for u in range(H_A, 2 * H_A):
                take(u)
            split(gla0 + 3)
            for t in range(T):
                dve.wait_ge(z_ln, t + 1)
                dve.tensor_tensor(gk[:, t, :], gk[:, t, :], z_t[:, t, :], ALU.subtract).then_inc(gk_ready, 1)
            for u in range(2 * H_A, 2 * H_A + T):
                take(u)
            split(gla0 + 4)
            for u in range(2 * H_A + T, U_GLA_TAIL):
                take(u)

            def decay(h):
                b = h % 2
                dve.wait_ge(bc_exp, 6 * (h + 1))
                dve.scalar_tensor_tensor(out=q_a[:, h, :], in0=q_a[:, h, :], scalar=float(DK) ** -0.5,
                                         in1=e_bc[:, b, :], op0=ALU.mult, op1=ALU.mult).then_inc(decayed, 1)
                for v in (k_inv, k_end):
                    dve.tensor_tensor(v[:, b, :], v[:, b, :], k_a[:, h, :], ALU.mult).then_inc(decayed, 1)

            dve.wait_ge(*taken(H_A - 1))
            dve.wait_ge(*taken(2 * H_A - 1))
            dve.wait_ge(consts, 17)
            dve.wait_ge(par_loaded, 16 * 8)
            decay(0)
            for h in range(H_A):
                b = h % 2
                dve.wait_ge(kt_done, h + 1)
                dve.tensor_copy(k_tok.rearrange("p t n -> p (t n)"), ps[:, 2, :]).then_inc(kt_ev, 1)
                dve.wait_ge(att_done, h + 1)
                mask = chunk_sums[:, 0:P].bitcast(U32).unsqueeze(1).to_broadcast([P, T, P])
                dve.copy_predicated(att, mask, ps[:, 3, :].rearrange("p (t n) -> p t n", t=T)).then_inc(att_ev, 1)
                for n in range(2 * T - 1):
                    t, c = divmod(n, CPT)
                    if c == 0:
                        dve.wait_ge(kv_done, 4 * h + t + 1)
                    kv = ps[:, KV_BANKS[t % 2] + c, 0:DV]
                    if n == 0:
                        dve.tensor_copy(states[:, 1, :], kv).then_inc(st_done, 1)
                    else:
                        dve.wait_ge(st_done, 7 * h + n)
                        last = n * CH + CH - 1
                        dve.scalar_tensor_tensor(out=states[:, n + 1, :], in0=states[:, n, :],
                                                 scalar=e_bc[:, b, last:last + 1], in1=kv,
                                                 op0=ALU.mult, op1=ALU.add).then_inc(st_done, 1)
                if h + 1 < H_A:
                    decay(h + 1)
                split(gla0 + 5, range(h, h + 1))
                for t in range(T):
                    dve.wait_ge(o_done, 4 * h + t + 1)
                    dve.tensor_copy(mix[:, t, h * DV:(h + 1) * DV], ps[:, 6 + t % 2, 0:DV]).then_inc(o_ev, 1)
            dve.wait_ge(sq_done, T * H_A)
            dve.tensor_scalar(ssq, ssq, 1.0 / DV, RMS_EPS, ALU.mult, ALU.add).then_inc(rms_in, 1)
            dve.wait_ge(rms_out, 1)
            for t in range(T):
                for h in range(H_A):
                    v = mix[:, t, h * DV:(h + 1) * DV]
                    own.mark(dve.scalar_tensor_tensor(out=v, in0=v, scalar=rms[:, t * H_A + h:t * H_A + h + 1],
                                                      in1=normg, op0=ALU.mult, op1=ALU.mult))
            own.settle(dve)
            dve.tensor_copy(ssq, rms).then_inc(normed, 1)
            dve.wait_ge(normed, 1)
            tail(0)
            router(0)
            experts(0)
            dve.wait_ge(fl_done, 1)
            f3 = f_tmp.rearrange("p (t h) -> p t h", t=T)
            halves = ps[:, 6, 0:2 * T * H_B].rearrange("p (t a h) -> p t a h", t=T, a=2)
            do(dve.tensor_tensor(f3, halves[:, :, 1, :], fbias[:, :].unsqueeze(1).to_broadcast([P, T, H_B]), ALU.add))
            do(dve.tensor_tensor(f3, halves[:, :, 0, :], f3, ALU.add))
            dve.tensor_scalar(f_log, f_tmp, 0.0, None, ALU.min).then_inc(fl_z, 1)
            dve.wait_ge(fl_ln, 1)
            dve.tensor_tensor(f_log, f_log, f_tmp, ALU.subtract).then_inc(f_ready, 1)
            for p in range(2):
                for t in range(T):
                    take(U_FOX + T * p + t)
                split(fox0 + 2 + p)
            dve.wait_ge(cum_done, 1)
            dve.tensor_copy(cumT[0:H_B, 0, :], ps[0:H_B, 7, :]).then_inc(cum_ev, 1)
            dve.tensor_scalar(cumT[0:H_B, 1, :], ps[0:H_B, 7, :], -1.0, None, ALU.mult).then_inc(cum_ev, 1)

            def values_out(g):
                hd, i = divmod(g, T)
                dve.wait_ge(pv_done, g + 1)
                dve.tensor_scalar(o_b[:, i, hd * DH:(hd + 1) * DH], ps[:, 4 + g % 2, 0:DH], rinv[:, g:g + 1],
                                  None, ALU.mult).then_inc(pv_ev, 1)

            for c in range(4):
                for m in range(4):
                    take(U_QUARTERS + 4 * c + m)
                for r in range(16 + 3):
                    if c % 2 and r < 16 and r % 2 == 0:
                        q = r // 2
                        split(fox0 + 4 + c - 1 + q // CHUNKS, range(q % CHUNKS, q % CHUNKS + 1))
                    if r < 16:
                        g, i = 16 * c + r, r % T
                        dve.wait_ge(sc_done, g + 1)
                        diag = ps[:, SCORE_BANKS[g % 4], i * P:(i + 1) * P]
                        dve.tensor_tensor(diag, diag, causal[:, :], ALU.add).then_inc(sc_masked, 1)
                        dve.wait_ge(sc_masked, g + 1)
                        dve.tensor_reduce(nmax[:, g:g + 1], ps[:, SCORE_BANKS[g % 4], 0:(i + 1) * P], AX.X, ALU.max,
                                          negate=True).then_inc(sc_max, 1)
                    if 2 <= r <= 17:
                        g, i = 16 * c + r - 2, (r - 2) % T
                        dve.wait_ge(pt_done, g + 1)
                        own.mark(dve.reciprocal(rinv[:, g:g + 1], rsum[:, g:g + 1]))
                        if g >= 2:
                            dve.wait_ge(pv_done, g - 1)
                        dve.tensor_copy(prob_t[:, g % 2, 0:(i + 1) * P],
                                        ps[:, 2 + g % 2, 0:(i + 1) * P]).then_inc(pt_ev, 1)
                    if r >= 3:
                        own.settle(dve)
                        values_out(16 * c + r - 3)
            own.settle(dve)
            tail(1)
            router(1)
            experts(1)


def one_hots4(dve, e, dst, done, ranks, slot1):
    T = ranks.shape[1]
    for s in range(T):
        ptr = ranks[:, s, e:e + 1] if isinstance(e, int) else ranks[:, s, bass.ds(e, 1)]
        ins = dve.tensor_scalar(dst[:, s * P:(s + 1) * P], slot1[:, :], ptr, None, ALU.is_equal)
    ins.then_inc(done, 1)


_INS = ["x", "gla_w_in", "gla_w_gk", "gla_b_gk", "gla_norm_g", "gla_w_out", "kv_w", "forget_bias", "fox_w_qg",
        "fox_w_out", "router_w", "router_bias", "moe_w_gate", "moe_w_up", "moe_w_down", "ln_g", "ln_b"]
_OUTS = [((1, 512, 1024), "float32")]


def kernel(**inputs):
    import numpy as _np
    import concourse.bacc as _bacc
    from concourse import mybir as _mybir
    from concourse.bass_utils import run_bass_kernel_spmd as _run

    nc = _bacc.Bacc("TRN2", target_bir_lowering=False, num_devices=1)
    arrays, args = {}, []
    for name in _INS:
        a = _np.ascontiguousarray(inputs[name])
        arrays[f"in_{name}_dram"] = a
        args.append(nc.dram_tensor(f"in_{name}_dram", a.shape, _mybir.dt.from_np(a.dtype), kind="ExternalInput").ap())
    for i, (shape, dtype) in enumerate(_OUTS):
        dt = _mybir.dt.from_np(_np.dtype(dtype))
        args.append(nc.dram_tensor(f"out_{i}_dram", shape, dt, kind="ExternalOutput").ap())
    yoco_trunk(nc, *args)
    r = _run(nc, [arrays], core_ids=[0])
    return r.results[0]["out_0_dram"]
```
